# Optimizing a Trainium2 kernel written in Bass

```python
import math
import functools
import jax
import jax.numpy as jnp
from jax import lax
import numpy as np

D_MODEL = 1024
BATCH = 1
SEQ = 512
DEPTH = 1
DEC_BATCH = 8
DEC_SEQ = 8
PAST_LEN = 2048
PAGE_SIZE = 128

N_HEADS = 8
HEAD_DIM = 128
HD_ATT = N_HEADS * HEAD_DIM
ATT_SCALE = HEAD_DIM ** -0.5
N_IDX_HEADS = 8
IDX_DIM = 64
IDX_SCALE = IDX_DIM ** -0.5 * N_IDX_HEADS ** -0.5
TOPK_MAX = 256
Q_BLOCK = 32
N_BUCKETS = 32
MAX_DISTANCE = 128
CHUNK = 128
SG_GROUPS = 8
SG_GROUP_DIM = 128
D_SG = SG_GROUPS * SG_GROUP_DIM
D_FF = 2816
CONV_W = 3
EPS = 1e-6
IN_SPLIT_SIZES = (HD_ATT, HD_ATT, HD_ATT, N_IDX_HEADS * IDX_DIM, N_IDX_HEADS, IDX_DIM, D_SG, D_SG, D_MODEL, D_MODEL)
W_IN_COLS = sum(IN_SPLIT_SIZES)

kernel_name = 'hybrid_dsa_gmlp_convffn_step'

def rmsnorm(x, g):
    xf = x.astype(jnp.float32)
    y = xf * lax.rsqrt(jnp.mean(xf * xf, axis=-1, keepdims=True) + EPS)
    return (y * g.astype(jnp.float32)).astype(x.dtype)

def rel_bucket(dist):
    n = jnp.maximum(dist, 0)
    max_exact = N_BUCKETS // 2
    nf = jnp.maximum(n, max_exact).astype(jnp.float32)
    large = max_exact + (jnp.log(nf / max_exact) / math.log(MAX_DISTANCE / max_exact)
                         * (N_BUCKETS - max_exact)).astype(jnp.int32)
    return jnp.where(n < max_exact, n, jnp.minimum(large, N_BUCKETS - 1))

def project(xn, w_in):
    B, T, _ = xn.shape
    h = xn @ w_in
    offs = np.cumsum(IN_SPLIT_SIZES)[:-1].tolist()
    q, k, v, iq, iw, ik, su, sv, ga, gb = jnp.split(h, offs, axis=-1)
    return (q.reshape(B, T, N_HEADS, HEAD_DIM), k.reshape(B, T, N_HEADS, HEAD_DIM),
            v.reshape(B, T, N_HEADS, HEAD_DIM), iq.reshape(B, T, N_IDX_HEADS, IDX_DIM),
            iw, ik, su, sv, ga, gb)

def dsa_select(iq, iw, ik, q_pos, topk):
    rel = jax.nn.relu(jnp.einsum('bthd,bsd->bths', iq, ik).astype(jnp.float32))
    score = jnp.einsum('bths,bth->bts', rel, iw.astype(jnp.float32)) * IDX_SCALE
    key_pos = jnp.arange(ik.shape[1], dtype=jnp.int32)
    score = jnp.where(key_pos[None, None, :] <= q_pos[None, :, None], score, -jnp.inf)
    _, idx = lax.top_k(score, topk)
    valid = idx <= q_pos[None, :, None]
    return idx, valid

def dsa_attend(q, k_sel, v_sel, idx, valid, q_pos, rel_bias):
    B, T = q.shape[:2]
    logits = jnp.einsum('bthd,btkhd->bthk', q, k_sel).astype(jnp.float32) * ATT_SCALE
    bias = rel_bias[rel_bucket(q_pos[None, :, None] - idx)]
    logits = logits + jnp.swapaxes(bias, -1, -2).astype(jnp.float32)
    logits = jnp.where(valid[:, :, None, :], logits, -jnp.inf)
    p = jax.nn.softmax(logits, axis=-1).astype(v_sel.dtype)
    out = jnp.einsum('bthk,btkhd->bthd', p, v_sel)
    return out.reshape(B, T, HD_ATT)

def dsa_prompt(q, k, v, iq, iw, ik, rel_bias):
    B, S = q.shape[:2]
    topk = min(TOPK_MAX, S // 4)
    gather = jax.vmap(lambda rows, ids: rows[ids])

    def block(i):
        s0 = i * Q_BLOCK
        qb = lax.dynamic_slice_in_dim(q, s0, Q_BLOCK, axis=1)
        iqb = lax.dynamic_slice_in_dim(iq, s0, Q_BLOCK, axis=1)
        iwb = lax.dynamic_slice_in_dim(iw, s0, Q_BLOCK, axis=1)
        q_pos = s0 + jnp.arange(Q_BLOCK, dtype=jnp.int32)
        idx, valid = dsa_select(iqb, iwb, ik, q_pos, topk)
        return dsa_attend(qb, gather(k, idx), gather(v, idx), idx, valid, q_pos, rel_bias)

    out = lax.map(block, jnp.arange(S // Q_BLOCK, dtype=jnp.int32))
    return jnp.swapaxes(out, 0, 1).reshape(B, S, HD_ATT)

def dsa_sample(q, k, v, iq, iw, ik, cache_k, cache_v, cache_idx_k, page_table, rel_bias):
    DB, DS = q.shape[:2]
    past = page_table.shape[1] * PAGE_SIZE
    topk = min(TOPK_MAX, (past + DS) // 4)
    ik_past = cache_idx_k[page_table].reshape(DB, past, IDX_DIM)
    ik_all = jnp.concatenate([ik_past.astype(ik.dtype), ik], axis=1)
    q_pos = past + jnp.arange(DS, dtype=jnp.int32)
    idx, valid = dsa_select(iq, iw, ik_all, q_pos, topk)
    is_past = (idx < past)[..., None, None]
    pidx = jnp.minimum(idx, past - 1)
    phys = jax.vmap(lambda pt, ids: pt[ids])(page_table, pidx // PAGE_SIZE)
    slot = pidx % PAGE_SIZE
    nidx = jnp.clip(idx - past, 0, DS - 1)
    gather = jax.vmap(lambda rows, ids: rows[ids])
    k_sel = jnp.where(is_past, cache_k[phys, slot].astype(k.dtype), gather(k, nidx))
    v_sel = jnp.where(is_past, cache_v[phys, slot].astype(v.dtype), gather(v, nidx))
    return dsa_attend(q, k_sel, v_sel, idx, valid, q_pos, rel_bias)

def spatial_gating(su, sv, g, w_s, b):
    B, T, _ = su.shape
    u = jax.nn.gelu(su)
    v = rmsnorm(jax.nn.gelu(sv), g)
    n_chunks = -(-T // CHUNK)
    pad = n_chunks * CHUNK - T
    vc = jnp.pad(v, ((0, 0), (0, pad), (0, 0))).reshape(B, n_chunks, CHUNK, SG_GROUPS, SG_GROUP_DIM)
    causal = jnp.tril(jnp.ones((CHUNK, CHUNK), dtype=bool))
    w_causal = jnp.where(causal[None], w_s, 0).astype(vc.dtype)
    s = jnp.einsum('gts,bcsgd->bctgd', w_causal, vc) + b.T[:, :, None]
    s = s.reshape(B, n_chunks * CHUNK, D_SG)[:, :T]
    return u * s, v

def conv_ffn(xn, conv_state, w_up, conv_w, conv_b, w_down):
    T = xn.shape[1]
    h = xn @ w_up
    hp = jnp.concatenate([conv_state.astype(h.dtype), h], axis=1)
    c = conv_b
    for j in range(CONV_W):
        c = c + conv_w[j] * hp[:, j:j + T]
    gate, val = jnp.split(c, 2, axis=-1)
    return (jax.nn.silu(gate) * val) @ w_down, hp[:, T:]

def trunk_layer(x, conv_state, attend, norm_mix_g, w_in, sg_norm_g, sg_w_s, sg_b, w_branch_a, w_branch_b,
                w_out, norm_ffn_g, w_up, ffn_conv_w, ffn_conv_b, w_down):
    xn = rmsnorm(x, norm_mix_g)
    q, k, v, iq, iw, ik, su, sv, ga, gb = project(xn, w_in)
    o_a = attend(q, k, v, iq, iw, ik)
    o_b, sg_v = spatial_gating(su, sv, sg_norm_g, sg_w_s, sg_b)
    merged = jax.nn.sigmoid(ga) * (o_a @ w_branch_a) + jax.nn.sigmoid(gb) * (o_b @ w_branch_b)
    x = x + merged @ w_out
    h, new_conv = conv_ffn(rmsnorm(x, norm_ffn_g), conv_state, w_up, ffn_conv_w, ffn_conv_b, w_down)
    return x + h, (k, v, ik, new_conv, sg_v)

def setup_inputs(seed: int = 0) -> dict:
    key = jax.random.key(seed)
    ks = jax.random.split(key, 24)
    f32 = jnp.float32
    n_pages = PAST_LEN // PAGE_SIZE
    n_used = DEC_BATCH * n_pages
    n_phys = n_used + n_used // 4

    def nrm(k, shape, scale=1.0):
        return jax.random.normal(k, shape, f32) * scale

    page_table = jax.random.permutation(ks[6], n_phys)[:n_used].reshape(DEC_BATCH, n_pages).astype(jnp.int32)
    return {
        'x_prompt': nrm(ks[0], (BATCH, SEQ, D_MODEL)),
        'x_sample': nrm(ks[1], (DEC_BATCH, DEC_SEQ, D_MODEL)),
        'cache_k': nrm(ks[2], (DEPTH, n_phys, PAGE_SIZE, N_HEADS, HEAD_DIM)),
        'cache_v': nrm(ks[3], (DEPTH, n_phys, PAGE_SIZE, N_HEADS, HEAD_DIM)),
        'cache_idx_k': nrm(ks[4], (DEPTH, n_phys, PAGE_SIZE, IDX_DIM)),
        'state_ffn_conv': nrm(ks[5], (DEPTH, DEC_BATCH, CONV_W - 1, 2 * D_FF)),
        'page_table': page_table,
        'rel_bias': nrm(ks[7], (N_BUCKETS, N_HEADS), 0.5),
        'norm_mix_g': 1.0 + nrm(ks[8], (DEPTH, D_MODEL), 0.05),
        'w_in': nrm(ks[9], (DEPTH, D_MODEL, W_IN_COLS), D_MODEL ** -0.5),
        'sg_norm_g': 1.0 + nrm(ks[10], (DEPTH, D_SG), 0.05),
        'sg_w_s': nrm(ks[11], (DEPTH, SG_GROUPS, CHUNK, CHUNK), CHUNK ** -0.5),
        'sg_b': 1.0 + nrm(ks[12], (DEPTH, SG_GROUPS, CHUNK), 0.05),
        'w_branch_a': nrm(ks[13], (DEPTH, HD_ATT, D_MODEL), HD_ATT ** -0.5),
        'w_branch_b': nrm(ks[14], (DEPTH, D_SG, D_MODEL), D_SG ** -0.5),
        'w_out': nrm(ks[15], (DEPTH, D_MODEL, D_MODEL), D_MODEL ** -0.5),
        'norm_ffn_g': 1.0 + nrm(ks[16], (DEPTH, D_MODEL), 0.05),
        'w_up': nrm(ks[17], (DEPTH, D_MODEL, 2 * D_FF), D_MODEL ** -0.5),
        'ffn_conv_w': nrm(ks[18], (DEPTH, CONV_W, 2 * D_FF), CONV_W ** -0.5),
        'ffn_conv_b': nrm(ks[19], (DEPTH, 2 * D_FF), 0.01),
        'w_down': nrm(ks[20], (DEPTH, D_FF, D_MODEL), D_FF ** -0.5),
        'norm_final_g': 1.0 + nrm(ks[21], (D_MODEL,), 0.05),
    }

def reference(x_prompt, x_sample, cache_k, cache_v, cache_idx_k, state_ffn_conv, page_table, rel_bias,
              norm_mix_g, w_in, sg_norm_g, sg_w_s, sg_b, w_branch_a, w_branch_b, w_out, norm_ffn_g,
              w_up, ffn_conv_w, ffn_conv_b, w_down, norm_final_g):
    yp, ys = x_prompt, x_sample
    kp_l, vp_l, ikp_l, cp_l = [], [], [], []
    ks_l, vs_l, iks_l, cs_l, sgs_l = [], [], [], [], []
    for l in range(DEPTH):
        lw = (norm_mix_g[l], w_in[l], sg_norm_g[l], sg_w_s[l], sg_b[l], w_branch_a[l], w_branch_b[l],
              w_out[l], norm_ffn_g[l], w_up[l], ffn_conv_w[l], ffn_conv_b[l], w_down[l])
        attend_p = functools.partial(dsa_prompt, rel_bias=rel_bias)
        attend_s = functools.partial(dsa_sample, cache_k=cache_k[l], cache_v=cache_v[l],
                                     cache_idx_k=cache_idx_k[l], page_table=page_table, rel_bias=rel_bias)
        conv0 = jnp.zeros((yp.shape[0], CONV_W - 1, 2 * D_FF), yp.dtype)
        yp, (kp, vp, ikp, cp, _) = trunk_layer(yp, conv0, attend_p, *lw)
        ys, (k_s, v_s, ik_s, c_s, sg_s) = trunk_layer(ys, state_ffn_conv[l], attend_s, *lw)
        kp_l.append(kp); vp_l.append(vp); ikp_l.append(ikp); cp_l.append(cp)
        ks_l.append(k_s); vs_l.append(v_s); iks_l.append(ik_s); cs_l.append(c_s); sgs_l.append(sg_s)
    y_prompt = rmsnorm(yp, norm_final_g)
    y_sample = rmsnorm(ys, norm_final_g)
    return (y_prompt, y_sample,
            jnp.stack(kp_l), jnp.stack(vp_l), jnp.stack(ikp_l), jnp.stack(cp_l),
            jnp.stack(ks_l), jnp.stack(vs_l), jnp.stack(iks_l), jnp.stack(cs_l), jnp.stack(sgs_l))


_drawn_inputs = setup_inputs


def setup_inputs(seed=0):
    import zlib

    import numpy as np

    out = dict(_drawn_inputs(seed))
    spreads = {}
    factors = {'sg_b': 3.138, 'ffn_conv_b': 8.0}
    for name, (base, spread) in spreads.items():
        noise = np.random.default_rng([zlib.crc32(name.encode()), seed]).standard_normal(out[name].shape)
        drawn = base * np.exp(spread * noise) if base else spread * noise
        out[name] = jnp.asarray(drawn.astype(out[name].dtype))
    for name, factor in factors.items():
        out[name] = (out[name] * factor).astype(out[name].dtype)
    return out
```

```python
import math
from contextlib import ExitStack

import numpy as np
import concourse.bass as bass
from concourse import mybir

F32 = mybir.dt.float32
I32 = mybir.dt.int32
ALU = mybir.AluOpType
ACT = mybir.ActivationFunctionType
AX_X = mybir.AxisListType.X

P = 128
D = 1024
KT = D // P
TP = 512
NB_, NS = 8, 8
TS = NB_ * NS
T = TP + TS
HALF = T // 2
R = 5
H, HD = 8, 128
IDX = 64
PAGE, NPAGES = 128, 16
PAST = PAGE * NPAGES
NKEY = PAST + NS
NPG = NPAGES + 1
NCOL = NPG * PAGE
FF = 2816
FB = FF // P
TOPK_P, TOPK_S = 128, 256
EPS = 1e-6
ATT_SCALE = HD ** -0.5
IDX_SCALE = IDX ** -0.5 * 8 ** -0.5
NEG = -float(2 ** 120)
MARK = -3.4028234663852886e38
BIASW = 384
COL = dict(q=0, k=1024, v=2048, iq=3072, iw=3584, ik=3592, su=3656, sv=4680, ga=5704, gb=6728)
SP_OFF = [0, 128, 384, 768]
SP_COLS = 1280

_CONST = [('ident', 128), ('swap', 128), ('dup', 128), ('selp', 512), ('selT', 256), ('hmask', 8),
          ('newcausal', 8), ('newblock', 64), ('caus', 128), ('bd', 64), ('rep', 64), ('bucket', BIASW)]
COFF, _at = {}, 0
for _n, _w in _CONST:
    COFF[_n] = (_at, _w)
    _at += _w
NCONST = _at


def shape_constants():
    c = np.zeros((P, NCONST), np.float32)

    def put(name, a):
        o, w = COFF[name]
        a = np.asarray(a, np.float32).reshape(a.shape[0], -1)
        c[:a.shape[0], o:o + w] = a

    eye = np.eye(P)
    put('ident', eye)
    put('swap', np.roll(eye, 64, axis=1))
    dup = np.zeros((72, P))
    for m in range(P):
        dup[m % 64, m] = 1
    put('dup', dup)
    selp = np.zeros((NB_, NS, 4, 2, H, NS))
    for b in range(NB_):
        for t in range(NS):
            selp[b, t, b // 2, b % 2, :, t] = 1
    put('selp', selp.reshape(TS, -1))
    put('selT', selp.transpose(3, 4, 5, 2, 0, 1).reshape(P, -1))
    hm = np.zeros((2, H, NS, H))
    for h in range(H):
        hm[:, h, :, h] = 1
    put('hmask', hm.reshape(P, H))
    t = np.arange(NS)
    put('newcausal', np.where(t[None, :] <= np.tile(t, NB_)[:, None], 0.0, NEG))
    b = np.repeat(np.arange(NB_), NS)
    put('newblock', np.where(b[:, None] == b[None, :], 0.0, NEG))
    put('bd', (b[:, None] == b[None, :]).astype(np.float32))
    i = np.arange(P)
    put('caus', np.where(i[None, :] <= i[:, None], 0.0, NEG))
    put('rep', (t[:, None] == np.tile(t, NB_)[None, :]).astype(np.float32))
    hot = np.zeros((32, BIASW))
    for x in range(BIASW):
        n = max(255 - x, 0)
        bk = n if n < 16 else min(16 + int(math.log(n / 16) / math.log(128 / 16) * 16), 31)
        hot[bk, x] = 1
    put('bucket', hot)
    return c


def hybrid_kernel(nc, x_prompt, x_sample, cache_k, cache_v, cache_idx_k, state_ffn_conv, page_table, rel_bias,
                  norm_mix_g, w_in, sg_norm_g, sg_w_s, sg_b, w_branch_a, w_branch_b, w_out, norm_ffn_g,
                  w_up, ffn_conv_w, ffn_conv_b, w_down, norm_final_g, consts,
                  y_prompt, y_sample, k_prompt, v_prompt, ik_prompt, conv_prompt,
                  k_sample, v_sample, ik_sample, conv_sample, sgv_sample):
    n_phys = cache_k.shape[1]
    bias_scr = nc.dram_tensor("bias_scratch", (P, H, BIASW), F32, kind="Internal").ap()
    mask_scr = nc.dram_tensor("mask_scratch", (TS, NCOL), F32, kind="Internal").ap()


    class Stream:
        def __init__(self, banks):
            self.banks, self.fills, self.uses, self.at, self.slots = banks, 0, [0] * banks, 0, {}

        def add(self, *name):
            bank = self.at
            self.slots[name] = (self.fills, bank, self.uses[bank])
            self.fills += 1
            self.uses[bank] += 1
            self.at = (bank + 1) % self.banks

    single, pair = Stream(4), Stream(2)
    for r in range(R):
        for q in range(2):
            single.add('x', r, q)
    single.add('vec')
    for h in range(H):
        single.add('bias', h)
    pair.add('rms', 0)
    for m in range(4):
        pair.add('iq', m)
    pair.add('ikw')
    for n in ('iqsw', 'ikd0', 'ikd1', 'ikwT', 'iwrep'):
        single.add(n)
    for r in range(1, 4):
        for h in range(H):
            single.add('ps', r, h)
    for s in range(17):
        if s < 16:
            single.add('t', s)
        if s >= 1:
            single.add('s1', s - 1)
    for kc in range(4):
        pair.add('ss', kc)
    single.add('s1n')
    pair.add('ssn')
    for c in range(8):
        pair.add('q', c)
    for c in range(8):
        pair.add('k', c)
    for r in range(R):
        for q in range(2):
            single.add('kt', r, q)
    for c in range(4):
        for r in range(R):
            pair.add('v', c, r)
    for h in range(H + 1):
        if h < H:
            for r in range(4):
                single.add('pl', h, r)
        if h:
            single.add('pv', h - 1)
        if h < H:
            for r in range(4):
                single.add('pt', h, r)
    for G in range(2):
        for n in range(64):
            single.add('kp', G, n, 0)
            single.add('kp', G, n, 1)
        for kp in range(NPG):
            pair.add('kl', G, kp)
        for g in range(2):
            for q in range(5):
                single.add('st', G, g, q)
        for b in range(4):
            pair.add('o', G, b)
            single.add('ot', G, b, 0)
            single.add('ot', G, b, 1)
    for c in range(4):
        for r in range(R):
            pair.add('sv', c, r)
    for c in range(8):
        pair.add('su', c)
    single.add('w', 0)
    single.add('w', 1)
    single.add('bd')
    for g in range(8):
        single.add('sg', g)
        single.add('sgs', g)
    for i in range(4):
        for kind in ('gb', 'wb', 'ga', 'wa'):
            for c in (2 * i, 2 * i + 1):
                pair.add(kind, c)
    for c in range(8):
        pair.add('out', c)
    pair.add('rms', 1)
    single.add('state', 0)
    single.add('state', 1)
    for f in range(FB):
        pair.add('up', f, 0)
        pair.add('up', f, 1)
    for c in range(8):
        pair.add('dn', c)
    single.add('ho', 0)
    single.add('ho', 1)
    pair.add('rms', 2)
    for r in range(R):
        for q in range(2):
            single.add('y', r, q)

    NW = 4
    chunks, slot_value, chunk_list = {}, [0] * NW, []

    def add_chunk(name, loads, last_tile):
        n = len(chunk_list)
        slot_value[n % NW] += 16 * loads
        free_at = pair.slots[chunk_list[n - NW][1]][0] + 1 if n >= NW else None
        chunks[name] = (n % NW, slot_value[n % NW], free_at)
        chunk_list.append((name, last_tile))

    for i in range(2):
        add_chunk(('iq', i), 1, ('iq', 2 * i + 1))
    add_chunk(('ikw',), 2, ('ikw',))
    for k in 'qk':
        for i in range(4):
            add_chunk((k, i), 1, (k, 2 * i + 1))
    for k in ('v', 'sv'):
        for i in range(4):
            add_chunk((k, i), 1, (k, i, R - 1))
    for i in range(4):
        add_chunk(('su', i), 1, ('su', 2 * i + 1))
    for i in range(4):
        for k in ('gb', 'wb', 'ga', 'wa'):
            add_chunk((k, i), 1, (k, 2 * i + 1))
    for i in range(4):
        add_chunk(('out', i), 1, ('out', 2 * i + 1))
    for f in range(FB):
        add_chunk(('up', f), 2, ('up', f, 1))
    for c in range(8):
        for kh in range(2):
            add_chunk(('dn', c, kh), 1, ('dn', c))

    ctx = ExitStack()
    with ctx:
        def sb(name, words, dt=F32):
            return ctx.enter_context(nc.sbuf_tensor(name, [P, words], dt))

        xT = sb("xT", KT * T)[:, :].rearrange("p (k t) -> p k t", k=KT)
        xnT_f = sb("xnT", KT * T)
        xnT = xnT_f[:, :].rearrange("p (k t) -> p k t", k=KT)
        oaT = sb("oaT", H * T)[:, :].rearrange("p (k t) -> p k t", k=H)
        W = [sb(f"W{i}", 2048) for i in range(NW)]
        CST = sb("CST", NCONST)
        VT = sb("VT", 200)
        R1 = sb("R1", 9728)
        R2 = sb("R2", 4608)
        SR = sb("SR", NCOL)
        R3 = sb("R3", 7424)
        RB = sb("RB", 2048)
        Vn = sb("Vn", H * HD)
        QN = sb("QN", H * TS)[:, :].rearrange("p (h t) -> p h t", h=H)
        NBd = sb("NBd", 512)[:, :].rearrange("p (g c) -> p g c", g=2)
        NBr = sb("NBr", 272)[:, :].rearrange("p (g c) -> p g c", g=2)
        IKWT = sb("IKWT", 5 * 72)[:, :].rearrange("p (r c) -> p r c", r=5)
        IWS = sb("IWS", 40)[:, :].rearrange("p (r h) -> p r h", r=5)
        ST = sb("ST", 120)
        PTAB = ctx.enter_context(nc.sbuf_tensor("PTAB", [1, NB_ * NPAGES], I32))

        def const(name, rows=P):
            o, w = COFF[name]
            return CST[0:rows, o:o + w]

        ident = const('ident')

        def blocks(a, n):
            return a.rearrange("p (n c) -> p n c", n=n)

        XL = blocks(R1[:, 0:5120], 5)
        BV = blocks(R1[:, 5120:8192], H)
        RBB = blocks(R1[0:32, 8192:9216], H)
        VR = blocks(R1[:, 9216:9472], 2)
        RBT = R1[0:32, 9472:9480]
        iqT = blocks(R2[:, 0:2304], 4)
        IKW = R2[:, 2304:2880]
        IKPAD = blocks(R2[:, 2880:3904], 2)
        MS = R3[:, 0:SP_COLS]
        IQB = blocks(R3[:, 1280:1792], 4)
        IQSW = blocks(R3[:, 1792:2048], 4)
        IKN = [R3[:, 2048 + 512 * i:2560 + 512 * i].rearrange("p (j a d) -> p j a d", j=4, a=2) for i in range(4)]
        IKT = [R3[:, 4096 + 512 * i:4608 + 512 * i] for i in range(2)]
        RL = [R3[:, 5120 + 512 * i:5632 + 512 * i] for i in range(2)]
        RL2 = [R3[:, 6144 + 512 * i:6656 + 512 * i] for i in range(2)]
        SWM = blocks(R3[:, 7168:7424], 4)
        ones = sb("ones", P)
        IKNEW = blocks(ST[:, 0:32], 4)
        RLN = ST[:, 32:64]
        TMP32 = blocks(ST[:, 64:96], 4)
        IWC = ST[:, 96:100]
        MAX8 = ST[0:TS, 0:8]
        MAX8P = ST[:, 8:16]
        M8 = ST[0:TS, 16:24]
        RS = SR[:, 0:T]
        S = SR[0:TS, :]
        BT = blocks(RB[:, 0:2048], H)
        qT = blocks(R2[:, :], H)
        kT = blocks(R1[:, 5120:9728], H)
        V = blocks(R1[:, 0:4096], 4)
        MB = [R3[:, 1280 + 1280 * i:2560 + 1280 * i] for i in range(2)]
        L = R3[:, 3840:5120]
        PT = blocks(R3[:, 5120:7168], 4)
        KO = [R3[:, 5120 + 1024 * i:6144 + 1024 * i] for i in range(2)]
        ring = [R1[:, 1024 * i:1024 * i + 1024] for i in range(8)]
        OS = [blocks(R1[:, 8192 + 256 * i:8448 + 256 * i], 2) for i in range(2)]
        LS = blocks(R2[:, 0:2 * NCOL], 2)
        MG = SR
        PTs = R3[:, 0:2 * NCOL].rearrange("p (g k c) -> p g k c", g=2, k=NPG)
        QZ = R3[:, 4352:6400].rearrange("p (h b c) -> p h b c", h=H, b=8)
        kTn = blocks(R3[:, 6400:7424], H)
        KTb = [blocks(RB[:, 1024 * i:1024 * i + 1024], H) for i in range(2)]
        SV = blocks(R1[:, 0:5120], 5)
        mT = blocks(R1[:, 5120:9728], KT)
        obT = blocks(R2[:, :], 8)
        SG = R3[:, 0:1024]
        SB = blocks(R3[:, 1024:2048], 8)
        WS = blocks(R3[:, 2048:3072], 8)
        WT = blocks(R3[:, 3072:4096], 8)
        BD = blocks(R3[0:TS, 4096:4608], 8)
        TMPS = [R3[:, 4608 + 576 * i:5184 + 576 * i] for i in range(2)]
        JUNK = R3[:, 5760:6784]
        SIGB = [blocks(RB[:, T * i:T * i + T], 2) for i in range(2)]
        SIGA = [blocks(SR[:, T * i:T * i + T], 2) for i in range(1, 3)]
        HPb = [[R3[:, 594 * (2 * i + k):594 * (2 * i + k) + 594] for k in range(2)] for i in range(2)]
        CB = [[R3[:, 2376 + 592 * (2 * i + k):2968 + 592 * (2 * i + k)] for k in range(2)] for i in range(2)]
        SRAW = blocks(R3[:, 4752:5520], 6)
        STT_ = R3[:, 5520:6224]
        HCP = R3[:, 6224:6312]
        HCS = R3[:, 6312:7016]
        CO = blocks(RB[:, 0:896], 7)

        def act_block(f):
            return R1[:, T * f:T * f + T] if f < 16 else R2[:, T * (f - 16):T * (f - 16) + T]
        YO = [R1[:, 1024 * i:1024 * i + 1024] for i in range(2)]
        MX = [ST[:, 24 + 16 * i:28 + 16 * i] for i in range(2)]
        NM = [ST[:, 28 + 16 * i:32 + 16 * i] for i in range(2)]
        SU = [ST[:, 32 + 16 * i:36 + 16 * i] for i in range(2)]
        RC = [ST[:, 36 + 16 * i:40 + 16 * i] for i in range(2)]
        SS = ST[:, 60:65]

        PS = ctx.enter_context(nc.psum_tensor("PS", [P, 8, 512], F32))

        sems = {}

        def S_(name):
            if name not in sems:
                sems[name] = ctx.enter_context(nc.semaphore(name))
            return sems[name]

        single_filled, pair_filled = S_("single_filled"), S_("pair_filled")
        single_drained = [S_(f"single_drained{i}") for i in range(4)]
        pair_drained = [S_(f"pair_drained{i}") for i in range(2)]
        weights_in = [S_(f"weights_in{i}") for i in range(NW)]
        idx_in = [S_(f"idx_pages_in{i}") for i in range(4)]
        page_in = [S_(f"page_in{i}") for i in range(8)]
        block = ctx.enter_context(nc.Block())

        def bank(*n):
            return PS[:, 4 + single.slots[n][1], :]

        def pbank(*n):
            return PS[:, 2 * pair.slots[n][1]:2 * pair.slots[n][1] + 2, :]

        def ptile(*n):
            return pbank(*n)[:, :, 0:HALF]

        def halves(a):
            return a.rearrange("p (a t) -> p a t", a=2)

        def filled(e, *n):
            if n in single.slots:
                e.wait_ge(single_filled, single.slots[n][0] + 1)
            else:
                e.wait_ge(pair_filled, pair.slots[n][0] + 1)

        def drained(e, *n):
            if n in single.slots:
                e.wait_ge(single_drained[single.slots[n][1]], single.slots[n][2] + 1)
            else:
                e.wait_ge(pair_drained[pair.slots[n][1]], pair.slots[n][2] + 1)

        def claim(e, *n):
            if n in single.slots:
                _, k, use = single.slots[n]
                if use:
                    e.wait_ge(single_drained[k], use)
            else:
                _, k, use = pair.slots[n]
                if use:
                    e.wait_ge(pair_drained[k], use)

        def drains(*n):
            return single_drained[single.slots[n][1]] if n in single.slots else pair_drained[pair.slots[n][1]]

        def width(r):
            return P if r < 4 else TS

        def page_freed(e, seq):
            if seq < 8:
                if seq == 0:
                    e.wait_ge(S_("ring_free"), 1)
                return
            G, kind, n = (seq - 8) // 128, (seq - 8) // 64 % 2, (seq - 8) % 64
            if kind == 0:
                e.wait_ge(single_filled, single.slots['kp', G, n, 1][0] + 1)
            else:
                e.wait_ge(S_("v_pages_used"), 64 * G + n + 1)

        @block.sync
        def _(sp):
            w_in_v = w_in[0].rearrange("(k p) n -> p k n", p=P)

            def load_chunk(name):
                slot, _, free_at = chunks[name]
                if free_at is not None:
                    sp.wait_ge(pair_filled, free_at)
                kind, i = name[0], (name[1] if len(name) > 1 else 0)
                dst = blocks(W[slot][:, :], KT)
                if kind in ('iq', 'q', 'k', 'v', 'sv', 'su', 'gb', 'ga'):
                    c = COL[kind] + 256 * i
                    sp.dma_start(dst, w_in_v[:, :, c:c + 256]).then_inc(weights_in[slot], 16)
                elif kind == 'ikw':
                    d = W[slot][:, 0:576].rearrange("p (k c) -> p k c", k=KT)
                    sp.dma_start(d[:, :, 0:64], w_in_v[:, :, COL['ik']:COL['ik'] + 64]).then_inc(weights_in[slot], 16)
                    sp.dma_start(d[:, :, 64:72], w_in_v[:, :, COL['iw']:COL['iw'] + 8]).then_inc(weights_in[slot], 16)
                elif kind in ('wb', 'wa', 'out'):
                    m = {'wb': w_branch_b, 'wa': w_branch_a, 'out': w_out}[kind]
                    sp.dma_start(dst, m[0].rearrange("(k p) n -> p k n", p=P)[:, :, 256 * i:256 * i + 256])\
                        .then_inc(weights_in[slot], 16)
                elif kind == 'up':
                    u = w_up[0].rearrange("(k p) n -> p k n", p=P)
                    for a in range(2):
                        sp.dma_start(dst[:, :, 128 * a:128 * a + 128], u[:, :, FF * a + P * i:FF * a + P * i + P])\
                            .then_inc(weights_in[slot], 16)
                else:
                    c, kh = name[1:]
                    u = w_down[0].rearrange("(k p) n -> p k n", p=P)
                    sp.dma_start(blocks(W[slot][:, 0:1408], 11), u[:, 11 * kh:11 * kh + 11, P * c:P * c + P])\
                        .then_inc(weights_in[slot], 16)

            sp.dma_start(CST[:, :], consts).then_inc(S_("consts_in"), 16)
            sp.dma_start(XL[:, 0:4, :], x_prompt[0].rearrange("(r p) d -> p r d", p=P)).then_inc(S_("x_in"), 16)
            sp.dma_start(XL[0:TS, 4, :], x_sample.rearrange("b s d -> (b s) d")).then_inc(S_("x_in"), 16)
            load_chunk(('iq', 0))
            load_chunk(('iq', 1))
            load_chunk(('ikw',))
            for i, g in enumerate((norm_mix_g[0], norm_ffn_g[0], norm_final_g)):
                sp.dma_start(VR[8 * i:8 * i + 8, 0, :], g.rearrange("(k c) -> k c", k=8)).then_inc(S_("vec_in"), 16)
            cw = ffn_conv_w[0].rearrange("j (f c) -> (j f) c", c=P)
            sp.dma_start(VR[24:128, 0, :], cw[0:104, :]).then_inc(S_("vec_in"), 16)
            sp.dma_start(VR[0:28, 1, :], cw[104:132, :]).then_inc(S_("vec_in"), 16)
            sp.dma_start(VR[28:72, 1, :], ffn_conv_b[0].rearrange("(f c) -> f c", c=P)).then_inc(S_("vec_in"), 16)
            sp.dma_start(RBT, rel_bias).then_inc(S_("rb_in"), 16)
            sp.dma_start(PTAB[:, :], page_table.rearrange("(o b) n -> o (b n)", o=1)).then_inc(S_("table_in"), 16)
            load_chunk(('q', 0))
            sp.wait_ge(S_("table_in"), 16)

            def page_id(b, kp):
                return sp.value_load(PTAB[0:1, b * NPAGES + kp:b * NPAGES + kp + 1], min_val=0, max_val=n_phys - 1)

            for s in range(16):
                kc, p = s // 4, s % 4
                if s >= 4:
                    filled(sp, 't', s - 4)
                for a in range(2):
                    for j in range(4):
                        v = page_id(2 * p + a, 4 * kc + j)
                        sp.dma_start(IKN[s % 4][:, j, a, :],
                                     cache_idx_k[0, bass.ds(v, 1), :, :].rearrange("o p d -> (o p) d"))\
                            .then_inc(idx_in[s % 4], 16)
            for i in range(1, 4):
                load_chunk(('q', i))
            for k in ('k', 'v', 'sv'):
                for i in range(4):
                    load_chunk((k, i))

            for G in range(2):
                for kind, cache in ((0, cache_k), (1, cache_v)):
                    for n in range(64):
                        seq = 128 * G + 64 * kind + n
                        b, kp = (4 * G + n % 4, n // 4) if kind == 0 else (4 * G + n // 16, n % 16)
                        page_freed(sp, seq)
                        v = page_id(b, kp)
                        sp.dma_start(ring[seq % 8], cache[0, bass.ds(v, 1)].rearrange("o p h d -> (o p) (h d)"))\
                            .then_inc(page_in[seq % 8], 16)

            filled(sp, 'ot', 1, 3, 1)
            sp.dma_start(SG, bass.AP(sg_norm_g.tensor, 0, [[0, P], [1, 1024]])).then_inc(S_("sg_in"), 16)
            sp.dma_start(SB, bass.AP(sg_b.tensor, 0, [[0, P], [1, 1024]]).rearrange("p (g t) -> p g t", g=8))\
                .then_inc(S_("sg_in"), 16)
            sp.dma_start(WS, sg_w_s[0].rearrange("g t s -> t g s")).then_inc(S_("ws_in"), 16)
            for i in range(4):
                load_chunk(('su', i))
            for i in range(4):
                for k in ('gb', 'wb', 'ga', 'wa'):
                    load_chunk((k, i))
            for i in range(4):
                load_chunk(('out', i))
            for f in range(4):
                load_chunk(('up', f))
            raw = state_ffn_conv[0].rearrange("b w (f c) -> (b w f) c", c=P)
            sp.dma_start(SRAW[:, 0:5, :], raw[0:640, :].rearrange("(r p) c -> p r c", p=P)).then_inc(S_("state_in"), 16)
            sp.dma_start(SRAW[0:64, 5, :], raw[640:704, :]).then_inc(S_("state_in"), 16)
            for f in range(4, FB):
                load_chunk(('up', f))
            for c in range(8):
                for kh in range(2):
                    load_chunk(('dn', c, kh))
            sp.wait_ge(S_("conv_rows"), 1)
            filled(sp, 'ho', 1)
            drained(sp, 'ho', 1)
            sp.dma_start(conv_prompt[0].rearrange("o w (f c) -> (o w f) c", c=P), CO[0:88, 0, :])\
                .then_inc(S_("stored_sp"), 16)
            cs = conv_sample[0].rearrange("b w (f c) -> (b w f) c", c=P)
            sp.dma_start(cs[0:640, :].rearrange("(r p) c -> p r c", p=P), CO[:, 1:6, :]).then_inc(S_("stored_sp"), 16)
            sp.dma_start(cs[640:704, :], CO[0:64, 6, :]).then_inc(S_("stored_sp"), 16)
            for r in range(R):
                drained(sp, 'y', r, 0)
                drained(sp, 'y', r, 1)
                dst = y_prompt[0, P * r:P * r + P, :] if r < 4 else y_sample.rearrange("b s d -> (b s) d")
                sp.dma_start(dst, YO[r % 2][0:width(r), :]).then_inc(S_(f"y_stored{r % 2}"), 16)
            sp.wait_ge(S_("stored_sp"), 48)
            sp.wait_ge(S_("y_stored0"), 48)
            sp.wait_ge(S_("y_stored1"), 32)

        @block.gpsimd
        def _(pool):
            steps = [0]

            def link(ins):
                steps[0] += 1
                ins.then_inc(S_("pool_step"), 1)
                pool.wait_ge(S_("pool_step"), steps[0])

            link(pool.memset(IKPAD[64:128, 0, :], 0.0))
            link(pool.memset(IKPAD[0:64, 1, :], 0.0))
            link(pool.memset(Vn[64:128, :], 0.0))
            link(pool.memset(IQB[:, :, :], 0.0))
            pool.memset(ones[:, :], 1.0).then_inc(S_("ones_set"), 1)
            pool.wait_ge(S_("ones_set"), 1)
            pool.wait_ge(S_("rb_in"), 16)
            pool.tensor_copy(RBB, RBT[:, :, None].broadcast_to([32, H, P])).then_inc(S_("rbb_set"), 1)
            pool.wait_ge(S_("rbb_set"), 1)
            drained(pool, 'bias', H - 1)
            pool.dma_start(bias_scr, BV).then_inc(S_("bias_out"), 16)
            pool.wait_ge(S_("bias_out"), 16)
            pool.dma_start(BT, bass.AP(bias_scr.tensor, 127, [[H * BIASW - 1, P], [BIASW, H], [1, 256]]))\
                .then_inc(S_("bt_in"), 16)
            for g in range(2):
                for j in range(4):
                    for b in range(4):
                        pool.dma_start(NBr[32 * j + 8 * b:32 * j + 8 * b + 8, g, :],
                                       bass.AP(bias_scr.tensor, 127 + (4 * g + j) * BIASW,
                                               [[H * BIASW - 1, 8], [1, 136]])).then_inc(S_("nbr_in"), 16)
            drained(pool, 'ikw')
            drained(pool, 'iqsw')
            for a in range(2):
                rows = slice(64 * a, 64 * a + 64)
                d = IQB[rows, :, 64 * a:64 * a + 64].rearrange("p q (m e t) -> p q m e t", m=4, e=2)
                o = iqT[rows, :, TP:T].rearrange("p m (q u t) -> p q m u t", q=4, u=2)[:, :, :, a, :]
                w = IQSW[rows, :, :].rearrange("p m (q u t) -> p q m u t", q=4, u=2)[:, :, :, a, :]
                link(pool.tensor_copy(d[:, :, :, a, :], o))
                link(pool.tensor_copy(d[:, :, :, 1 - a, :], w))
            pool.memset(ST[:, 110:111], 0.0).then_inc(S_("iqb_ready"), 1)
            pool.wait_ge(S_("iw_ready"), 1)
            pool.dma_start(ik_prompt[0, 0].rearrange("(r p) d -> p r d", p=P), IKWT[:, 0:4, 0:64])\
                .then_inc(S_("stored_pool"), 16)
            pool.dma_start(ik_sample[0].rearrange("b s d -> (b s) d"), IKWT[0:TS, 4, 0:64])\
                .then_inc(S_("stored_pool"), 16)
            for r in range(R):
                drained(pool, 'kt', r, 1)
                drained(pool, 'kt', r, 0)
                dst = (k_prompt[0, 0, P * r:P * r + P].rearrange("p h d -> p (h d)") if r < 4
                       else k_sample[0].rearrange("b s h d -> (b s) (h d)"))
                pool.dma_start(dst, KO[r % 2][0:width(r), :]).then_inc(S_(f"k_stored{r % 2}"), 16)
            drained(pool, 'v', 3, 4)
            pool.dma_start(v_prompt[0, 0].rearrange("(r p) h d -> p r (h d)", p=P), V).then_inc(S_("v_stored"), 16)
            pool.dma_start(v_sample[0].rearrange("b s h d -> (b s) (h d)"), Vn[0:TS, :]).then_inc(S_("v_stored"), 16)
            pool.wait_ge(S_("sample_mask"), 1)
            pool.dma_start(mask_scr, S).then_inc(S_("mask_out"), 16)
            pool.wait_ge(S_("prompt_mask"), 1)
            pool.wait_ge(S_("bt_in"), 16)
            for h in range(H):
                if h >= 2:
                    drained(pool, 'pl', h - 2, 3)
                m = MB[h % 2]
                pool.tensor_tensor(m[:, 0:128], MS[:, 0:128], BT[:, h, 128:256], ALU.add)
                for r in range(1, 4):
                    o = SP_OFF[r] + P * (r - 1)
                    if r > 1:
                        pool.tensor_scalar(m[:, SP_OFF[r]:o], MS[:, SP_OFF[r]:o], BT[:, h, 0:1], None, ALU.add)
                    last = pool.tensor_tensor(m[:, o:o + 256], MS[:, o:o + 256], BT[:, h, :], ALU.add)
                last.then_inc(S_("bias_mask_ready"), 1)

            filled(pool, 'pv', H - 1)
            drained(pool, 'pv', H - 1)
            link(pool.memset(QZ, 0.0))
            link(pool.memset(kTn, 0.0))
            for G in range(2):
                for c in range(4):
                    b = 4 * G + c
                    pool.tensor_copy(QZ[:, :, b, 8 * c:8 * c + 8], qT[:, :, TP + 8 * b:TP + 8 * b + 8])
            pool.tensor_copy(QN, qT[:, :, TP:T])
            link(pool.tensor_copy(kTn[:, :, 0:TS], kT[:, :, TP:T]))
            pool.wait_ge(S_("v_stored"), 32)
            pool.wait_ge(S_("k_stored0"), 48)
            pool.wait_ge(S_("k_stored1"), 32)
            pool.wait_ge(S_("nbr_in"), 16 * 32)
            for g in range(2):
                pool.tensor_scalar(NBd[:, g, 0:128], NBr[:, g, 0:128], NBr[:, g, 0:1], None, ALU.subtract)
                pool.tensor_scalar(NBd[:, g, 128:192].rearrange("p (b t) -> p b t", b=8),
                                   NBr[:, g, None, 128:136].broadcast_to([P, 8, 8]), NBr[:, g, 0:1], None,
                                   ALU.subtract)
            link(pool.memset(NBd[:, :, 192:256], 0.0))
            pool.memset(ST[0:1, 110:111], 0.0).then_inc(S_("ring_free"), 1)
            pool.wait_ge(S_("mask_out"), 16)
            for G in range(2):
                if G:
                    drained(pool, 'kl', 0, NPG - 1)
                for j in range(4):
                    pool.dma_start(MG[32 * j:32 * j + 32, :], mask_scr[32 * G:32 * G + 32, :]).then_inc(S_("mg_in"), 16)

            pool.wait_ge(S_("ws_in"), 16)
            pool.affine_select(out=WS, in_=WS, pattern=[[0, 8], [-1, P]], compare_op=ALU.is_ge, fill=0.0,
                               base=0, channel_multiplier=1).then_inc(S_("ws_causal"), 1)
            pool.wait_ge(S_("sv_normed"), 1)
            pool.dma_start(sgv_sample[0].rearrange("b s d -> (b s) d"), SV[0:TS, 4, :]).then_inc(S_("stored_pool"), 16)
            for g in range(8):
                drained(pool, 'sgs', g)
                drained(pool, 'su', g)
                pool.tensor_tensor(obT[:, g, :], obT[:, g, :], TMPS[g % 2], ALU.mult).then_inc(S_("ob_ready"), 1)
            for c in range(8):
                drained(pool, 'wa', c)
                pool.tensor_tensor(halves(mT[:, c, :]), halves(mT[:, c, :]), SIGA[c % 2], ALU.add)\
                    .then_inc(S_("merged"), 1)
            filled(pool, 'rms', 1)
            pool.wait_ge(S_("stored_pool"), 48)
            for i in range(2):
                for k in range(2):
                    link(pool.memset(HPb[i][k][:, 0:2], 0.0))
            drained(pool, 'state', 1)
            for f in range(FB):
                for k in range(2):
                    fb = FB * k + f
                    hp = HPb[f % 2][k]
                    smp = hp[:, 514:594].rearrange("p (b c) -> p b c", b=8)
                    if f >= 2:
                        pool.wait_ge(S_("act_ready"), f - 1)
                    pool.tensor_copy(smp[:, :, 0:2],
                                     STT_.rearrange("p (b w f) -> p b w f", b=8, w=2)[:, :, :, fb])\
                        .then_inc(S_("state_put"), 1)
                for k in range(2):
                    fb = FB * k + f
                    hp = HPb[f % 2][k]
                    smp = hp[:, 514:594].rearrange("p (b c) -> p b c", b=8)
                    drained(pool, 'up', f, k)
                    pool.tensor_copy(HCP.rearrange("p (w f) -> p w f", w=2)[:, :, fb], hp[:, 512:514])
                    last = pool.tensor_copy(HCS.rearrange("p (b w f) -> p b w f", b=8, w=2)[:, :, :, fb],
                                            smp[:, :, 8:10])
                last.then_inc(S_("conv_rows"), 1)

        @block.tensor
        def _(pe):
            def done(ins, *n):
                ins.then_inc(single_filled if n in single.slots else pair_filled, 1)

            def arrived(name):
                slot, value, _ = chunks[name]
                pe.wait_ge(weights_in[slot], value)
                return W[slot]

            def project(name, lhs, rhs, nk, first_wait=None):
                claim(pe, *name)
                m = lhs(0).shape[-1]
                for a in range(2):
                    for k in range(nk):
                        if first_wait and a == 0:
                            first_wait(k)
                        last = pe.matmul(ptile(*name)[0:m, a, :], lhs(k), rhs(k)[:, HALF * a:HALF * a + HALF],
                                         start=(k == 0), stop=(k == nk - 1))
                done(last, *name)

            def rms_sum(i):
                pe.wait_ge(S_("squares_act"), i + 1)
                pe.wait_ge(S_("squares_dve"), i + 1)
                project(('rms', i), lambda k: ones[:, :], lambda k: xnT[:, k, :], KT)

            def xn(k):
                return xnT[:, k, :]

            pe.wait_ge(S_("consts_in"), 16)
            pe.wait_ge(S_("x_in"), 32)
            for r in range(R):
                for q in range(2):
                    claim(pe, 'x', r, q)
                    w = width(r)
                    for i in range(4):
                        last = pe.transpose(bank('x', r, q)[:, P * i:P * i + w],
                                            XL[0:w, r, P * (4 * q + i):P * (4 * q + i) + P], ident[0:w, 0:w])
                    done(last, 'x', r, q)
            pe.wait_ge(S_("vec_in"), 96)
            claim(pe, 'vec')
            pe.transpose(bank('vec')[:, 0:128], VR[:, 0, :], ident)
            done(pe.transpose(bank('vec')[:, 128:200], VR[0:72, 1, :], ident[0:72, 0:72]), 'vec')
            pe.wait_ge(S_("rbb_set"), 1)
            for h in range(H):
                claim(pe, 'bias', h)
                done(pe.matmul(bank('bias', h)[:, 0:BIASW], RBB[:, h, :], const('bucket', 32), start=True, stop=True),
                     'bias', h)
            pe.wait_ge(S_("ones_set"), 1)
            rms_sum(0)
            for m in range(4):
                w = blocks(arrived(('iq', m // 2))[:, :], KT)
                project(('iq', m), lambda k: w[:, k, P * (m % 2):P * (m % 2) + P], xn, KT,
                        (lambda k: pe.wait_ge(S_("xn_ready"), k + 1)) if m == 0 else None)
            w = blocks(arrived(('ikw',))[:, 0:576], KT)
            project(('ikw',), lambda k: w[:, k, :], xn, KT)
            drained(pe, 'iq', 3)
            claim(pe, 'iqsw')
            for m in range(4):
                last = pe.matmul(bank('iqsw')[:, 64 * m:64 * m + 64], const('swap'), iqT[:, m, TP:T],
                                 start=True, stop=True)
            done(last, 'iqsw')
            drained(pe, 'ikw')
            for i, (a, b) in enumerate(((0, TP), (TP, T))):
                claim(pe, f'ikd{i}')
                done(pe.matmul(bank(f'ikd{i}')[:, 0:b - a], const('dup', 72), IKW[0:72, a:b], start=True, stop=True),
                     f'ikd{i}')
            claim(pe, 'ikwT')
            for r in range(R):
                last = pe.transpose(bank('ikwT')[0:width(r), 72 * r:72 * r + 72],
                                    IKW[0:72, P * r:P * r + width(r)], ident[0:72, 0:72])
            done(last, 'ikwT')
            pe.wait_ge(S_("iw_ready"), 1)
            claim(pe, 'iwrep')
            for p in range(4):
                last = pe.matmul(bank('iwrep')[:, 8 * p:8 * p + 8], const('selp', TS)[:, P * p:P * p + P],
                                 IWS[0:TS, 4, :], start=True, stop=True)
            done(last, 'iwrep')
            drained(pe, 'ikd0')
            for r in range(1, 4):
                for h in range(H):
                    claim(pe, 'ps', r, h)
                    done(pe.matmul(bank('ps', r, h)[:, 0:P * (r + 1)], iqT[:, h // 2, P * r:P * r + P],
                                   IKPAD[:, h % 2, 0:P * (r + 1)], start=True, stop=True), 'ps', r, h)
            pe.wait_ge(S_("iqb_ready"), 1)
            pe.wait_ge(S_("swm_ready"), 1)
            for s in range(18):
                if s < 16:
                    pe.wait_ge(idx_in[s % 4], 128 * (s // 4 + 1))
                    claim(pe, 't', s)
                    for j in range(4):
                        last = pe.transpose(bank('t', s)[:, P * j:P * j + P],
                                            IKN[s % 4][:, j, :, :].rearrange("p a d -> p (a d)"), ident)
                    done(last, 't', s)
                if 1 <= s < 17:
                    drained(pe, 't', s - 1)
                    claim(pe, 's1', s - 1)
                    done(pe.matmul(bank('s1', s - 1), IQB[:, (s - 1) % 4, :], IKT[(s - 1) % 2], start=True, stop=True),
                         's1', s - 1)
                if s >= 2:
                    kc, p = (s - 2) // 4, (s - 2) % 4
                    drained(pe, 's1', s - 2)
                    if p == 0:
                        claim(pe, 'ss', kc)
                    last = pe.matmul(pbank('ss', kc)[0:TS, 0, :], SWM[:, p, :], RL2[(s - 2) % 2],
                                     start=(p == 0), stop=(p == 3))
                    if p == 3:
                        done(last, 'ss', kc)
                    else:
                        last.then_inc(S_("heads_summed"), 1)
            drained(pe, 'ikd1')
            claim(pe, 's1n')
            for p in range(4):
                last = pe.matmul(bank('s1n')[:, 8 * p:8 * p + 8], IQB[:, p, :], IKNEW[:, p, :], start=True, stop=True)
            done(last, 's1n')
            drained(pe, 's1n')
            claim(pe, 'ssn')
            for p in range(4):
                last = pe.matmul(pbank('ssn')[0:TS, 0, 0:8], SWM[:, p, :], RLN[:, 8 * p:8 * p + 8],
                                 start=(p == 0), stop=(p == 3))
            done(last, 'ssn')

            def project_pairs(kind):
                for c in range(8):
                    w = blocks(arrived((kind, c // 2))[:, :], KT)
                    project((kind, c), lambda k: w[:, k, P * (c % 2):P * (c % 2) + P], xn, KT)

            def project_rows(kind):
                for c in range(4):
                    w = blocks(arrived((kind, c))[:, :], KT)
                    for r in range(R):
                        claim(pe, kind, c, r)
                        for k in range(KT):
                            last = pe.matmul(pbank(kind, c, r)[0:width(r), 0, 0:256],
                                             xnT[:, k, P * r:P * r + width(r)], w[:, k, :],
                                             start=(k == 0), stop=(k == KT - 1))
                        done(last, kind, c, r)

            project_pairs('q')
            project_pairs('k')
            drained(pe, 'k', 7)
            for r in range(R):
                for q in range(2):
                    claim(pe, 'kt', r, q)
                    for i in range(4):
                        last = pe.transpose(bank('kt', r, q)[0:width(r), P * i:P * i + P],
                                            kT[:, 4 * q + i, P * r:P * r + width(r)], ident)
                    done(last, 'kt', r, q)
            project_rows('v')
            drained(pe, 'v', 3, 4)
            for h in range(H + 1):
                if h < H:
                    for r in range(4):
                        claim(pe, 'pl', h, r)
                        done(pe.matmul(bank('pl', h, r)[:, 0:P * (r + 1)], qT[:, h, P * r:P * r + P],
                                       kT[:, h, 0:P * (r + 1)], start=True, stop=True), 'pl', h, r)
                if h:
                    drained(pe, 'pt', h - 1, 3)
                    claim(pe, 'pv', h - 1)
                    for s in range(4):
                        last = pe.matmul(bank('pv', h - 1)[:, P * s:TP], V[:, s, HD * (h - 1):HD * h],
                                         PT[:, s, P * s:TP], start=(s == 0), stop=(s == 3), skip_group_check=True)
                    done(last, 'pv', h - 1)
                if h < H:
                    for r in range(4):
                        pe.wait_ge(S_("probs_ready"), 4 * h + r + 1)
                        claim(pe, 'pt', h, r)
                        for s in range(r + 1):
                            last = pe.transpose(bank('pt', h, r)[:, P * s:P * s + P],
                                                L[:, SP_OFF[r] + P * s:SP_OFF[r] + P * s + P], ident)
                        done(last, 'pt', h, r)

            pe.wait_ge(S_("ring_free"), 1)
            for G in range(2):
                for n in range(65):
                    if n < 64:
                        seq = 128 * G + n
                        pe.wait_ge(page_in[seq % 8], 16 * (seq // 8 + 1))
                        for u in range(2):
                            claim(pe, 'kp', G, n, u)
                            for i in range(4):
                                h = 4 * u + i
                                last = pe.transpose(bank('kp', G, n, u)[:, P * i:P * i + P],
                                                    ring[seq % 8][:, HD * h:HD * h + HD], ident)
                            done(last, 'kp', G, n, u)
                    if n:
                        kp, bb = (n - 1) // 4, (n - 1) % 4
                        if bb == 0:
                            claim(pe, 'kl', G, kp)
                        for u in range(2):
                            drained(pe, 'kp', G, n - 1, u)
                            for j in range(4):
                                h = 4 * u + j
                                last = pe.matmul(pbank('kl', G, kp)[32 * j:32 * j + 32, u, 0:P],
                                                 QZ[:, h, 4 * G + bb, :], KTb[(n - 1) % 2][:, h, :],
                                                 start=(bb == 0), stop=(bb == 3))
                        if bb == 3:
                            done(last, 'kl', G, kp)
                claim(pe, 'kl', G, NPG - 1)
                for u in range(2):
                    for j in range(4):
                        h = 4 * u + j
                        last = pe.matmul(pbank('kl', G, NPG - 1)[32 * j:32 * j + 32, u, 0:P],
                                         QN[:, h, 32 * G:32 * G + 32], kTn[:, h, :], start=True, stop=True)
                done(last, 'kl', G, NPG - 1)
                for g in range(2):
                    pe.wait_ge(S_("sample_probs"), 2 * G + g + 1)
                    for q in range(5):
                        claim(pe, 'st', G, g, q)
                        for i in range(4 if q < 4 else 1):
                            c = P * (4 * q + i)
                            last = pe.transpose(bank('st', G, g, q)[:, P * i:P * i + P], LS[:, g, c:c + P], ident)
                        done(last, 'st', G, g, q)
                drained(pe, 'st', G, 0, 4)
                drained(pe, 'st', G, 1, 4)
                for b in range(4):
                    claim(pe, 'o', G, b)
                    for kp in range(NPG):
                        if kp < NPAGES:
                            seq = 128 * G + 64 + 16 * b + kp
                            pe.wait_ge(page_in[seq % 8], 16 * (seq // 8 + 1))
                            page = ring[seq % 8]
                        else:
                            page = Vn[:, :]
                        for u in range(2):
                            for j in range(4):
                                h = 4 * u + j
                                last = pe.matmul(pbank('o', G, b)[32 * j:32 * j + 32, u, 0:HD],
                                                 PTs[:, u, kp, 32 * j:32 * j + 32], page[:, HD * h:HD * h + HD],
                                                 start=(kp == 0), stop=(kp == NPG - 1))
                        if kp < NPAGES:
                            last.then_inc(S_("v_pages_used"), 1)
                        else:
                            done(last, 'o', G, b)
                    drained(pe, 'o', G, b)
                    for g in range(2):
                        claim(pe, 'ot', G, b, g)
                        done(pe.transpose(bank('ot', G, b, g)[:, 0:P], OS[b % 2][:, g, :], ident), 'ot', G, b, g)

            project_rows('sv')
            project_pairs('su')
            pe.wait_ge(S_("ws_causal"), 1)
            for q in range(2):
                claim(pe, 'w', q)
                for i in range(4):
                    last = pe.transpose(bank('w', q)[:, P * i:P * i + P], WS[:, 4 * q + i, :], ident)
                done(last, 'w', q)
            drained(pe, 'w', 1)
            claim(pe, 'bd')
            done(pe.matmul(bank('bd')[0:TS, 0:64], const('rep', 8), WT[0:8, :, 0:8], start=True, stop=True), 'bd')
            pe.wait_ge(S_("sv_normed"), 1)
            pe.wait_ge(S_("bd_ready"), 1)
            for g in range(8):
                claim(pe, 'sg', g)
                for c in range(4):
                    last = pe.matmul(bank('sg', g)[:, P * c:P * c + P], SV[:, c, P * g:P * g + P], WT[:, g, :],
                                     start=True, stop=True)
                done(last, 'sg', g)
                claim(pe, 'sgs', g)
                done(pe.matmul(bank('sgs', g)[:, 0:TS], SV[0:TS, 4, P * g:P * g + P], BD[:, g, :],
                               start=True, stop=True), 'sgs', g)
            for i in range(4):
                for kind in ('gb', 'wb', 'ga', 'wa'):
                    w = blocks(arrived((kind, i))[:, :], KT)
                    for c in (2 * i, 2 * i + 1):
                        src = {'wb': obT, 'wa': oaT}.get(kind, xnT)
                        if kind == 'wb' and c == 0:
                            pe.wait_ge(S_("ob_ready"), 8)
                        if kind == 'wa' and c == 0:
                            drained(pe, 'ot', 1, 3, 1)
                            drained(pe, 'ot', 1, 3, 0)
                        project((kind, c), lambda k: w[:, k, P * (c % 2):P * (c % 2) + P], lambda k: src[:, k, :], KT)
            pe.wait_ge(S_("merged"), 8)
            for c in range(8):
                w = blocks(arrived(('out', c // 2))[:, :], KT)
                project(('out', c), lambda k: w[:, k, P * (c % 2):P * (c % 2) + P], lambda k: mT[:, k, :], KT)
            rms_sum(1)
            pe.wait_ge(S_("state_in"), 32)
            for q in range(2):
                claim(pe, 'state', q)
                for i in range(4 if q == 0 else 2):
                    n = 64 if (q, i) == (1, 1) else P
                    last = pe.transpose(bank('state', q)[:, P * i:P * i + n], SRAW[0:n, 4 * q + i, :], ident[0:n, 0:n])
                done(last, 'state', q)
            for f in range(FB):
                w = blocks(arrived(('up', f))[:, :], KT)
                for k2 in range(2):
                    project(('up', f, k2), lambda k: w[:, k, P * k2:P * k2 + P], xn, KT,
                            (lambda k: pe.wait_ge(S_("xn_ready"), 8 + k + 1)) if (f, k2) == (0, 0) else None)
            for c in range(8):
                ws = [blocks(W[chunks['dn', c, kh][0]][:, 0:1408], 11) for kh in range(2)]
                arrived(('dn', c, 0))
                arrived(('dn', c, 1))
                project(('dn', c), lambda k: ws[k // 11][:, k % 11, :], lambda k: act_block(k), FB,
                        (lambda k: pe.wait_ge(S_("act_ready"), k + 1)) if c == 0 else None)
            pe.wait_ge(S_("conv_rows"), FB)
            for q in range(2):
                claim(pe, 'ho', q)
                for i in range(4 if q == 0 else 3):
                    n = 4 * q + i
                    src = HCP if n == 0 else HCS[:, P * (n - 1):min(P * n, 704)]
                    m = src.shape[-1]
                    last = pe.transpose(bank('ho', q)[0:m, P * i:P * i + P], src, ident)
                done(last, 'ho', q)
            rms_sum(2)
            pe.wait_ge(S_("xn_ready"), 24)
            for r in range(R):
                for q in range(2):
                    claim(pe, 'y', r, q)
                    for i in range(4):
                        last = pe.transpose(bank('y', r, q)[0:width(r), P * i:P * i + P],
                                            xnT[:, 4 * q + i, P * r:P * r + width(r)], ident)
                    done(last, 'y', r, q)

        @block.scalar
        def _(act):
            def squares(i):
                act.activation(xnT[:, 0:4, :], xT[:, 0:4, :], ACT.Square).then_inc(S_("squares_act"), 1)

            def root(i):
                drained(act, 'rms', i)
                act.activation(RS, RS, ACT.Sqrt).then_inc(S_("rms_root"), 1)

            for r in range(R):
                filled(act, 'x', r, 0)
                act.activation(xT[:, 0:4, P * r:P * r + width(r)], blocks(bank('x', r, 0), 4)[:, :, 0:width(r)],
                               ACT.Copy).then_inc(drains('x', r, 0), 1)
            drained(act, 'x', R - 1, 0)
            squares(0)
            for h in range(H):
                filled(act, 'bias', h)
                act.activation(BV[:, h, :], bank('bias', h)[:, 0:BIASW], ACT.Copy).then_inc(drains('bias', h), 1)
            root(0)
            for m in range(4):
                filled(act, 'iq', m)
                act.activation(halves(iqT[:, m, :]), ptile('iq', m), ACT.Copy).then_inc(drains('iq', m), 1)
            filled(act, 'ikw')
            act.activation(halves(IKW[0:72, :]), ptile('ikw')[0:72], ACT.Copy).then_inc(drains('ikw'), 1)
            k = 0
            for r in range(1, 4):
                for h in range(H):
                    filled(act, 'ps', r, h)
                    if k >= 2:
                        act.wait_ge(S_("relu_used"), k - 1)
                    act.activation(RL[k % 2][:, 0:P * (r + 1)], bank('ps', r, h)[:, 0:P * (r + 1)], ACT.Relu)\
                        .then_inc(drains('ps', r, h), 1)
                    k += 1
            for s in range(17):
                if s < 16:
                    filled(act, 't', s)
                    if s >= 2:
                        filled(act, 's1', s - 2)
                    act.activation(IKT[s % 2], bank('t', s), ACT.Copy).then_inc(drains('t', s), 1)
                if s >= 1:
                    filled(act, 's1', s - 1)
                    if s >= 3:
                        kc, p = (s - 3) // 4, (s - 3) % 4
                        if p == 3:
                            filled(act, 'ss', kc)
                        else:
                            act.wait_ge(S_("heads_summed"), 3 * kc + p + 1)
                    act.activation(RL2[(s - 1) % 2], bank('s1', s - 1), ACT.Relu).then_inc(drains('s1', s - 1), 1)
            filled(act, 's1n')
            act.activation(RLN, bank('s1n')[:, 0:32], ACT.Relu).then_inc(drains('s1n'), 1)
            for c in range(8):
                filled(act, 'q', c)
                act.activation(halves(qT[:, c, :]), ptile('q', c), ACT.Copy, scale=ATT_SCALE).then_inc(drains('q', c), 1)
            act.wait_ge(S_("bias_out"), 16)
            for c in range(8):
                filled(act, 'k', c)
                act.activation(halves(kT[:, c, :]), ptile('k', c), ACT.Copy).then_inc(drains('k', c), 1)
            for r in range(R):
                for q in range(2):
                    filled(act, 'kt', r, q)
                    if r >= 2 and q == 0:
                        act.wait_ge(S_(f"k_stored{r % 2}"), 16 * (r // 2))
                    act.activation(KO[r % 2][0:width(r), 512 * q:512 * q + 512], bank('kt', r, q)[0:width(r)],
                                   ACT.Copy).then_inc(drains('kt', r, q), 1)
            for c in range(4):
                for r in range(R):
                    filled(act, 'v', c, r)
                    dst = V[:, r, 256 * c:256 * c + 256] if r < 4 else Vn[0:TS, 256 * c:256 * c + 256]
                    act.activation(dst, pbank('v', c, r)[0:width(r), 0, 0:256], ACT.Copy).then_inc(drains('v', c, r), 1)
            for h in range(H + 1):
                if h < H:
                    act.wait_ge(S_("max_ready"), h + 1)
                    for r in range(4):
                        n, o = P * (r + 1), SP_OFF[r]
                        last = act.activation(L[:, o:o + n], L[:, o:o + n], ACT.Exp, bias=NM[h % 2][:, r:r + 1],
                                              accum_out=SU[h % 2][:, r:r + 1])
                    last.then_inc(S_("exp_done"), 1)
                if h:
                    filled(act, 'pv', h - 1)
                    act.activation(oaT[:, h - 1, 0:TP], bank('pv', h - 1), ACT.Copy).then_inc(drains('pv', h - 1), 1)
                if h < H:
                    if h == 0:
                        act.wait_ge(S_("k_stored0"), 48)
                        act.wait_ge(S_("k_stored1"), 32)
                    for r in range(4):
                        filled(act, 'pt', h, r)
                        act.activation(PT[:, 0:r + 1, P * r:P * r + P], blocks(bank('pt', h, r), 4)[:, 0:r + 1, :],
                                       ACT.Copy).then_inc(drains('pt', h, r), 1)
            for G in range(2):
                for n in range(64):
                    filled(act, 'kp', G, n, 0)
                    act.activation(KTb[n % 2][:, 0:4, :], blocks(bank('kp', G, n, 0), 4), ACT.Copy)\
                        .then_inc(drains('kp', G, n, 0), 1)
                act.wait_ge(S_("sample_max"), G + 1)
                for g in range(2):
                    act.activation(LS[:, g, :], LS[:, g, :], ACT.Exp, bias=NM[0][:, g:g + 1],
                                   accum_out=SU[0][:, g:g + 1]).then_inc(S_("sample_exp"), 1)
                for q in range(5):
                    filled(act, 'st', G, 0, q)
                    m = 4 if q < 4 else 1
                    act.activation(PTs[:, 0, 4 * q:4 * q + m, :], blocks(bank('st', G, 0, q), 4)[:, 0:m, :], ACT.Copy)\
                        .then_inc(drains('st', G, 0, q), 1)
                for b in range(4):
                    t = TP + 32 * G + 8 * b
                    for g in range(2):
                        filled(act, 'ot', G, b, g)
                        act.activation(oaT[:, 4 * g:4 * g + 4, t:t + 8],
                                       blocks(bank('ot', G, b, g)[:, 0:P], 4)[:, :, 8 * b:8 * b + 8], ACT.Copy)\
                            .then_inc(drains('ot', G, b, g), 1)
            for c in range(4):
                for r in range(R):
                    filled(act, 'sv', c, r)
                    act.activation(SV[0:width(r), r, 256 * c:256 * c + 256], pbank('sv', c, r)[0:width(r), 0, 0:256],
                                   ACT.Gelu_apprx_tanh).then_inc(drains('sv', c, r), 1)
            for c in range(8):
                filled(act, 'su', c)
                act.activation(halves(obT[:, c, :]), ptile('su', c), ACT.Gelu_apprx_tanh).then_inc(drains('su', c), 1)
                if c == 1:
                    act.wait_ge(S_("sv_mean"), 1)
                    act.activation(SS, SS, ACT.Sqrt).then_inc(S_("sv_root"), 1)
            for i in range(4):
                for kind in ('gb', 'ga'):
                    for c in (2 * i, 2 * i + 1):
                        filled(act, kind, c)
                        if kind == 'gb':
                            if c >= 2:
                                drained(act, 'wb', c - 2)
                            dst = SIGB[c % 2]
                        else:
                            if c >= 2:
                                act.wait_ge(S_("merged"), c - 1)
                            dst = SIGA[c % 2]
                        act.activation(dst, ptile(kind, c), ACT.Sigmoid).then_inc(drains(kind, c), 1)
            drained(act, 'out', 3)
            drained(act, 'out', 2)
            filled(act, 'out', 7)
            squares(1)
            root(1)
            for f in range(FB):
                for k in range(2):
                    filled(act, 'up', f, k)
                    if f >= 2:
                        act.wait_ge(S_("act_ready"), f - 1)
                        act.wait_ge(S_("conv_rows"), f - 1)
                    hp, pt = HPb[f % 2][k], pbank('up', f, k)
                    act.activation(hp[:, 2:2 + HALF], pt[:, 0, 0:HALF], ACT.Copy)
                    act.activation(hp[:, 2 + HALF:514], pt[:, 1, 0:TP - HALF], ACT.Copy)
                    act.activation(hp[:, 514:594].rearrange("p (b c) -> p b c", b=8)[:, :, 2:10],
                                   pt[:, 1, TP - HALF:HALF].rearrange("p (b c) -> p b c", b=8), ACT.Copy)\
                        .then_inc(drains('up', f, k), 1)
                    drained(act, 'up', f, k)
                    act.wait_ge(S_("state_put"), 2 * f + k + 1)
                    fb = FB * k + f
                    act.activation(CB[f % 2][k], hp[:, 2:594], ACT.Identity, bias=VT[:, 156 + fb:157 + fb],
                                   scale=VT[:, 112 + fb:113 + fb]).then_inc(S_("tap2_done"), 1)
                act.wait_ge(S_("taps_done"), 2 * f + 1)
                act.activation(CB[f % 2][0], CB[f % 2][0], ACT.Silu).then_inc(S_("silu_done"), 1)
            drained(act, 'dn', 3)
            drained(act, 'dn', 2)
            filled(act, 'dn', 7)
            squares(2)
            root(2)
            for r in range(R):
                filled(act, 'y', r, 0)
                if r >= 2:
                    act.wait_ge(S_(f"y_stored{r % 2}"), 16 * (r // 2))
                act.activation(YO[r % 2][0:width(r), 0:512], bank('y', r, 0)[0:width(r)], ACT.Copy)\
                    .then_inc(drains('y', r, 0), 1)

        @block.vector
        def _(dve):
            steps = [0]

            def link(ins):
                steps[0] += 1
                ins.then_inc(S_("dve_step"), 1)
                dve.wait_ge(S_("dve_step"), steps[0])

            def squares(i):
                dve.tensor_tensor(xnT[:, 4:8, :], xT[:, 4:8, :], xT[:, 4:8, :], ALU.mult).then_inc(S_("squares_dve"), 1)

            def normalise(i, gcol):
                filled(dve, 'rms', i)
                dve.tensor_scalar(halves(RS), ptile('rms', i), 1.0 / D, EPS, ALU.mult, ALU.add)\
                    .then_inc(drains('rms', i), 1)
                dve.wait_ge(S_("rms_root"), i + 1)
                link(dve.reciprocal(RS, RS))
                for k in range(KT):
                    dve.scalar_tensor_tensor(xnT[:, k, :], xT[:, k, :], VT[:, gcol + k:gcol + k + 1], RS,
                                             ALU.mult, ALU.mult).then_inc(S_("xn_ready"), 1)

            for r in range(R):
                filled(dve, 'x', r, 1)
                dve.tensor_copy(xT[:, 4:8, P * r:P * r + width(r)], blocks(bank('x', r, 1), 4)[:, :, 0:width(r)])\
                    .then_inc(drains('x', r, 1), 1)
            drained(dve, 'x', R - 1, 1)
            squares(0)
            filled(dve, 'vec')
            dve.tensor_copy(VT[:, :], bank('vec')[:, 0:200]).then_inc(drains('vec'), 1)
            drained(dve, 'vec')
            drained(dve, 'x', R - 1, 0)
            normalise(0, 0)
            dve.wait_ge(S_("consts_in"), 16)
            dve.tensor_copy(MS[:, 0:P], const('caus'))
            filled(dve, 'iqsw')
            dve.tensor_copy(IQSW, blocks(bank('iqsw')[:, 0:256], 4)).then_inc(drains('iqsw'), 1)
            filled(dve, 'ikd0')
            dve.tensor_copy(IKPAD[0:64, 0, :], bank('ikd0')[0:64])
            dve.tensor_copy(IKPAD[64:128, 1, :], bank('ikd0')[64:128]).then_inc(drains('ikd0'), 1)
            filled(dve, 'ikd1')
            nk = bank('ikd1')[:, 0:64].rearrange("p (q u t) -> p q u t", q=4, u=2)
            dve.tensor_copy(IKNEW[0:64], nk[0:64, :, 0, :])
            dve.tensor_copy(IKNEW[64:128], nk[64:128, :, 1, :]).then_inc(drains('ikd1'), 1)
            filled(dve, 'ikwT')
            dve.tensor_copy(IKWT[:, 0:4, :], blocks(bank('ikwT')[:, 0:288], 4))
            dve.tensor_copy(IKWT[0:TS, 4, :], bank('ikwT')[0:TS, 288:360]).then_inc(drains('ikwT'), 1)
            drained(dve, 'ikwT')
            dve.tensor_scalar(IWS[:, 0:4, :], IKWT[:, 0:4, 64:72], IDX_SCALE, None, ALU.mult)
            dve.tensor_scalar(IWS[0:TS, 4, :], IKWT[0:TS, 4, 64:72], IDX_SCALE, None, ALU.mult)\
                .then_inc(S_("iw_ready"), 1)
            filled(dve, 'iwrep')
            dve.tensor_tensor(TMP32, blocks(bank('iwrep')[:, 0:32], 4),
                              const('hmask')[:, None, :].broadcast_to([P, 4, 8]), ALU.mult).then_inc(drains('iwrep'), 1)
            drained(dve, 'iwrep')
            link(dve.tensor_reduce(IWC, TMP32, AX_X, ALU.add))
            for p in range(4):
                last = dve.tensor_scalar(SWM[:, p, :], const('selT')[:, TS * p:TS * p + TS], IWC[:, p:p + 1], None,
                                         ALU.mult)
            last.then_inc(S_("swm_ready"), 1)
            k = 0
            for r in range(1, 4):
                n, o = P * (r + 1), SP_OFF[r]
                for h in range(H):
                    drained(dve, 'ps', r, h)
                    if h == 0:
                        dve.tensor_scalar(MS[:, o:o + n], RL[k % 2][:, 0:n], IWS[:, r, h:h + 1], None, ALU.mult)\
                            .then_inc(S_("relu_used"), 1)
                    else:
                        dve.wait_ge(S_("relu_used"), k)
                        dve.scalar_tensor_tensor(MS[:, o:o + n], RL[k % 2][:, 0:n], IWS[:, r, h:h + 1],
                                                 MS[:, o:o + n], ALU.mult, ALU.add).then_inc(S_("relu_used"), 1)
                    k += 1
                dve.wait_ge(S_("relu_used"), k)
                link(dve.tensor_tensor(MS[:, o + P * r:o + n], MS[:, o + P * r:o + n], const('caus'), ALU.add))
            for kc in range(4):
                filled(dve, 'ss', kc)
                dve.tensor_copy(S[:, 512 * kc:512 * kc + 512], pbank('ss', kc)[0:TS, 0, :]).then_inc(drains('ss', kc), 1)
            filled(dve, 'ssn')
            dve.tensor_tensor(S[:, PAST:NKEY], pbank('ssn')[0:TS, 0, 0:8], const('newcausal', TS), ALU.add)\
                .then_inc(drains('ssn'), 1)
            drained(dve, 'ssn')
            for _ in range(TOPK_S // 8):
                link(dve.max(MAX8, S[:, 0:NKEY]))
                link(dve.match_replace(S[:, 0:NKEY], MAX8, S[:, 0:NKEY], MARK))
            link(dve.tensor_scalar(M8, S[:, PAST:NKEY], MARK, NEG, ALU.not_equal, ALU.mult))
            dve.tensor_scalar(S[:, 0:PAST], S[:, 0:PAST], MARK, NEG, ALU.not_equal, ALU.mult)
            dve.memset(S[:, PAST + TS:NCOL], NEG)
            dve.tensor_tensor(S[:, PAST:PAST + TS].rearrange("p (b t) -> p b t", b=8),
                              const('newblock', TS).rearrange("p (b t) -> p b t", b=8),
                              M8[:, None, :].broadcast_to([TS, 8, 8]), ALU.add).then_inc(S_("sample_mask"), 1)
            for r in range(1, 4):
                n, o = P * (r + 1), SP_OFF[r]
                for _ in range(TOPK_P // 8):
                    link(dve.max(MAX8P, MS[:, o:o + n]))
                    link(dve.match_replace(MS[:, o:o + n], MAX8P, MS[:, o:o + n], MARK))
                last = dve.tensor_scalar(MS[:, o:o + n], MS[:, o:o + n], MARK, NEG, ALU.not_equal, ALU.mult)
            last.then_inc(S_("prompt_mask"), 1)
            for h in range(H):
                dve.wait_ge(S_("bias_mask_ready"), h + 1)
                for r in range(4):
                    n, o = P * (r + 1), SP_OFF[r]
                    filled(dve, 'pl', h, r)
                    dve.tensor_tensor_reduce(out=L[:, o:o + n], in0=bank('pl', h, r)[:, 0:n], in1=MB[h % 2][:, o:o + n],
                                             scale=1.0, scalar=MARK, op0=ALU.add, op1=ALU.max,
                                             accum_out=MX[h % 2][:, r:r + 1]).then_inc(drains('pl', h, r), 1)
                drained(dve, 'pl', h, 3)
                dve.tensor_scalar(NM[h % 2], MX[h % 2], -1.0, None, ALU.mult).then_inc(S_("max_ready"), 1)
                dve.wait_ge(S_("exp_done"), h + 1)
                link(dve.reciprocal(RC[h % 2], SU[h % 2]))
                for r in range(4):
                    n, o = P * (r + 1), SP_OFF[r]
                    dve.tensor_scalar(L[:, o:o + n], L[:, o:o + n], RC[h % 2][:, r:r + 1], None, ALU.mult)\
                        .then_inc(S_("probs_ready"), 1)
            for G in range(2):
                dve.wait_ge(S_("mg_in"), 64 * (G + 1))

                def logits(kp):
                    filled(dve, 'kl', G, kp)
                    for g in range(2):
                        last = dve.scalar_tensor_tensor(LS[:, g, P * kp:P * kp + P], pbank('kl', G, kp)[:, g, 0:P],
                                                        NBr[:, g, 0:1], MG[:, P * kp:P * kp + P], ALU.add, ALU.add)
                    last.then_inc(drains('kl', G, kp), 1)

                for n in range(64):
                    filled(dve, 'kp', G, n, 1)
                    dve.tensor_copy(KTb[n % 2][:, 4:8, :], blocks(bank('kp', G, n, 1), 4))\
                        .then_inc(drains('kp', G, n, 1), 1)
                    if n % 4 == 0 and n:
                        logits(n // 4 - 1)
                logits(15)
                logits(16)
                drained(dve, 'kl', G, 16)
                link(dve.tensor_tensor(LS[:, :, 1920:NCOL], LS[:, :, 1920:NCOL], NBd, ALU.add))
                link(dve.tensor_reduce(MX[0][:, 0:2], LS, AX_X, ALU.max))
                dve.tensor_scalar(NM[0][:, 0:2], MX[0][:, 0:2], -1.0, None, ALU.mult).then_inc(S_("sample_max"), 1)
                for g in range(2):
                    dve.wait_ge(S_("sample_exp"), 2 * G + g + 1)
                    link(dve.reciprocal(RC[0][:, g:g + 1], SU[0][:, g:g + 1]))
                    dve.tensor_scalar(LS[:, g, :], LS[:, g, :], RC[0][:, g:g + 1], None, ALU.mult)\
                        .then_inc(S_("sample_probs"), 1)
                for q in range(5):
                    filled(dve, 'st', G, 1, q)
                    m = 4 if q < 4 else 1
                    dve.tensor_copy(PTs[:, 1, 4 * q:4 * q + m, :], blocks(bank('st', G, 1, q), 4)[:, 0:m, :])\
                        .then_inc(drains('st', G, 1, q), 1)
                for b in range(4):
                    filled(dve, 'o', G, b)
                    if b >= 2:
                        filled(dve, 'ot', G, b - 2, 1)
                    dve.tensor_copy(OS[b % 2], pbank('o', G, b)[:, :, 0:HD]).then_inc(drains('o', G, b), 1)
            link(dve.memset(SS, 1.0))
            dve.wait_ge(S_("sg_in"), 32)
            for r in range(R):
                w = width(r)
                drained(dve, 'sv', 3, r)
                link(dve.tensor_tensor_reduce(out=JUNK[0:w], in0=SV[0:w, r, :], in1=SV[0:w, r, :], scale=1.0, scalar=0.0,
                                              op0=ALU.mult, op1=ALU.add, accum_out=SS[0:w, r:r + 1]))
            dve.tensor_scalar(SS, SS, 1.0 / D, EPS, ALU.mult, ALU.add).then_inc(S_("sv_mean"), 1)
            dve.wait_ge(S_("sv_root"), 1)
            link(dve.reciprocal(SS, SS))
            for r in range(R):
                w = width(r)
                last = dve.scalar_tensor_tensor(SV[0:w, r, :], SV[0:w, r, :], SS[0:w, r:r + 1], SG[0:w, :],
                                                ALU.mult, ALU.mult)
            last.then_inc(S_("sv_normed"), 1)
            for q in range(2):
                filled(dve, 'w', q)
                dve.tensor_copy(WT[:, 4 * q:4 * q + 4, :], blocks(bank('w', q), 4)).then_inc(drains('w', q), 1)
            filled(dve, 'bd')
            dve.tensor_tensor(BD.rearrange("p g (b t) -> p g b t", b=8),
                              bank('bd')[0:TS, 0:64].rearrange("p (g t) -> p g t", g=8)[:, :, None, :]
                              .broadcast_to([TS, 8, 8, 8]),
                              const('bd', TS).rearrange("p (b t) -> p b t", b=8)[:, None, :, :]
                              .broadcast_to([TS, 8, 8, 8]), ALU.mult).then_inc(drains('bd'), 1)
            drained(dve, 'bd')
            dve.memset(ST[0:1, 111:112], 0.0).then_inc(S_("bd_ready"), 1)
            for g in range(8):
                filled(dve, 'sg', g)
                if g >= 2:
                    dve.wait_ge(S_("ob_ready"), g - 1)
                dve.tensor_tensor(blocks(TMPS[g % 2][:, 0:TP], 4), blocks(bank('sg', g), 4),
                                  SB[:, g, None, :].broadcast_to([P, 4, P]), ALU.add).then_inc(drains('sg', g), 1)
                filled(dve, 'sgs', g)
                dve.tensor_tensor(blocks(TMPS[g % 2][:, TP:T], 8), blocks(bank('sgs', g)[:, 0:TS], 8),
                                  SB[:, g, None, 0:8].broadcast_to([P, 8, 8]), ALU.add).then_inc(drains('sgs', g), 1)
            for i in range(4):
                for kind, gate in (('wb', SIGB), ('wa', SIGA)):
                    for c in (2 * i, 2 * i + 1):
                        filled(dve, kind, c)
                        drained(dve, 'gb' if kind == 'wb' else 'ga', c)
                        dst = halves(mT[:, c, :]) if kind == 'wb' else gate[c % 2]
                        dve.tensor_tensor(dst, gate[c % 2], ptile(kind, c), ALU.mult).then_inc(drains(kind, c), 1)

            def residual(kind):
                for c in range(8):
                    filled(dve, kind, c)
                    dve.tensor_tensor(halves(xT[:, c, :]), halves(xT[:, c, :]), ptile(kind, c), ALU.add)\
                        .then_inc(drains(kind, c), 1)
                drained(dve, kind, 7)

            residual('out')
            squares(1)
            normalise(1, 8)
            for q in range(2):
                filled(dve, 'state', q)
                n = 512 if q == 0 else 192
                dve.tensor_copy(STT_[:, 512 * q:512 * q + n], bank('state', q)[:, 0:n]).then_inc(drains('state', q), 1)
            for f in range(FB):
                for k in range(2):
                    fb = FB * k + f
                    hp, cb = HPb[f % 2][k], CB[f % 2][k]
                    dve.wait_ge(S_("tap2_done"), 2 * f + k + 1)
                    link(dve.scalar_tensor_tensor(cb, hp[:, 1:593], VT[:, 68 + fb:69 + fb], cb, ALU.mult, ALU.add))
                    dve.scalar_tensor_tensor(cb, hp[:, 0:592], VT[:, 24 + fb:25 + fb], cb, ALU.mult, ALU.add)\
                        .then_inc(S_("taps_done"), 1)
                dve.wait_ge(S_("silu_done"), f + 1)
                dve.wait_ge(S_("taps_done"), 2 * f + 2)
                a, (cg, cv) = act_block(f), CB[f % 2]
                dve.tensor_tensor(a[:, 0:TP], cg[:, 0:TP], cv[:, 0:TP], ALU.mult)
                dve.tensor_tensor(blocks(a[:, TP:T], 8), window(cg), window(cv), ALU.mult).then_inc(S_("act_ready"), 1)
            residual('dn')
            squares(2)
            normalise(2, 16)
            for q in range(2):
                filled(dve, 'ho', q)
                if q == 0:
                    dve.tensor_copy(CO[0:88, 0, :], bank('ho', 0)[0:88, 0:128])
                    dve.tensor_copy(CO[:, 1:4, :], blocks(bank('ho', 0)[:, 128:512], 3)).then_inc(drains('ho', 0), 1)
                else:
                    dve.tensor_copy(CO[:, 4:6, :], blocks(bank('ho', 1)[:, 0:256], 2))
                    dve.tensor_copy(CO[0:64, 6, :], bank('ho', 1)[0:64, 256:384]).then_inc(drains('ho', 1), 1)
            for r in range(R):
                filled(dve, 'y', r, 1)
                if r >= 2:
                    dve.wait_ge(S_(f"y_stored{r % 2}"), 16 * (r // 2))
                dve.tensor_copy(YO[r % 2][0:width(r), 512:1024], bank('y', r, 1)[0:width(r)])\
                    .then_inc(drains('y', r, 1), 1)


def window(c):
    return bass.AP(c.tensor, c.offset + 514, [c.ap[0], [10, 8], [1, 8]])


_INS = ['x_prompt', 'x_sample', 'cache_k', 'cache_v', 'cache_idx_k', 'state_ffn_conv', 'page_table', 'rel_bias',
        'norm_mix_g', 'w_in', 'sg_norm_g', 'sg_w_s', 'sg_b', 'w_branch_a', 'w_branch_b', 'w_out', 'norm_ffn_g',
        'w_up', 'ffn_conv_w', 'ffn_conv_b', 'w_down', 'norm_final_g']
_OUTS = [(1, TP, D), (NB_, NS, D), (1, 1, TP, H, HD), (1, 1, TP, H, HD), (1, 1, TP, IDX), (1, 1, 2, 2 * FF),
         (1, NB_, NS, H, HD), (1, NB_, NS, H, HD), (1, NB_, NS, IDX), (1, NB_, 2, 2 * FF), (1, NB_, NS, D)]


def kernel(**inputs):
    import concourse.bacc as _bacc
    from concourse.bass_utils import run_bass_kernel_spmd as _run

    nc = _bacc.Bacc("TRN2", target_bir_lowering=False, num_devices=1)
    arrays, args = {}, []
    for name in _INS:
        a = np.ascontiguousarray(inputs[name])
        arrays[f"in_{name}"] = a
        args.append(nc.dram_tensor(f"in_{name}", a.shape, mybir.dt.from_np(a.dtype), kind="ExternalInput").ap())
    c = shape_constants()
    arrays["in_consts"] = c
    args.append(nc.dram_tensor("in_consts", c.shape, F32, kind="ExternalInput").ap())
    for i, shape in enumerate(_OUTS):
        args.append(nc.dram_tensor(f"out_{i}", shape, F32, kind="ExternalOutput").ap())
    hybrid_kernel(nc, *args)
    r = _run(nc, [arrays], core_ids=[0])
    return tuple(r.results[0][f"out_{i}"] for i in range(len(_OUTS)))
```

```python
import math
from contextlib import ExitStack

import numpy as np
import concourse.bass as bass
from concourse import mybir

F32 = mybir.dt.float32
F32R = mybir.dt.float32r
I32 = mybir.dt.int32
ALU = mybir.AluOpType
ACT = mybir.ActivationFunctionType
AX_X = mybir.AxisListType.X

P = 128
D = 1024
KT = D // P
TP = 512
NB_, NS = 8, 8
TS = NB_ * NS
T = TP + TS
HALF = T // 2
R = 5
H, HD = 8, 128
IDX = 64
PAGE, NPAGES = 128, 16
PAST = PAGE * NPAGES
NKEY = PAST + NS
NPG = NPAGES + 1
NCOL = NPG * PAGE
FF = 2816
FB = FF // P
TOPK_P, TOPK_S = 128, 256
EPS = 1e-6
ATT_SCALE = HD ** -0.5
IDX_SCALE = IDX ** -0.5 * 8 ** -0.5
NEG = -float(2 ** 120)
MARK = -3.4028234663852886e38
ARENA = 16512
BIASW = 384
COL = dict(q=0, k=1024, v=2048, iq=3072, iw=3584, ik=3592, su=3656, sv=4680, ga=5704, gb=6728)
SP_OFF = [0, 128, 384, 768]
SP_COLS = 1280

_CONST = [('ident', 128), ('newcausal', 8), ('newblock', 64), ('caus', 128), ('bd', 64), ('rep', 64),
          ('swap', 128), ('dup', 128), ('selp', 512), ('selT', 256), ('hmask', 8), ('bucket', BIASW)]
KEPT = 6
COFF, _at = {}, 0
for _n, _w in _CONST:
    COFF[_n] = (_at, _w)
    _at += _w
NCONST = _at
NKEPT = sum(w for _, w in _CONST[:KEPT])


def shape_constants():
    c = np.zeros((P, NCONST), np.float32)

    def put(name, a):
        o, w = COFF[name]
        a = np.asarray(a, np.float32).reshape(a.shape[0], -1)
        c[:a.shape[0], o:o + w] = a

    eye = np.eye(P)
    put('ident', eye)
    put('swap', np.roll(eye, 64, axis=1))
    dup = np.zeros((72, P))
    for m in range(P):
        dup[m % 64, m] = 1
    put('dup', dup)
    selp = np.zeros((NB_, NS, 4, 2, H, NS))
    for b in range(NB_):
        for t in range(NS):
            selp[b, t, b // 2, b % 2, :, t] = 1
    put('selp', selp.reshape(TS, -1))
    put('selT', selp.transpose(3, 4, 5, 2, 0, 1).reshape(P, -1))
    hm = np.zeros((2, H, NS, H))
    for h in range(H):
        hm[:, h, :, h] = 1
    put('hmask', hm.reshape(P, H))
    t = np.arange(NS)
    put('newcausal', np.where(t[None, :] <= np.tile(t, NB_)[:, None], 0.0, NEG))
    b = np.repeat(np.arange(NB_), NS)
    put('newblock', np.where(b[:, None] == b[None, :], 0.0, NEG))
    put('bd', (b[:, None] == b[None, :]).astype(np.float32))
    i = np.arange(P)
    put('caus', np.where(i[None, :] <= i[:, None], 0.0, NEG))
    put('rep', (t[:, None] == np.tile(t, NB_)[None, :]).astype(np.float32))
    hot = np.zeros((32, BIASW))
    for x in range(BIASW):
        n = max(255 - x, 0)
        bk = n if n < 16 else min(16 + int(math.log(n / 16) / math.log(128 / 16) * 16), 31)
        hot[bk, x] = 1
    put('bucket', hot)
    return c


def hybrid_kernel(nc, x_prompt, x_sample, cache_k, cache_v, cache_idx_k, state_ffn_conv, page_table, rel_bias,
                  norm_mix_g, w_in, sg_norm_g, sg_w_s, sg_b, w_branch_a, w_branch_b, w_out, norm_ffn_g,
                  w_up, ffn_conv_w, ffn_conv_b, w_down, norm_final_g, consts,
                  y_prompt, y_sample, k_prompt, v_prompt, ik_prompt, conv_prompt,
                  k_sample, v_sample, ik_sample, conv_sample, sgv_sample):
    n_phys = cache_k.shape[1]
    bias_scr = nc.dram_tensor("bias_scratch", (P, H, BIASW), F32, kind="Internal").ap()
    mask_scr = nc.dram_tensor("mask_scratch", (TS, NCOL), F32, kind="Internal").ap()
    sv_scr = nc.dram_tensor("sv_scratch", (R, P, D), F32, kind="Internal").ap()
    side_scr = {k: nc.dram_tensor(f"{k}_scratch", (P, KT, T), F32, kind="Internal").ap() for k in ('ga', 'gb', 'su')}
    x_scr = [nc.dram_tensor(f"x_scratch{i}", (P, KT, T), F32, kind="Internal").ap() for i in range(2)]

    class Singles:
        def __init__(self, banks):
            self.banks, self.fills, self.slots = banks, 0, {}

        def add(self, *name):
            self.slots[name] = (self.fills, self.fills % self.banks, self.fills // self.banks)
            self.fills += 1

    class Pairs:
        def __init__(self):
            self.uses, self.at, self.slots = [0, 0], 0, {}

        def add(self, *name, at=None):
            at = self.at if at is None else at
            self.slots[name] = (at, self.uses[at])
            self.uses[at] += 1
            self.at = 1 - at

    single, pair = Singles(4), Pairs()
    side = ([('sv', c, r) for c in range(4) for r in range(R)] + [('ga', c) for c in range(8)]
            + [('gb', c) for c in range(8)] + [('su', c) for c in range(8)])
    SIDE_B = [(1, 1), (1, 1), (1, 1), (1, 1), (1, 2), (1, 2), (1, 2), (1, 2)]
    SIDE_V = [{7: 1, 16: 1}, {7: 1, 16: 1}, {7: 1, 16: 1}, {4: 1, 11: 1, 16: 1}]
    side_at, todo = {}, list(side)

    def put_side(place, n):
        side_at[place] = [todo.pop(0) for _ in range(n)]

    for h in range(H):
        for i in range(2):
            put_side(('B', h, i), SIDE_B[h][i])
    for G in range(2):
        for i, n in enumerate((2, 1)):
            put_side(('softmax', G, i), n)
        for b in range(4):
            for kp, n in SIDE_V[b].items():
                put_side(('V', G, b, kp), n)
    assert not todo
    for r in range(R):
        for q in range(2):
            single.add('x', r, q)
    single.add('vec')
    for h in range(H):
        single.add('bias', h)
    pair.add('rms', 0)
    for m in range(4):
        pair.add('iq', m)
    pair.add('ikw')
    for n in ('iqsw', 'ikd0', 'ikd1', 'ikwT', 'iwrep'):
        single.add(n)
    for r in range(1, 4):
        for h in range(H):
            single.add('ps', r, h)
    for s in range(18):
        if s < 16:
            single.add('t', s)
        if 1 <= s < 17:
            single.add('s1', s - 1)
        if s >= 2 and s % 4 == 2:
            pair.add('ss', s // 4, at=0)
        if s % 2 == 1 and s < 16:
            pair.add('q', s // 2, at=1)
    single.add('s1n')
    pair.add('ssn', at=0)
    for c in range(8):
        pair.add('k', c)
    for r in range(R):
        for q in range(2):
            single.add('kt', r, q)
    for c in range(4):
        for r in range(R):
            pair.add('v', c, r)
    for h in range(H + 1):
        if h < H:
            for r in range(4):
                single.add('pl', h, r)
            for tile in side_at['B', h, 0]:
                pair.add(*tile)
        if h:
            single.add('pv', h - 1)
        if h < H:
            for tile in side_at['B', h, 1]:
                pair.add(*tile)
            for r in range(4):
                single.add('pt', h, r)
    for G in range(2):
        for n in range(64):
            single.add('kp', G, n, 0)
            single.add('kp', G, n, 1)
        for kp in range(NPG):
            pair.add('kl', G, kp, at=kp % 2)
        for i, tile in enumerate(side_at['softmax', G, 0] + side_at['softmax', G, 1]):
            pair.add(*tile, at=(i + 1) % 2)
        for g in range(2):
            for q in range(5):
                single.add('st', G, g, q)
        for b in range(4):
            pair.add('o', G, b, at=0)
            for kp in range(NPG):
                for tile in side_at.get(('V', G, b, kp), ()):
                    pair.add(*tile, at=1)
            single.add('ot', G, b, 0)
            single.add('ot', G, b, 1)
    for c in range(8):
        pair.add('wa', c)
    single.add('w', 0)
    single.add('w', 1)
    single.add('bd')
    for g in range(8):
        single.add('sg', g)
        single.add('sgs', g)
    for kind in ('wb', 'out'):
        for c in range(8):
            pair.add(kind, c)
    pair.add('rms', 1)
    single.add('state', 0)
    single.add('state', 1)
    for f in range(FB):
        pair.add('up', f, 0)
        pair.add('up', f, 1)
    for c in range(8):
        pair.add('dn', c)
    single.add('ho', 0)
    single.add('ho', 1)
    pair.add('rms', 2)
    for r in range(R):
        for q in range(2):
            single.add('y', r, q)

    NW, NH = 3, 2
    chunks, slot_value, chunk_list = {}, [0] * NW, []

    def add_chunk(name, loads, last_tile):
        n = len(chunk_list)
        slot_value[n % NW] += 16 * loads
        chunks[name] = (n, slot_value[n % NW])
        chunk_list.append((name, last_tile))

    for i in range(2):
        add_chunk(('iq', i), 1, ('iq', 2 * i + 1))
    add_chunk(('ikw',), 2, ('ikw',))
    for k in 'qk':
        for i in range(4):
            add_chunk((k, i), 1, (k, 2 * i + 1))
    for k in ('v', 'sv'):
        for i in range(4):
            add_chunk((k, i), 1, (k, i, R - 1))
    for k in ('ga', 'gb', 'su', 'wa', 'wb', 'out'):
        for i in range(4):
            add_chunk((k, i), 1, (k, 2 * i + 1))
    for f in range(FB):
        add_chunk(('up', f), 2, ('up', f, 1))
    for c in range(8):
        for kh in range(2):
            add_chunk(('dn', c, kh), 1, ('dn', c))

    ctx = ExitStack()
    with ctx:
        def at(name, off, words, dt=F32, rows=P):
            return nc.alloc_sbuf_tensor_at(name, [rows, words], dt, offset=ARENA + 4 * off)

        def blocks(a, n):
            return a.rearrange("p (n c) -> p n c", n=n)

        BLK = KT * T
        o_st, o_vt, o_ones, o_ptab, o_cst = 0, 120, 320, 448, 576
        o_tmp = o_cst + NKEPT
        o_nbr = o_cst + NCONST
        o_w = o_nbr + 272
        o_wh = o_w + 2048 * NW
        o_xh = o_wh + 2048 * NH
        o_xl = o_xh + BLK
        o_x = o_xl + BLK
        o_r1 = o_x + BLK
        o_r2 = o_r1 + 9728
        o_sr = o_r2 + 4608
        o_r3 = o_sr + NCOL
        o_rb = o_r3 + 7424
        o_ikw = o_rb + 2048
        assert ARENA + 4 * (o_ikw + 400) <= 229368
        ST = at("ST", o_st, 120)
        VT = at("VT", o_vt, 200)
        ones = at("ones", o_ones, P)
        PTAB = at("PTAB", o_ptab, NB_ * NPAGES, I32, 1)
        CST = at("CST", o_cst, NCONST)
        NBr = blocks(at("NBr", o_nbr, 272)[:, :], 2)
        W = [at(f"W{i}", o_w + 2048 * i, 2048) for i in range(NW)]
        WL = [at(f"WL{i}", o_w + 2048 * i, 2048, F32R) for i in range(NW)]
        WH = [at(f"WH{i}", o_wh + 2048 * i, 2048, F32R) for i in range(NH)]
        R1 = at("R1", o_r1, 9728)
        R2 = at("R2", o_r2, 4608)
        SR = at("SR", o_sr, NCOL)
        R3 = at("R3", o_r3, 7424)
        RB = at("RB", o_rb, 2048)
        IKWT = blocks(at("IKWT", o_ikw, 360)[:, :], 5)
        IWS = blocks(at("IWS", o_ikw + 360, 40)[:, :], 5)

        class Act:
            def __init__(self, name, hi, lo, n=KT):
                self.whole = blocks(at(name, lo, n * T)[:, :], n)
                self.hi = blocks(at(name + "_hi", hi, n * T, F32R)[:, :], n)
                self.lo = blocks(at(name + "_lo", lo, n * T, F32R)[:, :], n)

            def hi_block(self, k):
                return self.hi[:, k, :]

            def lo_block(self, k):
                return self.lo[:, k, :]

            def whole_block(self, k):
                return self.whole[:, k, :]

        xn1 = Act("xn1", o_xh, o_xl)
        xn2 = Act("xn2", o_xl, o_x)
        oa = Act("oa", o_r1, o_x)
        ob = Act("ob", o_r1, o_r2)
        mg = Act("mg", o_r2, o_r3 + 4608)
        GAT = blocks(at("GAT", o_xl, BLK)[:, :], KT)
        GBT = blocks(at("GBT", o_xh, BLK)[:, :], KT)
        xT0 = blocks(at("xT0", o_x, BLK)[:, :], KT)
        xT1 = blocks(at("xT1", o_xh, BLK)[:, :], KT)
        xT2 = blocks(at("xT2", o_xl, BLK)[:, :], KT)
        SQ = [blocks(at(f"SQ{i}", o, BLK)[:, :], KT) for i, o in enumerate((o_xh, o_r1, o_x))]
        YN = SQ[2]
        xT = [xT0, xT1, xT2]
        oaT, obT, mT = oa.whole, ob.whole, mg.whole
        NG = 18
        GA = [[at(f"G{i}{s}", o, 2 * T * n, d) for i, (o, n) in enumerate(((o_r1, NG), (o_xh, FB - NG)))]
              for s, d in (("", F32), ("_hilo", F32R))]
        o_conv = o_r1 + 2 * T * NG
        CV = at("CV", o_conv, 4752)
        RSF = at("RSF", o_conv + 4752, T)
        STH = at("STH", o_tmp, 1496)
        STG = at("STG", o_tmp, 2 * T)
        stage = [STG[:, T * i:T * i + T] for i in range(2)]

        def gated(f, part):
            g, i = (0, f) if f < NG else (1, f - NG)
            return GA[1][g][:, 2 * T * i + T * part:2 * T * i + T * part + T]

        def gated_whole(f):
            g, i = (0, f) if f < NG else (1, f - NG)
            return GA[0][g][:, 2 * T * i + T:2 * T * i + 2 * T]

        def const(name, rows=P):
            o, w = COFF[name]
            return CST[0:rows, o:o + w]

        ident = const('ident')

        XL = blocks(R1[:, 0:5120], 5)
        BV = blocks(R1[:, 5120:8192], H)
        RBB = blocks(R1[0:32, 8192:9216], H)
        VR = blocks(R1[:, 9216:9472], 2)
        RBT = R1[0:32, 9472:9480]
        iqT = blocks(R2[:, 0:2304], 4)
        IKW = R2[:, 2304:2880]
        IKPAD = blocks(R2[:, 2880:3904], 2)
        MS = R3[:, 0:SP_COLS]
        IQB = blocks(R3[:, 1280:1792], 4)
        IQSW = blocks(R3[:, 1792:2048], 4)
        IKN = [R3[:, 2048 + 512 * i:2560 + 512 * i].rearrange("p (j a d) -> p j a d", j=4, a=2) for i in range(4)]
        IKT = [R3[:, 4096 + 512 * i:4608 + 512 * i] for i in range(2)]
        RL = [R3[:, 5120 + 512 * i:5632 + 512 * i] for i in range(2)]
        RL2 = [R3[:, 6144 + 512 * i:6656 + 512 * i] for i in range(2)]
        SWM = blocks(R3[:, 7168:7424], 4)
        IKNEW = blocks(ST[:, 0:32], 4)
        RLN = ST[:, 32:64]
        TMP32 = blocks(ST[:, 64:96], 4)
        IWC = ST[:, 96:100]
        MAX8 = ST[0:TS, 0:8]
        MAX8P = ST[:, 100:108]
        M8 = ST[0:TS, 16:24]
        RS = [SR[:, 0:T], RSF[:, :], RSF[:, :]]
        S = SR[0:TS, :]
        BT = blocks(RB[:, 0:2048], H)
        qT = blocks(R2[:, :], H)
        V = blocks(R1[:, 0:4096], 4)
        kT = blocks(R1[:, 4096:8704], H)
        Vn = R1[:, 8704:9728]
        MB = [R3[:, 1280 + 1280 * i:2560 + 1280 * i] for i in range(2)]
        L = R3[:, 3840:5120]
        PT = blocks(R3[:, 5120:7168], 4)
        KO = [R3[:, 5120 + 1024 * i:6144 + 1024 * i] for i in range(2)]
        ring = [R1[:, 1024 * i:1024 * i + 1024] for i in range(8)]
        LS = blocks(R2[:, 0:2 * NCOL], 2)
        OS = [blocks(R2[:, 256 * i:256 * i + 256], 2) for i in range(2)]
        MG = SR
        QN = blocks(R1[:, 8192:8704], H)
        NBd = [R2[:, 4352:4608], at("NBd1", o_ikw, 256)[:, :]]
        PTs = R3[:, 0:2 * NCOL].rearrange("p (g k c) -> p g k c", g=2, k=NPG)
        QZ = R3[:, 4352:6400].rearrange("p (h b c) -> p h b c", h=H, b=8)
        kTn = blocks(R3[:, 6400:7424], H)
        KTb = [blocks(RB[:, 1024 * i:1024 * i + 1024], H) for i in range(2)]
        SV = blocks(R1[:, 4608:9728], 5)
        SG = R3[:, 0:1024]
        SB = blocks(R3[:, 1024:2048], 8)
        WS = blocks(R3[:, 2048:3072], 8)
        WT = blocks(R3[:, 3072:4096], 8)
        BD = blocks(R3[0:TS, 4096:4608], 8)
        TMPS = [SR[:, 576 * i:576 * i + 576] for i in range(2)]
        JUNK = SR[:, 1152:2176]
        HPb = [[CV[:, 594 * (2 * i + k):594 * (2 * i + k) + 594] for k in range(2)] for i in range(2)]
        CB = [[CV[:, 2376 + 592 * (2 * i + k):2968 + 592 * (2 * i + k)] for k in range(2)] for i in range(2)]
        SRAW = blocks(R1[:, 5760:6528], 6)
        STT_ = STH[:, 0:704]
        HCP = STH[:, 704:792]
        HCS = STH[:, 792:1496]
        CO = blocks(RB[:, 0:896], 7)
        YO = [R1[:, 1024 * i:1024 * i + 1024] for i in range(2)]
        MX = [ST[:, 24 + 16 * i:28 + 16 * i] for i in range(2)]
        NM = [ST[:, 28 + 16 * i:32 + 16 * i] for i in range(2)]
        SU = [ST[:, 32 + 16 * i:36 + 16 * i] for i in range(2)]
        RC = [ST[:, 36 + 16 * i:40 + 16 * i] for i in range(2)]
        SS = ST[:, 60:65]

        PS = ctx.enter_context(nc.psum_tensor("PS", [P, 8, 512], F32))

        sems = {}

        def S_(name):
            if name not in sems:
                sems[name] = ctx.enter_context(nc.semaphore(name))
            return sems[name]

        single_filled = S_("single_filled")
        pair_filled = [S_(f"pair_filled{i}") for i in range(2)]
        single_drained = [S_(f"single_drained{i}") for i in range(4)]
        pair_drained = [S_(f"pair_drained{i}") for i in range(2)]
        weights_in = [S_(f"weights_in{i}") for i in range(NW)]
        idx_in = [S_(f"idx_pages_in{i}") for i in range(4)]
        page_in = [S_(f"page_in{i}") for i in range(8)]
        block = ctx.enter_context(nc.Block())

        def bank(*n):
            return PS[:, 4 + single.slots[n][1], :]

        def pbank(*n):
            return PS[:, 2 * pair.slots[n][0]:2 * pair.slots[n][0] + 2, :]

        def ptile(*n):
            return pbank(*n)[:, :, 0:HALF]

        def halves(a):
            return a.rearrange("p (a t) -> p a t", a=2)

        def filled(e, *n):
            if n in single.slots:
                e.wait_ge(single_filled, single.slots[n][0] + 1)
            else:
                at, use = pair.slots[n]
                e.wait_ge(pair_filled[at], use + 1)

        def drained(e, *n):
            if n in single.slots:
                e.wait_ge(single_drained[single.slots[n][1]], single.slots[n][2] + 1)
            else:
                at, use = pair.slots[n]
                e.wait_ge(pair_drained[at], use + 1)

        def claim(e, *n):
            if n in single.slots:
                _, k, use = single.slots[n]
                if use:
                    e.wait_ge(single_drained[k], use)
            else:
                k, use = pair.slots[n]
                if use:
                    e.wait_ge(pair_drained[k], use)

        def drains(*n):
            return single_drained[single.slots[n][1]] if n in single.slots else pair_drained[pair.slots[n][0]]

        def width(r):
            return P if r < 4 else TS

        def chunk_used(e, n):
            name, last_tile = chunk_list[n]
            if name[0] == 'dn' and name[2] == 0:
                e.wait_ge(S_("down_halves"), name[1] + 1)
            else:
                filled(e, *last_tile)

        def page_freed(e, seq):
            if seq < 8:
                if seq == 0:
                    e.wait_ge(S_("ring_free"), 1)
                return
            G, kind, n = (seq - 8) // 128, (seq - 8) // 64 % 2, (seq - 8) % 64
            if kind == 0:
                e.wait_ge(single_filled, single.slots['kp', G, n, 1][0] + 1)
            else:
                e.wait_ge(S_("v_pages_used"), 64 * G + n + 1)

        def next_chunk(tile):
            n = chunk_of(tile)
            return chunk_list[n + NW][0] if chunk_list[n][1] == tile else None

        def chunk_of(tile):
            return chunks[(tile[0], tile[1])][0] if tile[0] == 'sv' else chunks[(tile[0], tile[1] // 2)][0]

        def chunk_words(name):
            return {'ikw': 72 * KT, 'dn': 11 * P}.get(name[0], 256 * KT)

        def split_after(split):
            first, seen = {}, set()
            for n, (name, tile) in enumerate(chunk_list):
                kind = name[0]
                if kind == 'dn':
                    t = ('dn', name[1])
                elif kind in ('v', 'sv'):
                    t = (kind, name[1], 0)
                elif kind == 'up':
                    t = (kind, name[1], 0)
                elif kind == 'ikw':
                    t = name
                else:
                    t = (kind, 2 * name[1])
                first.setdefault(t, []).append(n)

            def after(*tile):
                for n in first.get(tile, ()):
                    if n + 1 < len(chunk_list):
                        split(*chunk_list[n + 1][0])
            return after

        @block.sync
        def _(sp):
            w_in_v = w_in[0].rearrange("(k p) n -> p k n", p=P)

            def load_chunk(name):
                n = chunks[name][0]
                slot = n % NW
                if n >= NW:
                    chunk_used(sp, n - NW)
                kind, i = name[0], (name[1] if len(name) > 1 else 0)
                dst = blocks(W[slot][:, :], KT)
                if kind in ('iq', 'q', 'k', 'v', 'sv', 'su', 'gb', 'ga'):
                    c = COL[kind] + 256 * i
                    sp.dma_start(dst, w_in_v[:, :, c:c + 256]).then_inc(weights_in[slot], 16)
                elif kind == 'ikw':
                    d = W[slot][:, 0:576].rearrange("p (k c) -> p k c", k=KT)
                    sp.dma_start(d[:, :, 0:64], w_in_v[:, :, COL['ik']:COL['ik'] + 64]).then_inc(weights_in[slot], 16)
                    sp.dma_start(d[:, :, 64:72], w_in_v[:, :, COL['iw']:COL['iw'] + 8]).then_inc(weights_in[slot], 16)
                elif kind in ('wb', 'wa', 'out'):
                    m = {'wb': w_branch_b, 'wa': w_branch_a, 'out': w_out}[kind]
                    sp.dma_start(dst, m[0].rearrange("(k p) n -> p k n", p=P)[:, :, 256 * i:256 * i + 256])\
                        .then_inc(weights_in[slot], 16)
                elif kind == 'up':
                    u = w_up[0].rearrange("(k p) n -> p k n", p=P)
                    for a in range(2):
                        sp.dma_start(dst[:, :, 128 * a:128 * a + 128], u[:, :, FF * a + P * i:FF * a + P * i + P])\
                            .then_inc(weights_in[slot], 16)
                else:
                    c, kh = name[1:]
                    u = w_down[0].rearrange("(k p) n -> p k n", p=P)
                    sp.dma_start(blocks(W[slot][:, 0:1408], 11), u[:, 11 * kh:11 * kh + 11, P * c:P * c + P])\
                        .then_inc(weights_in[slot], 16)

            sp.dma_start(CST[:, :], consts).then_inc(S_("consts_in"), 16)
            sp.dma_start(XL[:, 0:4, :], x_prompt[0].rearrange("(r p) d -> p r d", p=P)).then_inc(S_("x_in"), 16)
            sp.dma_start(XL[0:TS, 4, :], x_sample.rearrange("b s d -> (b s) d")).then_inc(S_("x_in"), 16)
            for name in (('iq', 0), ('iq', 1), ('ikw',)):
                load_chunk(name)
            for i, g in enumerate((norm_mix_g[0], norm_ffn_g[0], norm_final_g)):
                sp.dma_start(VR[8 * i:8 * i + 8, 0, :], g.rearrange("(k c) -> k c", k=8)).then_inc(S_("vec_in"), 16)
            cw = ffn_conv_w[0].rearrange("j (f c) -> (j f) c", c=P)
            sp.dma_start(VR[24:128, 0, :], cw[0:104, :]).then_inc(S_("vec_in"), 16)
            sp.dma_start(VR[0:28, 1, :], cw[104:132, :]).then_inc(S_("vec_in"), 16)
            sp.dma_start(VR[28:72, 1, :], ffn_conv_b[0].rearrange("(f c) -> f c", c=P)).then_inc(S_("vec_in"), 16)
            sp.dma_start(RBT, rel_bias).then_inc(S_("rb_in"), 16)
            sp.dma_start(PTAB[:, :], page_table.rearrange("(o b) n -> o (b n)", o=1)).then_inc(S_("table_in"), 16)
            for r in range(R):
                for q in range(2):
                    drained(sp, 'x', r, q)
            sp.dma_start(x_scr[0], xT0).then_inc(S_("x_out"), 16)
            sp.wait_ge(S_("table_in"), 16)

            def page_id(b, kp):
                return sp.value_load(PTAB[0:1, b * NPAGES + kp:b * NPAGES + kp + 1], min_val=0, max_val=n_phys - 1)

            for s in range(16):
                kc, p = s // 4, s % 4
                if s >= 4:
                    for name in {4: [('q', 0), ('q', 1), ('q', 2)], 8: [('q', 3)], 12: [('k', 0)]}.get(s, ()):
                        load_chunk(name)
                    filled(sp, 't', s - 4)
                for a in range(2):
                    for j in range(4):
                        v = page_id(2 * p + a, 4 * kc + j)
                        sp.dma_start(IKN[s % 4][:, j, a, :],
                                     cache_idx_k[0, bass.ds(v, 1), :, :].rearrange("o p d -> (o p) d"))\
                            .then_inc(idx_in[s % 4], 16)
            for k in ('k', 'v', 'sv'):
                for i in range(4):
                    if (k, i) != ('k', 0) and (k, i) != ('sv', 3):
                        load_chunk((k, i))

            def side_loads(*place):
                for tile in side_at.get(place, ()):
                    name = next_chunk(tile)
                    if name:
                        load_chunk(name)

            for h in range(H):
                for i in range(2):
                    side_loads('B', h, i)

            def load_page(seq):
                if seq >= 256:
                    return
                G, kind, n = seq // 128, seq // 64 % 2, seq % 64
                b, kp = (4 * G + n % 4, n // 4) if kind == 0 else (4 * G + n // 16, n % 16)
                page_freed(sp, seq)
                v = page_id(b, kp)
                sp.dma_start(ring[seq % 8], (cache_k, cache_v)[kind][0, bass.ds(v, 1)]
                             .rearrange("o p h d -> (o p) (h d)")).then_inc(page_in[seq % 8], 16)

            for seq in range(8):
                load_page(seq)
            for G in range(2):
                for n in range(64):
                    load_page(128 * G + n + 8)
                side_loads('softmax', G, 0)
                side_loads('softmax', G, 1)
                for b in range(4):
                    for kp in range(NPG):
                        if kp < NPAGES:
                            load_page(128 * G + 64 + 16 * b + kp + 8)
                        side_loads('V', G, b, kp)

            filled(sp, *side[-1])
            for i in range(2):
                sp.wait_ge(S_(f"side_stored{i}"), 16 * len(side) // 2)
            sp.dma_start(GAT, side_scr['ga']).then_inc(S_("ga_back"), 16)
            sp.dma_start(GBT, side_scr['gb']).then_inc(S_("gb_back"), 16)
            filled(sp, 'ot', 1, 3, 1)
            sp.dma_start(SV[:, 0:4, :], sv_scr[0:4].rearrange("r p c -> p r c")).then_inc(S_("sv_back"), 16)
            sp.dma_start(SV[0:TS, 4, :], sv_scr[4, 0:TS, :]).then_inc(S_("sv_back"), 16)
            sp.dma_start(SG, bass.AP(sg_norm_g.tensor, 0, [[0, P], [1, 1024]])).then_inc(S_("sg_in"), 16)
            sp.dma_start(SB, bass.AP(sg_b.tensor, 0, [[0, P], [1, 1024]]).rearrange("p (g t) -> p g t", g=8))\
                .then_inc(S_("sg_in"), 16)
            sp.dma_start(WS, sg_w_s[0].rearrange("g t s -> t g s")).then_inc(S_("ws_in"), 16)
            sp.dma_start(obT, side_scr['su']).then_inc(S_("su_back"), 16)
            load_chunk(('wa', 3))
            for i in range(4):
                load_chunk(('wb', i))
            load_chunk(('out', 0))
            load_chunk(('out', 1))
            for c in (6, 7):
                drained(sp, 'wb', c)
            sp.dma_start(xT1, x_scr[0]).then_inc(S_("x_back"), 16)
            for i in (2, 3):
                load_chunk(('out', i))
            filled(sp, 'wb', 7)
            raw = state_ffn_conv[0].rearrange("b w (f c) -> (b w f) c", c=P)
            sp.dma_start(SRAW[:, 0:5, :], raw[0:640, :].rearrange("(r p) c -> p r c", p=P)).then_inc(S_("state_in"), 16)
            sp.dma_start(SRAW[0:64, 5, :], raw[640:704, :]).then_inc(S_("state_in"), 16)
            for f in range(FB):
                load_chunk(('up', f))
                if f == 2:
                    drained(sp, 'out', 7)
                    drained(sp, 'out', 6)
                    sp.dma_start(x_scr[1], xT1).then_inc(S_("x_out"), 16)
            filled(sp, 'up', FB - 1, 1)
            sp.dma_start(xT2, x_scr[1]).then_inc(S_("x_back"), 16)
            for c in range(8):
                for kh in range(2):
                    load_chunk(('dn', c, kh))
            sp.wait_ge(S_("conv_rows"), 1)
            filled(sp, 'ho', 1)
            drained(sp, 'ho', 1)
            sp.dma_start(conv_prompt[0].rearrange("o w (f c) -> (o w f) c", c=P), CO[0:88, 0, :])\
                .then_inc(S_("stored_sp"), 16)
            cs = conv_sample[0].rearrange("b w (f c) -> (b w f) c", c=P)
            sp.dma_start(cs[0:640, :].rearrange("(r p) c -> p r c", p=P), CO[:, 1:6, :]).then_inc(S_("stored_sp"), 16)
            sp.dma_start(cs[640:704, :], CO[0:64, 6, :]).then_inc(S_("stored_sp"), 16)
            for r in range(R):
                drained(sp, 'y', r, 0)
                drained(sp, 'y', r, 1)
                dst = y_prompt[0, P * r:P * r + P, :] if r < 4 else y_sample.rearrange("b s d -> (b s) d")
                sp.dma_start(dst, YO[r % 2][0:width(r), :]).then_inc(S_(f"y_stored{r % 2}"), 16)
            sp.wait_ge(S_("stored_sp"), 48)
            sp.wait_ge(S_("y_stored0"), 48)
            sp.wait_ge(S_("y_stored1"), 32)

        @block.gpsimd
        def _(pool):
            steps = [0]

            def link(ins):
                steps[0] += 1
                ins.then_inc(S_("pool_step"), 1)
                pool.wait_ge(S_("pool_step"), steps[0])

            link(pool.memset(IKPAD[64:128, 0, :], 0.0))
            link(pool.memset(IKPAD[0:64, 1, :], 0.0))
            link(pool.memset(IQB[:, :, :], 0.0))
            pool.memset(ones[:, :], 1.0).then_inc(S_("ones_set"), 1)
            pool.wait_ge(S_("ones_set"), 1)
            pool.wait_ge(S_("rb_in"), 16)
            pool.tensor_copy(RBB, RBT[:, :, None].broadcast_to([32, H, P])).then_inc(S_("rbb_set"), 1)
            pool.wait_ge(S_("rbb_set"), 1)
            drained(pool, 'bias', H - 1)
            link(pool.memset(Vn[64:128, :], 0.0))
            pool.dma_start(bias_scr, BV).then_inc(S_("bias_out"), 16)
            pool.wait_ge(S_("bias_out"), 16)
            pool.dma_start(BT, bass.AP(bias_scr.tensor, 127, [[H * BIASW - 1, P], [BIASW, H], [1, 256]]))\
                .then_inc(S_("bt_in"), 16)
            for g in range(2):
                for j in range(4):
                    for b in range(4):
                        pool.dma_start(NBr[32 * j + 8 * b:32 * j + 8 * b + 8, g, :],
                                       bass.AP(bias_scr.tensor, 127 + (4 * g + j) * BIASW,
                                               [[H * BIASW - 1, 8], [1, 136]])).then_inc(S_("nbr_in"), 16)
            drained(pool, 'ikw')
            drained(pool, 'iqsw')
            for a in range(2):
                rows = slice(64 * a, 64 * a + 64)
                d = IQB[rows, :, 64 * a:64 * a + 64].rearrange("p q (m e t) -> p q m e t", m=4, e=2)
                o = iqT[rows, :, TP:T].rearrange("p m (q u t) -> p q m u t", q=4, u=2)[:, :, :, a, :]
                w = IQSW[rows, :, :].rearrange("p m (q u t) -> p q m u t", q=4, u=2)[:, :, :, a, :]
                link(pool.tensor_copy(d[:, :, :, a, :], o))
                link(pool.tensor_copy(d[:, :, :, 1 - a, :], w))
            pool.memset(ST[:, 110:111], 0.0).then_inc(S_("iqb_ready"), 1)
            pool.wait_ge(S_("iw_ready"), 1)
            pool.dma_start(ik_prompt[0, 0].rearrange("(r p) d -> p r d", p=P), IKWT[:, 0:4, 0:64])\
                .then_inc(S_("stored_pool"), 16)
            pool.dma_start(ik_sample[0].rearrange("b s d -> (b s) d"), IKWT[0:TS, 4, 0:64])\
                .then_inc(S_("stored_pool"), 16)
            for r in range(R):
                drained(pool, 'kt', r, 1)
                drained(pool, 'kt', r, 0)
                dst = (k_prompt[0, 0, P * r:P * r + P].rearrange("p h d -> p (h d)") if r < 4
                       else k_sample[0].rearrange("b s h d -> (b s) (h d)"))
                pool.dma_start(dst, KO[r % 2][0:width(r), :]).then_inc(S_(f"k_stored{r % 2}"), 16)
            drained(pool, 'v', 3, 4)
            pool.dma_start(v_prompt[0, 0].rearrange("(r p) h d -> p r (h d)", p=P), V).then_inc(S_("v_stored"), 16)
            pool.dma_start(v_sample[0].rearrange("b s h d -> (b s) (h d)"), Vn[0:TS, :]).then_inc(S_("v_stored"), 16)
            pool.wait_ge(S_("prompt_mask"), 3)
            pool.wait_ge(S_("bt_in"), 16)
            for h in range(H):
                if h >= 2:
                    drained(pool, 'pl', h - 2, 3)
                m = MB[h % 2]
                pool.tensor_tensor(m[:, 0:128], MS[:, 0:128], BT[:, h, 128:256], ALU.add)
                for r in range(1, 4):
                    o = SP_OFF[r] + P * (r - 1)
                    if r > 1:
                        pool.tensor_scalar(m[:, SP_OFF[r]:o], MS[:, SP_OFF[r]:o], BT[:, h, 0:1], None, ALU.add)
                    last = pool.tensor_tensor(m[:, o:o + 256], MS[:, o:o + 256], BT[:, h, :], ALU.add)
                last.then_inc(S_("bias_mask_ready"), 1)

            filled(pool, 'pv', H - 1)
            drained(pool, 'pv', H - 1)
            link(pool.memset(QZ, 0.0))
            link(pool.memset(kTn, 0.0))
            for G in range(2):
                for c in range(4):
                    b = 4 * G + c
                    pool.tensor_copy(QZ[:, :, b, 8 * c:8 * c + 8], qT[:, :, TP + 8 * b:TP + 8 * b + 8])
            link(pool.tensor_copy(kTn[:, :, 0:TS], kT[:, :, TP:T]))
            link(pool.tensor_copy(QN, qT[:, :, TP:T]))
            pool.wait_ge(S_("v_stored"), 32)
            pool.wait_ge(S_("k_stored0"), 48)
            pool.wait_ge(S_("k_stored1"), 32)
            pool.wait_ge(S_("nbr_in"), 16 * 32)
            pool.wait_ge(S_("stored_pool"), 32)
            for g in range(2):
                pool.tensor_scalar(NBd[g][:, 0:128], NBr[:, g, 0:128], NBr[:, g, 0:1], None, ALU.subtract)
                pool.tensor_scalar(NBd[g][:, 128:192].rearrange("p (b t) -> p b t", b=8),
                                   NBr[:, g, None, 128:136].broadcast_to([P, 8, 8]), NBr[:, g, 0:1], None,
                                   ALU.subtract)
                link(pool.memset(NBd[g][:, 192:256], 0.0))
            pool.memset(ST[0:1, 110:111], 0.0).then_inc(S_("ring_free"), 1)
            pool.wait_ge(S_("sample_mask"), 1)
            pool.dma_start(mask_scr, S).then_inc(S_("mask_out"), 16)
            pool.wait_ge(S_("mask_out"), 16)
            for G in range(2):
                if G:
                    drained(pool, 'kl', 0, NPG - 1)
                for j in range(4):
                    pool.dma_start(MG[32 * j:32 * j + 32, :], mask_scr[32 * G:32 * G + 32, :]).then_inc(S_("mg_in"), 16)

            pool.wait_ge(S_("ws_in"), 16)
            pool.affine_select(out=WS, in_=WS, pattern=[[0, 8], [-1, P]], compare_op=ALU.is_ge, fill=0.0,
                               base=0, channel_multiplier=1).then_inc(S_("ws_causal"), 1)
            pool.wait_ge(S_("sv_normed"), 1)
            pool.dma_start(sgv_sample[0].rearrange("b s d -> (b s) d"), SV[0:TS, 4, :]).then_inc(S_("stored_pool"), 16)
            pool.wait_ge(S_("su_back"), 16)
            for g in range(8):
                drained(pool, 'sgs', g)
                pool.tensor_tensor(obT[:, g, :], obT[:, g, :], TMPS[g % 2], ALU.mult).then_inc(S_("ob_whole"), 1)
            for c in range(8):
                drained(pool, 'wb', c)
                pool.tensor_tensor(mT[:, c, :], mT[:, c, :], TMPS[c % 2], ALU.add)\
                    .then_inc(S_("merged"), 1)
            filled(pool, 'rms', 1)
            pool.wait_ge(S_("stored_pool"), 48)
            for i in range(2):
                for k in range(2):
                    link(pool.memset(HPb[i][k][:, 0:2], 0.0))
            drained(pool, 'state', 1)
            for f in range(FB):
                for k in range(2):
                    fb = FB * k + f
                    hp = HPb[f % 2][k]
                    smp = hp[:, 514:594].rearrange("p (b c) -> p b c", b=8)
                    if f >= 2:
                        pool.wait_ge(S_("act_whole"), f - 1)
                    pool.tensor_copy(smp[:, :, 0:2],
                                     STT_.rearrange("p (b w f) -> p b w f", b=8, w=2)[:, :, :, fb])\
                        .then_inc(S_("state_put"), 1)
                for k in range(2):
                    fb = FB * k + f
                    hp = HPb[f % 2][k]
                    smp = hp[:, 514:594].rearrange("p (b c) -> p b c", b=8)
                    drained(pool, 'up', f, k)
                    pool.tensor_copy(HCP.rearrange("p (w f) -> p w f", w=2)[:, :, fb], hp[:, 512:514])
                    last = pool.tensor_copy(HCS.rearrange("p (b w f) -> p b w f", b=8, w=2)[:, :, :, fb],
                                            smp[:, :, 8:10])
                last.then_inc(S_("conv_rows"), 1)

        @block.tensor
        def _(pe):
            def done(ins, *n):
                ins.then_inc(single_filled if n in single.slots else pair_filled[pair.slots[n][0]], 1)

            def split(name, width, nk=KT):
                n = chunks[name][0]
                pe.wait_ge(S_("low_ready"), n + 1)
                return (blocks(WH[n % NH][:, 0:nk * width], nk), blocks(WL[n % NW][:, 0:nk * width], nk))

            def project(name, lhs, rhs, nk, first_wait=None):
                claim(pe, *name)
                m = lhs(0).shape[-1]
                for a in range(2):
                    for k in range(nk):
                        if first_wait and a == 0:
                            first_wait(k)
                        last = pe.matmul(ptile(*name)[0:m, a, :], lhs(k), rhs(k)[:, HALF * a:HALF * a + HALF],
                                         start=(k == 0), stop=(k == nk - 1))
                done(last, *name)

            def products(out, wts, cols, x, k, n, tokens, first, last):
                hi, lo = wts
                pe.matmul(out, hi[:, k, cols], x.hi_block(n)[:, tokens], start=first, stop=False)
                pe.matmul(out, hi[:, k, cols], x.lo_block(n)[:, tokens], start=False, stop=False)
                return pe.matmul(out, lo[:, k, cols], x.hi_block(n)[:, tokens], start=False, stop=last)

            def project3(name, wts, cols, x, ready=None):
                claim(pe, *name)
                m = cols.stop - cols.start
                for a in range(2):
                    for k in range(KT):
                        if ready and a == 0:
                            ready(k)
                        last = products(ptile(*name)[0:m, a, :], wts, cols, x, k, k,
                                        slice(HALF * a, HALF * a + HALF), k == 0, k == KT - 1)
                done(last, *name)

            def column(c):
                return slice(P * (c % 2), P * (c % 2) + P)

            def rms_sum(i):
                pe.wait_ge(S_("squares_act"), i + 1)
                pe.wait_ge(S_("squares_dve"), i + 1)
                project(('rms', i), lambda k: ones[:, :], lambda k: SQ[i][:, k, :], KT)

            def row_tile(kind, c, r):
                hi, lo = split((kind, c), 256)
                claim(pe, kind, c, r)
                out, t = pbank(kind, c, r)[0:width(r), 0, 0:256], slice(P * r, P * r + width(r))
                for k in range(KT):
                    pe.matmul(out, xn1.hi_block(k)[:, t], hi[:, k, :], start=(k == 0), stop=False)
                    pe.matmul(out, xn1.hi_block(k)[:, t], lo[:, k, :], start=False, stop=False)
                    last = pe.matmul(out, xn1.lo_block(k)[:, t], hi[:, k, :], start=False, stop=(k == KT - 1))
                done(last, kind, c, r)

            def column_tile(kind, c):
                project3((kind, c), split((kind, c // 2), 256), column(c), xn1)

            def sides(*place):
                for tile in side_at.get(place, ()):
                    (row_tile if tile[0] == 'sv' else column_tile)(*tile)

            pe.wait_ge(S_("consts_in"), 16)
            pe.wait_ge(S_("x_in"), 32)
            for r in range(R):
                for q in range(2):
                    claim(pe, 'x', r, q)
                    w = width(r)
                    for i in range(4):
                        last = pe.transpose(bank('x', r, q)[:, P * i:P * i + w],
                                            XL[0:w, r, P * (4 * q + i):P * (4 * q + i) + P], ident[0:w, 0:w])
                    done(last, 'x', r, q)
            pe.wait_ge(S_("vec_in"), 96)
            claim(pe, 'vec')
            pe.transpose(bank('vec')[:, 0:128], VR[:, 0, :], ident)
            done(pe.transpose(bank('vec')[:, 128:200], VR[0:72, 1, :], ident[0:72, 0:72]), 'vec')
            pe.wait_ge(S_("rbb_set"), 1)
            for h in range(H):
                claim(pe, 'bias', h)
                done(pe.matmul(bank('bias', h)[:, 0:BIASW], RBB[:, h, :], const('bucket', 32), start=True, stop=True),
                     'bias', h)
            pe.wait_ge(S_("ones_set"), 1)
            rms_sum(0)
            for m in range(4):
                project3(('iq', m), split(('iq', m // 2), 256), column(m), xn1,
                         (lambda k: pe.wait_ge(S_("xn_ready"), k + 1)) if m == 0 else None)
            project3(('ikw',), split(('ikw',), 72), slice(0, 72), xn1)
            drained(pe, 'iq', 3)
            claim(pe, 'iqsw')
            for m in range(4):
                last = pe.matmul(bank('iqsw')[:, 64 * m:64 * m + 64], const('swap'), iqT[:, m, TP:T],
                                 start=True, stop=True)
            done(last, 'iqsw')
            drained(pe, 'ikw')
            for i, (a, b) in enumerate(((0, TP), (TP, T))):
                claim(pe, f'ikd{i}')
                done(pe.matmul(bank(f'ikd{i}')[:, 0:b - a], const('dup', 72), IKW[0:72, a:b], start=True, stop=True),
                     f'ikd{i}')
            claim(pe, 'ikwT')
            for r in range(R):
                last = pe.transpose(bank('ikwT')[0:width(r), 72 * r:72 * r + 72],
                                    IKW[0:72, P * r:P * r + width(r)], ident[0:72, 0:72])
            done(last, 'ikwT')
            pe.wait_ge(S_("iw_ready"), 1)
            claim(pe, 'iwrep')
            for p in range(4):
                last = pe.matmul(bank('iwrep')[:, 8 * p:8 * p + 8], const('selp', TS)[:, P * p:P * p + P],
                                 IWS[0:TS, 4, :], start=True, stop=True)
            done(last, 'iwrep')
            drained(pe, 'ikd0')
            for r in range(1, 4):
                for h in range(H):
                    claim(pe, 'ps', r, h)
                    done(pe.matmul(bank('ps', r, h)[:, 0:P * (r + 1)], iqT[:, h // 2, P * r:P * r + P],
                                   IKPAD[:, h % 2, 0:P * (r + 1)], start=True, stop=True), 'ps', r, h)
            pe.wait_ge(S_("iqb_ready"), 1)
            pe.wait_ge(S_("swm_ready"), 1)
            for s in range(18):
                if s < 16:
                    pe.wait_ge(idx_in[s % 4], 128 * (s // 4 + 1))
                    claim(pe, 't', s)
                    for j in range(4):
                        last = pe.transpose(bank('t', s)[:, P * j:P * j + P],
                                            IKN[s % 4][:, j, :, :].rearrange("p a d -> p (a d)"), ident)
                    done(last, 't', s)
                if 1 <= s < 17:
                    drained(pe, 't', s - 1)
                    claim(pe, 's1', s - 1)
                    done(pe.matmul(bank('s1', s - 1), IQB[:, (s - 1) % 4, :], IKT[(s - 1) % 2], start=True, stop=True),
                         's1', s - 1)
                if s >= 2:
                    kc, p = (s - 2) // 4, (s - 2) % 4
                    drained(pe, 's1', s - 2)
                    if p == 0:
                        claim(pe, 'ss', kc)
                    last = pe.matmul(pbank('ss', kc)[0:TS, 0, :], SWM[:, p, :], RL2[(s - 2) % 2],
                                     start=(p == 0), stop=(p == 3))
                    if p == 3:
                        done(last, 'ss', kc)
                    else:
                        last.then_inc(S_("heads_summed"), 1)
                if s % 2 == 1 and s < 16:
                    column_tile('q', s // 2)
            drained(pe, 'ikd1')
            claim(pe, 's1n')
            for p in range(4):
                last = pe.matmul(bank('s1n')[:, 8 * p:8 * p + 8], IQB[:, p, :], IKNEW[:, p, :], start=True, stop=True)
            done(last, 's1n')
            drained(pe, 's1n')
            claim(pe, 'ssn')
            for p in range(4):
                last = pe.matmul(pbank('ssn')[0:TS, 0, 0:8], SWM[:, p, :], RLN[:, 8 * p:8 * p + 8],
                                 start=(p == 0), stop=(p == 3))
            done(last, 'ssn')

            for c in range(8):
                column_tile('k', c)
            drained(pe, 'k', 7)
            for r in range(R):
                for q in range(2):
                    claim(pe, 'kt', r, q)
                    for i in range(4):
                        last = pe.transpose(bank('kt', r, q)[0:width(r), P * i:P * i + P],
                                            kT[:, 4 * q + i, P * r:P * r + width(r)], ident)
                    done(last, 'kt', r, q)
            for c in range(4):
                for r in range(R):
                    row_tile('v', c, r)
            drained(pe, 'v', 3, 4)
            for h in range(H + 1):
                if h < H:
                    for r in range(4):
                        claim(pe, 'pl', h, r)
                        done(pe.matmul(bank('pl', h, r)[:, 0:P * (r + 1)], qT[:, h, P * r:P * r + P],
                                       kT[:, h, 0:P * (r + 1)], start=True, stop=True), 'pl', h, r)
                    sides('B', h, 0)
                if h:
                    drained(pe, 'pt', h - 1, 3)
                    claim(pe, 'pv', h - 1)
                    for s in range(4):
                        last = pe.matmul(bank('pv', h - 1)[:, P * s:TP], V[:, s, HD * (h - 1):HD * h],
                                         PT[:, s, P * s:TP], start=(s == 0), stop=(s == 3), skip_group_check=True)
                    done(last, 'pv', h - 1)
                if h < H:
                    sides('B', h, 1)
                    for r in range(4):
                        pe.wait_ge(S_("probs_ready"), 4 * h + r + 1)
                        claim(pe, 'pt', h, r)
                        for s in range(r + 1):
                            last = pe.transpose(bank('pt', h, r)[:, P * s:P * s + P],
                                                L[:, SP_OFF[r] + P * s:SP_OFF[r] + P * s + P], ident)
                        done(last, 'pt', h, r)

            pe.wait_ge(S_("ring_free"), 1)
            for G in range(2):
                for n in range(65):
                    if n < 64:
                        seq = 128 * G + n
                        pe.wait_ge(page_in[seq % 8], 16 * (seq // 8 + 1))
                        for u in range(2):
                            claim(pe, 'kp', G, n, u)
                            for i in range(4):
                                h = 4 * u + i
                                last = pe.transpose(bank('kp', G, n, u)[:, P * i:P * i + P],
                                                    ring[seq % 8][:, HD * h:HD * h + HD], ident)
                            done(last, 'kp', G, n, u)
                    if n:
                        kp, bb = (n - 1) // 4, (n - 1) % 4
                        if bb == 0:
                            claim(pe, 'kl', G, kp)
                        for u in range(2):
                            drained(pe, 'kp', G, n - 1, u)
                            for j in range(4):
                                h = 4 * u + j
                                last = pe.matmul(pbank('kl', G, kp)[32 * j:32 * j + 32, u, 0:P],
                                                 QZ[:, h, 4 * G + bb, :], KTb[(n - 1) % 2][:, h, :],
                                                 start=(bb == 0), stop=(bb == 3))
                        if bb == 3:
                            done(last, 'kl', G, kp)
                claim(pe, 'kl', G, NPG - 1)
                for u in range(2):
                    for j in range(4):
                        h = 4 * u + j
                        last = pe.matmul(pbank('kl', G, NPG - 1)[32 * j:32 * j + 32, u, 0:P],
                                         QN[:, h, 32 * G:32 * G + 32], kTn[:, h, :], start=True, stop=True)
                done(last, 'kl', G, NPG - 1)
                for g in range(2):
                    sides('softmax', G, g)
                    pe.wait_ge(S_("sample_probs"), 2 * G + g + 1)
                    for q in range(5):
                        claim(pe, 'st', G, g, q)
                        for i in range(4 if q < 4 else 1):
                            c = P * (4 * q + i)
                            last = pe.transpose(bank('st', G, g, q)[:, P * i:P * i + P], LS[:, g, c:c + P], ident)
                        done(last, 'st', G, g, q)
                drained(pe, 'st', G, 0, 4)
                drained(pe, 'st', G, 1, 4)
                for b in range(4):
                    claim(pe, 'o', G, b)
                    for kp in range(NPG):
                        if kp < NPAGES:
                            seq = 128 * G + 64 + 16 * b + kp
                            pe.wait_ge(page_in[seq % 8], 16 * (seq // 8 + 1))
                            page = ring[seq % 8]
                        else:
                            page = Vn[:, :]
                        for u in range(2):
                            for j in range(4):
                                h = 4 * u + j
                                last = pe.matmul(pbank('o', G, b)[32 * j:32 * j + 32, u, 0:HD],
                                                 PTs[:, u, kp, 32 * j:32 * j + 32], page[:, HD * h:HD * h + HD],
                                                 start=(kp == 0), stop=(kp == NPG - 1))
                        if kp < NPAGES:
                            last.then_inc(S_("v_pages_used"), 1)
                        else:
                            done(last, 'o', G, b)
                        sides('V', G, b, kp)
                    drained(pe, 'o', G, b)
                    for g in range(2):
                        claim(pe, 'ot', G, b, g)
                        done(pe.transpose(bank('ot', G, b, g)[:, 0:P], OS[b % 2][:, g, :], ident), 'ot', G, b, g)

            for c in range(8):
                project3(('wa', c), split(('wa', c // 2), 256), column(c), oa,
                         (lambda k: pe.wait_ge(S_("oa_split"), k + 1)) if c == 0 else None)
            pe.wait_ge(S_("ws_causal"), 1)
            for q in range(2):
                claim(pe, 'w', q)
                for i in range(4):
                    last = pe.transpose(bank('w', q)[:, P * i:P * i + P], WS[:, 4 * q + i, :], ident)
                done(last, 'w', q)
            drained(pe, 'w', 1)
            claim(pe, 'bd')
            done(pe.matmul(bank('bd')[0:TS, 0:64], const('rep', 8), WT[0:8, :, 0:8], start=True, stop=True), 'bd')
            pe.wait_ge(S_("sv_normed"), 1)
            pe.wait_ge(S_("bd_ready"), 1)
            for g in range(8):
                claim(pe, 'sg', g)
                for c in range(4):
                    last = pe.matmul(bank('sg', g)[:, P * c:P * c + P], SV[:, c, P * g:P * g + P], WT[:, g, :],
                                     start=True, stop=True)
                done(last, 'sg', g)
                claim(pe, 'sgs', g)
                done(pe.matmul(bank('sgs', g)[:, 0:TS], SV[0:TS, 4, P * g:P * g + P], BD[:, g, :],
                               start=True, stop=True), 'sgs', g)
            for c in range(8):
                project3(('wb', c), split(('wb', c // 2), 256), column(c), ob,
                         (lambda k: pe.wait_ge(S_("ob_split"), k + 1)) if c == 0 else None)
            for c in range(8):
                project3(('out', c), split(('out', c // 2), 256), column(c), mg,
                         (lambda k: pe.wait_ge(S_("mg_split"), k + 1)) if c == 0 else None)
            rms_sum(1)
            pe.wait_ge(S_("state_in"), 32)
            for q in range(2):
                claim(pe, 'state', q)
                for i in range(4 if q == 0 else 2):
                    n = 64 if (q, i) == (1, 1) else P
                    last = pe.transpose(bank('state', q)[:, P * i:P * i + n], SRAW[0:n, 4 * q + i, :], ident[0:n, 0:n])
                done(last, 'state', q)
            for f in range(FB):
                wts = split(('up', f), 256)
                for k2 in range(2):
                    project3(('up', f, k2), wts, column(k2), xn2,
                             (lambda k: pe.wait_ge(S_("xn_ready"), 8 + k + 1)) if (f, k2) == (0, 0) else None)
            for c in range(8):
                claim(pe, 'dn', c)
                for kh in range(2):
                    hi, lo = split(('dn', c, kh), P, 11)
                    for a in range(2):
                        out, t = ptile('dn', c)[:, a, :], slice(HALF * a, HALF * a + HALF)
                        for k in range(11):
                            n = 11 * kh + k
                            if c == 0 and a == 0:
                                pe.wait_ge(S_("act_ready"), n + 1)
                            pe.matmul(out, hi[:, k, :], gated(n, 0)[:, t], start=(n == 0), stop=False)
                            pe.matmul(out, hi[:, k, :], gated(n, 1)[:, t], start=False, stop=False)
                            last = pe.matmul(out, lo[:, k, :], gated(n, 0)[:, t], start=False, stop=(n == FB - 1))
                    if kh == 0:
                        last.then_inc(S_("down_halves"), 1)
                done(last, 'dn', c)
            pe.wait_ge(S_("conv_rows"), FB)
            for q in range(2):
                claim(pe, 'ho', q)
                for i in range(4 if q == 0 else 3):
                    n = 4 * q + i
                    src = HCP if n == 0 else HCS[:, P * (n - 1):min(P * n, 704)]
                    m = src.shape[-1]
                    last = pe.transpose(bank('ho', q)[0:m, P * i:P * i + P], src, ident)
                done(last, 'ho', q)
            rms_sum(2)
            pe.wait_ge(S_("xn_whole"), 24)
            for r in range(R):
                for q in range(2):
                    claim(pe, 'y', r, q)
                    for i in range(4):
                        last = pe.transpose(bank('y', r, q)[0:width(r), P * i:P * i + P],
                                            YN[:, 4 * q + i, P * r:P * r + width(r)], ident)
                    done(last, 'y', r, q)

        @block.scalar
        def _(act):
            def split_high(*name):
                n, value = chunks[name]
                act.wait_ge(weights_in[n % NW], value)
                if n >= NH:
                    chunk_used(act, n - NH)
                c = chunk_words(name)
                act.activation(WH[n % NH][:, 0:c], W[n % NW][:, 0:c], ACT.Copy).then_inc(S_("high_ready"), 1)

            def squares(i):
                act.activation(SQ[i][:, 0:4, :], xT[i][:, 0:4, :], ACT.Square).then_inc(S_("squares_act"), 1)

            def root(i):
                drained(act, 'rms', i)
                act.activation(RS[i], RS[i], ACT.Sqrt).then_inc(S_("rms_root"), 1)

            def high(x, k, ready, value, signal):
                act.wait_ge(S_(ready), value)
                act.activation(x.hi_block(k), x.whole_block(k), ACT.Copy).then_inc(S_(signal), 1)

            after = split_after(split_high)

            def side_tile(*tile):
                i = side.index(tile)
                after(*tile)
                filled(act, *tile)
                if i >= 2:
                    act.wait_ge(S_(f"side_stored{i % 2}"), 16 * (i // 2))
                kind, c = tile[0], tile[1]
                if kind == 'sv':
                    n = width(tile[2])
                    dst, src = stage[i % 2][0:n, 0:256], pbank(*tile)[0:n, 0, 0:256]
                    out = sv_scr[tile[2], 0:n, 256 * c:256 * c + 256]
                else:
                    dst, src, out = halves(stage[i % 2]), ptile(*tile), side_scr[kind][:, c, :]
                act.activation(dst, src, ACT.Sigmoid if kind in ('ga', 'gb') else ACT.Gelu_apprx_tanh)\
                    .then_inc(drains(*tile), 1)
                drained(act, *tile)
                act.dma_start(out, dst if kind == 'sv' else stage[i % 2]).then_inc(S_(f"side_stored{i % 2}"), 16)

            def sides(*place):
                for tile in side_at.get(place, ()):
                    side_tile(*tile)

            def query(c):
                after('q', c)
                filled(act, 'q', c)
                act.activation(halves(qT[:, c, :]), ptile('q', c), ACT.Copy, scale=ATT_SCALE).then_inc(drains('q', c), 1)

            for r in range(R):
                filled(act, 'x', r, 0)
                act.activation(xT0[:, 0:4, P * r:P * r + width(r)], blocks(bank('x', r, 0), 4)[:, :, 0:width(r)],
                               ACT.Copy).then_inc(drains('x', r, 0), 1)
            drained(act, 'x', R - 1, 0)
            squares(0)
            split_high('iq', 0)
            for h in range(H):
                filled(act, 'bias', h)
                act.activation(BV[:, h, :], bank('bias', h)[:, 0:BIASW], ACT.Copy).then_inc(drains('bias', h), 1)
            root(0)
            for k in range(KT):
                high(xn1, k, "xn_whole", k + 1, "xn_high")
            for m in range(4):
                after('iq', m)
                filled(act, 'iq', m)
                act.activation(halves(iqT[:, m, :]), ptile('iq', m), ACT.Copy).then_inc(drains('iq', m), 1)
            after('ikw')
            filled(act, 'ikw')
            act.activation(halves(IKW[0:72, :]), ptile('ikw')[0:72], ACT.Copy).then_inc(drains('ikw'), 1)
            k = 0
            for r in range(1, 4):
                for h in range(H):
                    filled(act, 'ps', r, h)
                    if k >= 2:
                        act.wait_ge(S_("relu_used"), k - 1)
                    act.activation(RL[k % 2][:, 0:P * (r + 1)], bank('ps', r, h)[:, 0:P * (r + 1)], ACT.Relu)\
                        .then_inc(drains('ps', r, h), 1)
                    k += 1
            for s in range(18):
                if s < 16:
                    filled(act, 't', s)
                    if s >= 2:
                        filled(act, 's1', s - 2)
                    act.activation(IKT[s % 2], bank('t', s), ACT.Copy).then_inc(drains('t', s), 1)
                if 1 <= s < 17:
                    filled(act, 's1', s - 1)
                    if s >= 3:
                        kc, p = (s - 3) // 4, (s - 3) % 4
                        if p == 3:
                            filled(act, 'ss', kc)
                        else:
                            act.wait_ge(S_("heads_summed"), 3 * kc + p + 1)
                    act.activation(RL2[(s - 1) % 2], bank('s1', s - 1), ACT.Relu).then_inc(drains('s1', s - 1), 1)
                if s % 2 == 1 and s < 16:
                    query(s // 2)
            filled(act, 's1n')
            act.activation(RLN, bank('s1n')[:, 0:32], ACT.Relu).then_inc(drains('s1n'), 1)
            act.wait_ge(S_("bias_out"), 16)
            for c in range(8):
                after('k', c)
                filled(act, 'k', c)
                act.activation(halves(kT[:, c, :]), ptile('k', c), ACT.Copy).then_inc(drains('k', c), 1)
            for r in range(R):
                for q in range(2):
                    filled(act, 'kt', r, q)
                    if r >= 2 and q == 0:
                        act.wait_ge(S_(f"k_stored{r % 2}"), 16 * (r // 2))
                    act.activation(KO[r % 2][0:width(r), 512 * q:512 * q + 512], bank('kt', r, q)[0:width(r)],
                                   ACT.Copy).then_inc(drains('kt', r, q), 1)
            for c in range(4):
                for r in range(R):
                    after('v', c, r)
                    filled(act, 'v', c, r)
                    dst = V[:, r, 256 * c:256 * c + 256] if r < 4 else Vn[0:TS, 256 * c:256 * c + 256]
                    act.activation(dst, pbank('v', c, r)[0:width(r), 0, 0:256], ACT.Copy).then_inc(drains('v', c, r), 1)
            for h in range(H + 1):
                if h < H:
                    act.wait_ge(S_("max_ready"), h + 1)
                    for r in range(4):
                        n, o = P * (r + 1), SP_OFF[r]
                        last = act.activation(L[:, o:o + n], L[:, o:o + n], ACT.Exp, bias=NM[h % 2][:, r:r + 1],
                                              accum_out=SU[h % 2][:, r:r + 1])
                    last.then_inc(S_("exp_done"), 1)
                    sides('B', h, 0)
                if h:
                    filled(act, 'pv', h - 1)
                    if h == 1:
                        act.wait_ge(S_("x_out"), 16)
                    act.activation(oaT[:, h - 1, 0:TP], bank('pv', h - 1), ACT.Copy).then_inc(drains('pv', h - 1), 1)
                if h < H:
                    sides('B', h, 1)
                    if h == 0:
                        act.wait_ge(S_("k_stored0"), 48)
                        act.wait_ge(S_("k_stored1"), 32)
                    for r in range(4):
                        filled(act, 'pt', h, r)
                        act.activation(PT[:, 0:r + 1, P * r:P * r + P], blocks(bank('pt', h, r), 4)[:, 0:r + 1, :],
                                       ACT.Copy).then_inc(drains('pt', h, r), 1)
            for G in range(2):
                for n in range(64):
                    filled(act, 'kp', G, n, 0)
                    act.activation(KTb[n % 2][:, 0:4, :], blocks(bank('kp', G, n, 0), 4), ACT.Copy)\
                        .then_inc(drains('kp', G, n, 0), 1)
                act.wait_ge(S_("sample_max"), G + 1)
                for g in range(2):
                    act.activation(LS[:, g, :], LS[:, g, :], ACT.Exp, bias=NM[0][:, g:g + 1],
                                   accum_out=SU[0][:, g:g + 1]).then_inc(S_("sample_exp"), 1)
                sides('softmax', G, 0)
                for q in range(5):
                    filled(act, 'st', G, 0, q)
                    m = 4 if q < 4 else 1
                    act.activation(PTs[:, 0, 4 * q:4 * q + m, :], blocks(bank('st', G, 0, q), 4)[:, 0:m, :], ACT.Copy)\
                        .then_inc(drains('st', G, 0, q), 1)
                sides('softmax', G, 1)
                for b in range(4):
                    for kp in range(NPG):
                        sides('V', G, b, kp)
                    t = TP + 32 * G + 8 * b
                    for g in range(2):
                        filled(act, 'ot', G, b, g)
                        act.activation(oaT[:, 4 * g:4 * g + 4, t:t + 8],
                                       blocks(bank('ot', G, b, g)[:, 0:P], 4)[:, :, 8 * b:8 * b + 8], ACT.Copy)\
                            .then_inc(drains('ot', G, b, g), 1)
            for g in range(2):
                drained(act, 'ot', 1, 3, g)
            for g in range(8):
                act.activation(oa.hi_block(g), oa.whole_block(g), ACT.Copy).then_inc(S_("oa_high"), 1)
            for c in (0, 2, 4):
                after('wa', c)
            act.wait_ge(S_("sv_mean"), 1)
            act.activation(SS, SS, ACT.Sqrt).then_inc(S_("sv_root"), 1)
            after('wa', 6)
            filled(act, 'wa', 7)
            for g in range(8):
                high(ob, g, "ob_whole", g + 1, "ob_high")
            for c in (0, 2, 4, 6):
                after('wb', c)
            filled(act, 'wb', 7)
            for c in range(8):
                high(mg, c, "merged", c + 1, "mg_high")
            for c in range(0, 8, 2):
                after('out', c)
            drained(act, 'out', 3)
            drained(act, 'out', 2)
            filled(act, 'out', 7)
            squares(1)
            root(1)
            for k in range(KT):
                high(xn2, k, "xn_whole", 8 + k + 1, "xn_high")

            def gated_high(f):
                act.wait_ge(S_("act_whole"), f + 1)
                act.activation(gated(f, 0), gated_whole(f), ACT.Copy).then_inc(S_("act_high"), 1)

            for f in range(FB):
                for k in range(2):
                    after('up', f, k)
                    filled(act, 'up', f, k)
                    if f >= 2:
                        act.wait_ge(S_("act_whole"), f - 1)
                        act.wait_ge(S_("conv_rows"), f - 1)
                    hp, pt = HPb[f % 2][k], pbank('up', f, k)
                    act.activation(hp[:, 2:2 + HALF], pt[:, 0, 0:HALF], ACT.Copy)
                    act.activation(hp[:, 2 + HALF:514], pt[:, 1, 0:TP - HALF], ACT.Copy)
                    act.activation(hp[:, 514:594].rearrange("p (b c) -> p b c", b=8)[:, :, 2:10],
                                   pt[:, 1, TP - HALF:HALF].rearrange("p (b c) -> p b c", b=8), ACT.Copy)\
                        .then_inc(drains('up', f, k), 1)
                    if k == 1 and f:
                        gated_high(f - 1)
                    drained(act, 'up', f, k)
                    act.wait_ge(S_("state_put"), 2 * f + k + 1)
                    fb = FB * k + f
                    act.activation(CB[f % 2][k], hp[:, 2:594], ACT.Identity, bias=VT[:, 156 + fb:157 + fb],
                                   scale=VT[:, 112 + fb:113 + fb]).then_inc(S_("tap2_done"), 1)
                act.wait_ge(S_("taps_done"), 2 * f + 1)
                act.activation(CB[f % 2][0], CB[f % 2][0], ACT.Silu).then_inc(S_("silu_done"), 1)
            gated_high(FB - 1)
            for c in range(8):
                after('dn', c)
            drained(act, 'dn', 3)
            drained(act, 'dn', 2)
            filled(act, 'dn', 7)
            squares(2)
            root(2)
            for r in range(R):
                filled(act, 'y', r, 0)
                if r >= 2:
                    act.wait_ge(S_(f"y_stored{r % 2}"), 16 * (r // 2))
                act.activation(YO[r % 2][0:width(r), 0:512], bank('y', r, 0)[0:width(r)], ACT.Copy)\
                    .then_inc(drains('y', r, 0), 1)

        @block.vector
        def _(dve):
            steps = [0]

            def link(ins):
                steps[0] += 1
                ins.then_inc(S_("dve_step"), 1)
                dve.wait_ge(S_("dve_step"), steps[0])

            def split_low(*name):
                n, c = chunks[name][0], chunk_words(name)
                dve.wait_ge(S_("high_ready"), n + 1)
                dve.tensor_tensor(WL[n % NW][:, 0:c], W[n % NW][:, 0:c], WH[n % NH][:, 0:c].bitcast(F32),
                                  ALU.subtract).then_inc(S_("low_ready"), 1)

            def low(x, k, ready, value, signal):
                dve.wait_ge(S_(ready), value)
                dve.tensor_tensor(x.lo_block(k), x.whole_block(k), x.hi_block(k).bitcast(F32), ALU.subtract)\
                    .then_inc(S_(signal), 1)

            after = split_after(split_low)

            def squares(i):
                dve.tensor_tensor(SQ[i][:, 4:8, :], xT[i][:, 4:8, :], xT[i][:, 4:8, :], ALU.mult).then_inc(S_("squares_dve"), 1)

            def normalise(i, gcol):
                filled(dve, 'rms', i)
                dve.tensor_scalar(halves(RS[i]), ptile('rms', i), 1.0 / D, EPS, ALU.mult, ALU.add)\
                    .then_inc(drains('rms', i), 1)
                dve.wait_ge(S_("rms_root"), i + 1)
                link(dve.reciprocal(RS[i], RS[i]))

                def whole(k):
                    dst = YN if i == 2 else (xn1, xn2)[i].whole
                    dve.scalar_tensor_tensor(dst[:, k, :], xT[i][:, k, :], VT[:, gcol + k:gcol + k + 1], RS[i],
                                             ALU.mult, ALU.mult).then_inc(S_("xn_whole"), 1)

                for k in range(KT):
                    whole(k)
                    if i < 2 and k:
                        low((xn1, xn2)[i], k - 1, "xn_high", 8 * i + k, "xn_ready")
                if i < 2:
                    low((xn1, xn2)[i], KT - 1, "xn_high", 8 * i + KT, "xn_ready")

            for r in range(R):
                filled(dve, 'x', r, 1)
                dve.tensor_copy(xT0[:, 4:8, P * r:P * r + width(r)], blocks(bank('x', r, 1), 4)[:, :, 0:width(r)])\
                    .then_inc(drains('x', r, 1), 1)
            drained(dve, 'x', R - 1, 1)
            squares(0)
            filled(dve, 'vec')
            dve.tensor_copy(VT[:, :], bank('vec')[:, 0:200]).then_inc(drains('vec'), 1)
            drained(dve, 'vec')
            drained(dve, 'x', R - 1, 0)
            split_low('iq', 0)
            normalise(0, 0)
            for t in (('iq', 0), ('iq', 2)):
                after(*t)
            dve.wait_ge(S_("consts_in"), 16)
            dve.tensor_copy(MS[:, 0:P], const('caus'))
            filled(dve, 'iqsw')
            dve.tensor_copy(IQSW, blocks(bank('iqsw')[:, 0:256], 4)).then_inc(drains('iqsw'), 1)
            filled(dve, 'ikd0')
            dve.tensor_copy(IKPAD[0:64, 0, :], bank('ikd0')[0:64])
            dve.tensor_copy(IKPAD[64:128, 1, :], bank('ikd0')[64:128]).then_inc(drains('ikd0'), 1)
            filled(dve, 'ikd1')
            nk = bank('ikd1')[:, 0:64].rearrange("p (q u t) -> p q u t", q=4, u=2)
            dve.tensor_copy(IKNEW[0:64], nk[0:64, :, 0, :])
            dve.tensor_copy(IKNEW[64:128], nk[64:128, :, 1, :]).then_inc(drains('ikd1'), 1)
            filled(dve, 'ikwT')
            dve.tensor_copy(IKWT[:, 0:4, :], blocks(bank('ikwT')[:, 0:288], 4))
            dve.tensor_copy(IKWT[0:TS, 4, :], bank('ikwT')[0:TS, 288:360]).then_inc(drains('ikwT'), 1)
            drained(dve, 'ikwT')
            dve.tensor_scalar(IWS[:, 0:4, :], IKWT[:, 0:4, 64:72], IDX_SCALE, None, ALU.mult)
            dve.tensor_scalar(IWS[0:TS, 4, :], IKWT[0:TS, 4, 64:72], IDX_SCALE, None, ALU.mult)\
                .then_inc(S_("iw_ready"), 1)
            filled(dve, 'iwrep')
            dve.tensor_tensor(TMP32, blocks(bank('iwrep')[:, 0:32], 4),
                              const('hmask')[:, None, :].broadcast_to([P, 4, 8]), ALU.mult).then_inc(drains('iwrep'), 1)
            drained(dve, 'iwrep')
            link(dve.tensor_reduce(IWC, TMP32, AX_X, ALU.add))
            for p in range(4):
                last = dve.tensor_scalar(SWM[:, p, :], const('selT')[:, TS * p:TS * p + TS], IWC[:, p:p + 1], None,
                                         ALU.mult)
            last.then_inc(S_("swm_ready"), 1)
            def prompt_best(r):
                n, o = P * (r + 1), SP_OFF[r]
                for k in range(TOPK_P // 8):
                    link(dve.max(MAX8P, MS[:, o:o + n]))
                    link(dve.match_replace(MS[:, o:o + n], MAX8P, MS[:, o:o + n], MARK))
                dve.tensor_scalar(MS[:, o:o + n], MS[:, o:o + n], MARK, NEG, ALU.not_equal, ALU.mult)\
                    .then_inc(S_("prompt_mask"), 1)

            k = 0
            for r in range(1, 4):
                n, o = P * (r + 1), SP_OFF[r]
                for h in range(H):
                    drained(dve, 'ps', r, h)
                    if h == 0:
                        dve.tensor_scalar(MS[:, o:o + n], RL[k % 2][:, 0:n], IWS[:, r, h:h + 1], None, ALU.mult)\
                            .then_inc(S_("relu_used"), 1)
                    else:
                        dve.wait_ge(S_("relu_used"), k)
                        dve.scalar_tensor_tensor(MS[:, o:o + n], RL[k % 2][:, 0:n], IWS[:, r, h:h + 1],
                                                 MS[:, o:o + n], ALU.mult, ALU.add).then_inc(S_("relu_used"), 1)
                    k += 1
                dve.wait_ge(S_("relu_used"), k)
                link(dve.tensor_tensor(MS[:, o + P * r:o + n], MS[:, o + P * r:o + n], const('caus'), ALU.add))
            after('ikw')
            after('q', 0)
            prompt_best(1)
            for kc in range(4):
                filled(dve, 'ss', kc)
                dve.tensor_copy(S[:, 512 * kc:512 * kc + 512], pbank('ss', kc)[0:TS, 0, :]).then_inc(drains('ss', kc), 1)
                if kc < 3:
                    after('q', 2 * kc + 2)
                if kc < 2:
                    prompt_best(kc + 2)
            filled(dve, 'ssn')
            dve.tensor_tensor(S[:, PAST:NKEY], pbank('ssn')[0:TS, 0, 0:8], const('newcausal', TS), ALU.add)\
                .then_inc(drains('ssn'), 1)
            drained(dve, 'ssn')
            rounds = [TOPK_S // 8]

            def sample_best(n):
                for _ in range(min(n, rounds[0])):
                    rounds[0] -= 1
                    link(dve.max(MAX8, S[:, 0:NKEY]))
                    link(dve.match_replace(S[:, 0:NKEY], MAX8, S[:, 0:NKEY], MARK))

            for t in [('k', 2 * i) for i in range(4)] + [('v', i, 0) for i in range(4)]:
                sample_best(2 + t[1] % 2 if t[0] == 'v' else 2 + t[1] // 2 % 2)
                after(*t)
            for h in range(H):
                dve.wait_ge(S_("bias_mask_ready"), h + 1)
                for r in range(4):
                    n, o = P * (r + 1), SP_OFF[r]
                    filled(dve, 'pl', h, r)
                    dve.tensor_tensor_reduce(out=L[:, o:o + n], in0=bank('pl', h, r)[:, 0:n], in1=MB[h % 2][:, o:o + n],
                                             scale=1.0, scalar=MARK, op0=ALU.add, op1=ALU.max,
                                             accum_out=MX[h % 2][:, r:r + 1]).then_inc(drains('pl', h, r), 1)
                drained(dve, 'pl', h, 3)
                dve.tensor_scalar(NM[h % 2], MX[h % 2], -1.0, None, ALU.mult).then_inc(S_("max_ready"), 1)
                for i in range(2):
                    for tile in side_at['B', h, i]:
                        after(*tile)
                sample_best(1)
                dve.wait_ge(S_("exp_done"), h + 1)
                link(dve.reciprocal(RC[h % 2], SU[h % 2]))
                for r in range(4):
                    n, o = P * (r + 1), SP_OFF[r]
                    dve.tensor_scalar(L[:, o:o + n], L[:, o:o + n], RC[h % 2][:, r:r + 1], None, ALU.mult)\
                        .then_inc(S_("probs_ready"), 1)
                sample_best(h % 2)
            sample_best(TOPK_S)
            link(dve.tensor_scalar(M8, S[:, PAST:NKEY], MARK, NEG, ALU.not_equal, ALU.mult))
            dve.tensor_scalar(S[:, 0:PAST], S[:, 0:PAST], MARK, NEG, ALU.not_equal, ALU.mult)
            dve.memset(S[:, PAST + TS:NCOL], NEG)
            dve.tensor_tensor(S[:, PAST:PAST + TS].rearrange("p (b t) -> p b t", b=8),
                              const('newblock', TS).rearrange("p (b t) -> p b t", b=8),
                              M8[:, None, :].broadcast_to([TS, 8, 8]), ALU.add).then_inc(S_("sample_mask"), 1)
            def splits(*place):
                for tile in side_at.get(place, ()):
                    after(*tile)

            for G in range(2):
                dve.wait_ge(S_("mg_in"), 64 * (G + 1))

                def logits(kp):
                    filled(dve, 'kl', G, kp)
                    for g in range(2):
                        last = dve.scalar_tensor_tensor(LS[:, g, P * kp:P * kp + P], pbank('kl', G, kp)[:, g, 0:P],
                                                        NBr[:, g, 0:1], MG[:, P * kp:P * kp + P], ALU.add, ALU.add)
                    last.then_inc(drains('kl', G, kp), 1)

                for n in range(64):
                    filled(dve, 'kp', G, n, 1)
                    dve.tensor_copy(KTb[n % 2][:, 4:8, :], blocks(bank('kp', G, n, 1), 4))\
                        .then_inc(drains('kp', G, n, 1), 1)
                    if n % 4 == 0 and n:
                        logits(n // 4 - 1)
                logits(15)
                logits(16)
                drained(dve, 'kl', G, 16)
                for g in range(2):
                    link(dve.tensor_tensor(LS[:, g, 1920:NCOL], LS[:, g, 1920:NCOL], NBd[g], ALU.add))
                link(dve.tensor_reduce(MX[0][:, 0:2], LS, AX_X, ALU.max))
                dve.tensor_scalar(NM[0][:, 0:2], MX[0][:, 0:2], -1.0, None, ALU.mult).then_inc(S_("sample_max"), 1)
                splits('softmax', G, 0)
                for g in range(2):
                    dve.wait_ge(S_("sample_exp"), 2 * G + g + 1)
                    link(dve.reciprocal(RC[0][:, g:g + 1], SU[0][:, g:g + 1]))
                    dve.tensor_scalar(LS[:, g, :], LS[:, g, :], RC[0][:, g:g + 1], None, ALU.mult)\
                        .then_inc(S_("sample_probs"), 1)
                splits('softmax', G, 1)
                for q in range(5):
                    filled(dve, 'st', G, 1, q)
                    m = 4 if q < 4 else 1
                    dve.tensor_copy(PTs[:, 1, 4 * q:4 * q + m, :], blocks(bank('st', G, 1, q), 4)[:, 0:m, :])\
                        .then_inc(drains('st', G, 1, q), 1)
                for b in range(4):
                    for kp in range(NPAGES):
                        splits('V', G, b, kp)
                    filled(dve, 'o', G, b)
                    if b >= 2:
                        filled(dve, 'ot', G, b - 2, 1)
                    dve.tensor_copy(OS[b % 2], pbank('o', G, b)[:, :, 0:HD]).then_inc(drains('o', G, b), 1)
                    splits('V', G, b, NPAGES)
            for k in range(8):
                low(oa, k, "oa_high", k + 1, "oa_split")
            link(dve.memset(SS, 1.0))
            dve.wait_ge(S_("ga_back"), 16)
            for c in range(8):
                after('wa', c)
                filled(dve, 'wa', c)
                dve.tensor_tensor(halves(mT[:, c, :]), halves(GAT[:, c, :]), ptile('wa', c), ALU.mult)\
                    .then_inc(drains('wa', c), 1)
                if c == 0:
                    dve.wait_ge(S_("sv_back"), 32)
                if c < R:
                    w = width(c)
                    link(dve.tensor_tensor_reduce(out=JUNK[0:w], in0=SV[0:w, c, :], in1=SV[0:w, c, :], scale=1.0,
                                                  scalar=0.0, op0=ALU.mult, op1=ALU.add, accum_out=SS[0:w, c:c + 1]))
                if c == R - 1:
                    dve.tensor_scalar(SS, SS, 1.0 / D, EPS, ALU.mult, ALU.add).then_inc(S_("sv_mean"), 1)
                if c == R:
                    dve.wait_ge(S_("sv_root"), 1)
                    dve.wait_ge(S_("sg_in"), 32)
                    link(dve.reciprocal(SS, SS))
                    for r in range(R):
                        w = width(r)
                        last = dve.scalar_tensor_tensor(SV[0:w, r, :], SV[0:w, r, :], SS[0:w, r:r + 1], SG[0:w, :],
                                                        ALU.mult, ALU.mult)
                    last.then_inc(S_("sv_normed"), 1)
            for q in range(2):
                filled(dve, 'w', q)
                dve.tensor_copy(WT[:, 4 * q:4 * q + 4, :], blocks(bank('w', q), 4)).then_inc(drains('w', q), 1)
            filled(dve, 'bd')
            dve.tensor_tensor(BD.rearrange("p g (b t) -> p g b t", b=8),
                              bank('bd')[0:TS, 0:64].rearrange("p (g t) -> p g t", g=8)[:, :, None, :]
                              .broadcast_to([TS, 8, 8, 8]),
                              const('bd', TS).rearrange("p (b t) -> p b t", b=8)[:, None, :, :]
                              .broadcast_to([TS, 8, 8, 8]), ALU.mult).then_inc(drains('bd'), 1)
            drained(dve, 'bd')
            dve.memset(ST[0:1, 111:112], 0.0).then_inc(S_("bd_ready"), 1)
            for g in range(8):
                filled(dve, 'sg', g)
                if g >= 2:
                    dve.wait_ge(S_("ob_whole"), g - 1)
                dve.tensor_tensor(blocks(TMPS[g % 2][:, 0:TP], 4), blocks(bank('sg', g), 4),
                                  SB[:, g, None, :].broadcast_to([P, 4, P]), ALU.add).then_inc(drains('sg', g), 1)
                filled(dve, 'sgs', g)
                dve.tensor_tensor(blocks(TMPS[g % 2][:, TP:T], 8), blocks(bank('sgs', g)[:, 0:TS], 8),
                                  SB[:, g, None, 0:8].broadcast_to([P, 8, 8]), ALU.add).then_inc(drains('sgs', g), 1)
                if g:
                    low(ob, g - 1, "ob_high", g, "ob_split")
            low(ob, 7, "ob_high", 8, "ob_split")
            dve.wait_ge(S_("gb_back"), 16)
            for c in range(8):
                after('wb', c)
                filled(dve, 'wb', c)
                if c >= 2:
                    dve.wait_ge(S_("merged"), c - 1)
                else:
                    dve.wait_ge(S_("ob_whole"), 8)
                dve.tensor_tensor(halves(TMPS[c % 2]), halves(GBT[:, c, :]), ptile('wb', c), ALU.mult)\
                    .then_inc(drains('wb', c), 1)

            def residual(kind, x, value):
                for c in range(8):
                    after(kind, c)
                    filled(dve, kind, c)
                    dve.wait_ge(S_("x_back"), value)
                    dve.tensor_tensor(halves(x[:, c, :]), halves(x[:, c, :]), ptile(kind, c), ALU.add)\
                        .then_inc(drains(kind, c), 1)
                drained(dve, kind, 7)

            for c in range(8):
                low(mg, c, "mg_high", c + 1, "mg_split")
            residual('out', xT1, 16)
            squares(1)
            normalise(1, 8)
            for q in range(2):
                filled(dve, 'state', q)
                n = 512 if q == 0 else 192
                dve.tensor_copy(STT_[:, 512 * q:512 * q + n], bank('state', q)[:, 0:n]).then_inc(drains('state', q), 1)

            def gated_low(f):
                dve.wait_ge(S_("act_high"), f + 1)
                dve.tensor_tensor(gated(f, 1), gated_whole(f), gated(f, 0).bitcast(F32), ALU.subtract)\
                    .then_inc(S_("act_ready"), 1)

            for f in range(FB):
                for k in range(2):
                    after('up', f, k)
                    fb = FB * k + f
                    hp, cb = HPb[f % 2][k], CB[f % 2][k]
                    dve.wait_ge(S_("tap2_done"), 2 * f + k + 1)
                    link(dve.scalar_tensor_tensor(cb, hp[:, 1:593], VT[:, 68 + fb:69 + fb], cb, ALU.mult, ALU.add))
                    dve.scalar_tensor_tensor(cb, hp[:, 0:592], VT[:, 24 + fb:25 + fb], cb, ALU.mult, ALU.add)\
                        .then_inc(S_("taps_done"), 1)
                dve.wait_ge(S_("silu_done"), f + 1)
                dve.wait_ge(S_("taps_done"), 2 * f + 2)
                if f == NG:
                    dve.wait_ge(S_("x_out"), 32)
                a, (cg, cv) = gated_whole(f), CB[f % 2]
                dve.tensor_tensor(a[:, 0:TP], cg[:, 0:TP], cv[:, 0:TP], ALU.mult)
                dve.tensor_tensor(blocks(a[:, TP:T], 8), window(cg), window(cv), ALU.mult).then_inc(S_("act_whole"), 1)
                if f:
                    gated_low(f - 1)
            gated_low(FB - 1)
            residual('dn', xT2, 32)
            squares(2)
            normalise(2, 16)
            for q in range(2):
                filled(dve, 'ho', q)
                if q == 0:
                    dve.tensor_copy(CO[0:88, 0, :], bank('ho', 0)[0:88, 0:128])
                    dve.tensor_copy(CO[:, 1:4, :], blocks(bank('ho', 0)[:, 128:512], 3)).then_inc(drains('ho', 0), 1)
                else:
                    dve.tensor_copy(CO[:, 4:6, :], blocks(bank('ho', 1)[:, 0:256], 2))
                    dve.tensor_copy(CO[0:64, 6, :], bank('ho', 1)[0:64, 256:384]).then_inc(drains('ho', 1), 1)
            for r in range(R):
                filled(dve, 'y', r, 1)
                if r >= 2:
                    dve.wait_ge(S_(f"y_stored{r % 2}"), 16 * (r // 2))
                dve.tensor_copy(YO[r % 2][0:width(r), 512:1024], bank('y', r, 1)[0:width(r)])\
                    .then_inc(drains('y', r, 1), 1)


def window(c):
    return bass.AP(c.tensor, c.offset + 514, [c.ap[0], [10, 8], [1, 8]])


_INS = ['x_prompt', 'x_sample', 'cache_k', 'cache_v', 'cache_idx_k', 'state_ffn_conv', 'page_table', 'rel_bias',
        'norm_mix_g', 'w_in', 'sg_norm_g', 'sg_w_s', 'sg_b', 'w_branch_a', 'w_branch_b', 'w_out', 'norm_ffn_g',
        'w_up', 'ffn_conv_w', 'ffn_conv_b', 'w_down', 'norm_final_g']
_OUTS = [(1, TP, D), (NB_, NS, D), (1, 1, TP, H, HD), (1, 1, TP, H, HD), (1, 1, TP, IDX), (1, 1, 2, 2 * FF),
         (1, NB_, NS, H, HD), (1, NB_, NS, H, HD), (1, NB_, NS, IDX), (1, NB_, 2, 2 * FF), (1, NB_, NS, D)]


def kernel(**inputs):
    import concourse.bacc as _bacc
    from concourse.bass_utils import run_bass_kernel_spmd as _run

    nc = _bacc.Bacc("TRN2", target_bir_lowering=False, num_devices=1)
    arrays, args = {}, []
    for name in _INS:
        a = np.ascontiguousarray(inputs[name])
        arrays[f"in_{name}"] = a
        args.append(nc.dram_tensor(f"in_{name}", a.shape, mybir.dt.from_np(a.dtype), kind="ExternalInput").ap())
    c = shape_constants()
    arrays["in_consts"] = c
    args.append(nc.dram_tensor("in_consts", c.shape, F32, kind="ExternalInput").ap())
    for i, shape in enumerate(_OUTS):
        args.append(nc.dram_tensor(f"out_{i}", shape, F32, kind="ExternalOutput").ap())
    hybrid_kernel(nc, *args)
    r = _run(nc, [arrays], core_ids=[0])
    return tuple(r.results[0][f"out_{i}"] for i in range(len(_OUTS)))
```

```python
import math
from contextlib import ExitStack

import numpy as np
import concourse.bass as bass
from concourse import mybir

F32 = mybir.dt.float32
F32R = mybir.dt.float32r
I32 = mybir.dt.int32
ALU = mybir.AluOpType
ACT = mybir.ActivationFunctionType
AX_X = mybir.AxisListType.X

P = 128
D = 1024
KT = D // P
TP = 512
NB_, NS = 8, 8
TS = NB_ * NS
T = TP + TS
HALF = T // 2
R = 5
H, HD = 8, 128
IDX = 64
PAGE, NPAGES = 128, 16
PAST = PAGE * NPAGES
NKEY = PAST + NS
NPG = NPAGES + 1
NCOL = NPG * PAGE
FF = 2816
FB = FF // P
TOPK_P, TOPK_S = 128, 256
EPS = 1e-6
ATT_SCALE = HD ** -0.5
IDX_SCALE = IDX ** -0.5 * 8 ** -0.5
NEG = -float(2 ** 120)
MARK = -3.4028234663852886e38
ARENA = 16512
BIASW = 384
COL = dict(q=0, k=1024, v=2048, iq=3072, iw=3584, ik=3592, su=3656, sv=4680, ga=5704, gb=6728)
SP_OFF = [0, 128, 384, 768]
SP_COLS = 1280

_CONST = [('ident', 128), ('newcausal', 8), ('newblock', 64), ('caus', 128), ('bd', 64), ('rep', 64),
          ('swap', 128), ('dup', 128), ('selp', 512), ('selT', 256), ('hmask', 8), ('bucket', BIASW)]
KEPT = 6
COFF, _at = {}, 0
for _n, _w in _CONST:
    COFF[_n] = (_at, _w)
    _at += _w
NCONST = _at
NKEPT = sum(w for _, w in _CONST[:KEPT])


def shape_constants():
    c = np.zeros((P, NCONST), np.float32)

    def put(name, a):
        o, w = COFF[name]
        a = np.asarray(a, np.float32).reshape(a.shape[0], -1)
        c[:a.shape[0], o:o + w] = a

    eye = np.eye(P)
    put('ident', eye)
    put('swap', np.roll(eye, 64, axis=1))
    dup = np.zeros((72, P))
    for m in range(P):
        dup[m % 64, m] = 1
    put('dup', dup)
    selp = np.zeros((NB_, NS, 4, 2, H, NS))
    for b in range(NB_):
        for t in range(NS):
            selp[b, t, b // 2, b % 2, :, t] = 1
    put('selp', selp.reshape(TS, -1))
    put('selT', selp.transpose(3, 4, 5, 2, 0, 1).reshape(P, -1))
    hm = np.zeros((2, H, NS, H))
    for h in range(H):
        hm[:, h, :, h] = 1
    put('hmask', hm.reshape(P, H))
    t = np.arange(NS)
    put('newcausal', np.where(t[None, :] <= np.tile(t, NB_)[:, None], 0.0, NEG))
    b = np.repeat(np.arange(NB_), NS)
    put('newblock', np.where(b[:, None] == b[None, :], 0.0, NEG))
    put('bd', (b[:, None] == b[None, :]).astype(np.float32))
    i = np.arange(P)
    put('caus', np.where(i[None, :] <= i[:, None], 0.0, NEG))
    put('rep', (t[:, None] == np.tile(t, NB_)[None, :]).astype(np.float32))
    hot = np.zeros((32, BIASW))
    for x in range(BIASW):
        n = max(255 - x, 0)
        bk = n if n < 16 else min(16 + int(math.log(n / 16) / math.log(128 / 16) * 16), 31)
        hot[bk, x] = 1
    put('bucket', hot)
    return c


def hybrid_kernel(nc, x_prompt, x_sample, cache_k, cache_v, cache_idx_k, state_ffn_conv, page_table, rel_bias,
                  norm_mix_g, w_in, sg_norm_g, sg_w_s, sg_b, w_branch_a, w_branch_b, w_out, norm_ffn_g,
                  w_up, ffn_conv_w, ffn_conv_b, w_down, norm_final_g, consts,
                  y_prompt, y_sample, k_prompt, v_prompt, ik_prompt, conv_prompt,
                  k_sample, v_sample, ik_sample, conv_sample, sgv_sample):
    n_phys = cache_k.shape[1]
    bias_scr = nc.dram_tensor("bias_scratch", (P, H, BIASW), F32, kind="Internal").ap()
    mask_scr = nc.dram_tensor("mask_scratch", (TS, NCOL), F32, kind="Internal").ap()
    sv_scr = nc.dram_tensor("sv_scratch", (R, P, D), F32, kind="Internal").ap()
    side_scr = {k: nc.dram_tensor(f"{k}_scratch", (P, KT, T), F32, kind="Internal").ap() for k in ('ga', 'gb', 'su')}
    x_scr = [nc.dram_tensor(f"x_scratch{i}", (P, KT, T), F32, kind="Internal").ap() for i in range(2)]

    class Singles:
        def __init__(self, banks):
            self.banks, self.fills, self.slots = banks, 0, {}

        def add(self, *name):
            self.slots[name] = (self.fills, self.fills % self.banks, self.fills // self.banks)
            self.fills += 1

    class Pairs:
        def __init__(self):
            self.uses, self.at, self.slots = [0, 0], 0, {}

        def add(self, *name, at=None):
            at = self.at if at is None else at
            self.slots[name] = (at, self.uses[at])
            self.uses[at] += 1
            self.at = 1 - at

    single, pair = Singles(4), Pairs()
    side = ([('sv', c, r) for c in range(4) for r in range(R)] + [('ga', c) for c in range(8)]
            + [('gb', c) for c in range(8)] + [('su', c) for c in range(8)])
    SIDE_B = [(1, 1), (1, 1), (1, 1), (1, 1), (1, 2), (1, 2), (1, 2), (1, 2)]
    two, three = {7: 1, 16: 1}, {4: 1, 10: 1, 16: 1}
    SIDE_V = [two, two, two, three, two, two, three, {4: 1, 10: 1}]
    side_at, todo = {}, list(side)

    def put_side(place, n):
        side_at[place] = [todo.pop(0) for _ in range(n)]

    for h in range(H):
        for i in range(2):
            put_side(('B', h, i), SIDE_B[h][i])
    put_side(('start',), 3)
    for G in range(2):
        put_side(('softmax', G, 0), 1)
        put_side(('softmax', G, 1), 0)
        for b in range(4):
            for kp, n in SIDE_V[4 * G + b].items():
                put_side(('V', G, b, kp), n)
    put_side(('end',), 1)
    assert not todo
    for r in range(R):
        for q in range(2):
            single.add('x', r, q)
    single.add('vec')
    for a in range(2):
        single.add('rms', 0, a)
    for h in range(H):
        single.add('bias', h)
    for m in range(4):
        pair.add('iq', m)
    pair.add('ikw')
    for n in ('iqsw', 'ikd0', 'ikd1', 'ikwT', 'iwrep'):
        single.add(n)
    for r in range(1, 4):
        for h in range(H):
            single.add('ps', r, h)
    for s in range(18):
        if s < 16:
            single.add('t', s)
        if 1 <= s < 17:
            single.add('s1', s - 1)
        if s >= 2 and s % 4 == 2:
            pair.add('ss', s // 4, at=0)
        if s % 2 == 1 and s < 16:
            pair.add('q', s // 2, at=1)
    single.add('s1n')
    pair.add('ssn', at=0)
    for c in range(8):
        pair.add('k', c)
    for r in range(R):
        for q in range(2):
            single.add('kt', r, q)
    for c in range(4):
        for r in range(R):
            pair.add('v', c, r)
    for r in range(4):
        single.add('pl', 0, r)
    for h in range(H + 1):
        if h < H:
            if h + 1 < H:
                for r in range(4):
                    single.add('pl', h + 1, r)
            for tile in side_at['B', h, 0]:
                pair.add(*tile)
        if h:
            single.add('pv', h - 1)
        if h < H:
            for tile in side_at['B', h, 1]:
                pair.add(*tile)
            for r in range(4):
                single.add('pt', h, r)
    for tile in side_at['start',]:
        pair.add(*tile)
    for G in range(2):
        for n in range(64):
            single.add('kp', G, n, 0)
            single.add('kp', G, n, 1)
        for kp in range(NPG):
            pair.add('kl', G, kp, at=kp % 2)
        for i, tile in enumerate(side_at['softmax', G, 0] + side_at['softmax', G, 1]):
            pair.add(*tile, at=(i + 1) % 2)
        for g in range(2):
            for q in range(5):
                single.add('st', G, g, q)
        for b in range(4):
            pair.add('o', G, b, at=0)
            for kp in range(NPG):
                for tile in side_at.get(('V', G, b, kp), ()):
                    pair.add(*tile, at=1)
            single.add('ot', G, b, 0)
            single.add('ot', G, b, 1)
    pair.add(*side[-1], at=1)
    for c in range(8):
        pair.add('wa', c)
    single.add('w', 0)
    single.add('w', 1)
    single.add('bd')
    for g in range(8):
        single.add('sg', g)
        single.add('sgs', g)
    for kind in ('wb', 'out'):
        for c in range(8):
            pair.add(kind, c)
    single.add('state', 0)
    single.add('state', 1)
    for a in range(2):
        single.add('rms', 1, a)
    for f in range(FB):
        pair.add('up', f, 0)
        pair.add('up', f, 1)
    for c in range(8):
        pair.add('dn', c)
    single.add('ho', 0)
    single.add('ho', 1)
    for a in range(2):
        single.add('rms', 2, a)
    for q in range(2):
        for r in range(R):
            single.add('y', r, q)

    NW, NH = 3, 2
    chunks, slot_value, chunk_list = {}, [0] * NW, []

    def add_chunk(name, loads, last_tile):
        n = len(chunk_list)
        slot_value[n % NW] += 16 * loads
        chunks[name] = (n, slot_value[n % NW])
        chunk_list.append((name, last_tile))

    for i in range(2):
        add_chunk(('iq', i), 1, ('iq', 2 * i + 1))
    add_chunk(('ikw',), 2, ('ikw',))
    for k in 'qk':
        for i in range(4):
            add_chunk((k, i), 1, (k, 2 * i + 1))
    for k in ('v', 'sv'):
        for i in range(4):
            add_chunk((k, i), 1, (k, i, R - 1))
    for k in ('ga', 'gb', 'su', 'wa', 'wb', 'out'):
        for i in range(4):
            add_chunk((k, i), 1, (k, 2 * i + 1))
    for f in range(FB):
        add_chunk(('up', f), 2, ('up', f, 1))
    DOWN = [(0, 0), (1, 0), (0, 1), (1, 1)] + [(c, kh) for c in range(2, 8) for kh in range(2)]
    for c, kh in DOWN:
        add_chunk(('dn', c, kh), 1, ('dn', c))

    ctx = ExitStack()
    with ctx:
        def at(name, off, words, dt=F32, rows=P):
            return nc.alloc_sbuf_tensor_at(name, [rows, words], dt, offset=ARENA + 4 * off)

        def blocks(a, n):
            return a.rearrange("p (n c) -> p n c", n=n)

        BLK = KT * T
        o_st, o_vt, o_ones, o_ptab, o_cst = 0, 120, 320, 448, 576
        o_tmp = o_cst + NKEPT
        o_nbr = o_cst + NCONST
        o_w = o_nbr + 272
        o_wh = o_w + 2048 * NW
        o_xh = o_wh + 2048 * NH
        o_xl = o_xh + BLK
        o_x = o_xl + BLK
        o_r1 = o_x + BLK
        o_r2 = o_r1 + 9728
        o_sr = o_r2 + 4608
        o_r3 = o_sr + NCOL
        o_rb = o_r3 + 7424
        o_ikw = o_rb + 2048
        assert ARENA + 4 * (o_ikw + 400) <= 229368
        ST = at("ST", o_st, 120)
        VT = at("VT", o_vt, 200)
        ones = at("ones", o_ones, P)
        PTAB = at("PTAB", o_ptab, NB_ * NPAGES, I32, 1)
        CST = at("CST", o_cst, NCONST)
        NBr = blocks(at("NBr", o_nbr, 272)[:, :], 2)
        W = [at(f"W{i}", o_w + 2048 * i, 2048) for i in range(NW)]
        WL = [at(f"WL{i}", o_w + 2048 * i, 2048, F32R) for i in range(NW)]
        WH = [at(f"WH{i}", o_wh + 2048 * i, 2048, F32R) for i in range(NH)]
        R1 = at("R1", o_r1, 9728)
        R2 = at("R2", o_r2, 4608)
        SR = at("SR", o_sr, NCOL)
        R3 = at("R3", o_r3, 7424)
        RB = at("RB", o_rb, 2048)
        IKWT = blocks(at("IKWT", o_ikw, 360)[:, :], 5)
        IWS = blocks(at("IWS", o_ikw + 360, 40)[:, :], 5)

        class Act:
            def __init__(self, name, hi, lo, n=KT):
                self.whole = blocks(at(name, lo, n * T)[:, :], n)
                self.hi = blocks(at(name + "_hi", hi, n * T, F32R)[:, :], n)
                self.lo = blocks(at(name + "_lo", lo, n * T, F32R)[:, :], n)

            def hi_block(self, k):
                return self.hi[:, k, :]

            def lo_block(self, k):
                return self.lo[:, k, :]

            def whole_block(self, k):
                return self.whole[:, k, :]

        xn1 = Act("xn1", o_xh, o_xl)
        xn2 = Act("xn2", o_xl, o_x)
        oa = Act("oa", o_r1, o_x)
        ob = Act("ob", o_r1, o_r2)
        mg = Act("mg", o_x, o_r3 + 4608)
        GAT = blocks(at("GAT", o_xl, BLK)[:, :], KT)
        GBT = blocks(at("GBT", o_xh, BLK)[:, :], KT)
        xT0 = blocks(at("xT0", o_x, BLK)[:, :], KT)
        xT1 = blocks(at("xT1", o_xh, BLK)[:, :], KT)
        xT2 = blocks(at("xT2", o_xl, BLK)[:, :], KT)
        SQ = [blocks(at(f"SQ{i}", o, BLK)[:, :], KT) for i, o in enumerate((o_xh, o_r1, o_x))]
        YN = SQ[2]
        xT = [xT0, xT1, xT2]
        oaT, obT, mT = oa.whole, ob.whole, mg.whole
        NG = 18
        GA = [[at(f"G{i}{s}", o, 2 * T * n, d) for i, (o, n) in enumerate(((o_r1, NG), (o_xh, FB - NG)))]
              for s, d in (("", F32), ("_hilo", F32R))]
        o_conv = o_r1 + 2 * T * NG
        CV = at("CV", o_conv, 4752)
        RSF = at("RSF", o_conv + 4752, T)
        STH = at("STH", o_tmp, 1496)
        STG = at("STG", o_tmp, 2 * T)
        stage = [STG[:, T * i:T * i + T] for i in range(2)]

        def gated(f, part):
            g, i = (0, f) if f < NG else (1, f - NG)
            return GA[1][g][:, 2 * T * i + T * part:2 * T * i + T * part + T]

        def gated_whole(f):
            g, i = (0, f) if f < NG else (1, f - NG)
            return GA[0][g][:, 2 * T * i + T:2 * T * i + 2 * T]

        def const(name, rows=P):
            o, w = COFF[name]
            return CST[0:rows, o:o + w]

        ident = const('ident')

        XL = blocks(R1[:, 0:5120], 5)
        BV = blocks(R1[:, 5120:8192], H)
        RBB = blocks(R1[0:32, 8192:9216], H)
        VR = blocks(R1[:, 9216:9472], 2)
        RBT = R1[0:32, 9472:9480]
        iqT = blocks(R2[:, 0:2304], 4)
        IKW = R2[:, 2304:2880]
        IKPAD = blocks(R2[:, 2880:3904], 2)
        MS = R3[:, 0:SP_COLS]
        IQB = blocks(R3[:, 1280:1792], 4)
        IQSW = blocks(R3[:, 1792:2048], 4)
        IKN = [R3[:, 2048 + 512 * i:2560 + 512 * i].rearrange("p (j a d) -> p j a d", j=4, a=2) for i in range(4)]
        IKT = [R3[:, 4096 + 512 * i:4608 + 512 * i] for i in range(2)]
        RL = [R3[:, 5120 + 512 * i:5632 + 512 * i] for i in range(2)]
        RL2 = [R3[:, 6144 + 512 * i:6656 + 512 * i] for i in range(2)]
        SWM = blocks(R3[:, 7168:7424], 4)
        IKNEW = blocks(ST[:, 0:32], 4)
        RLN = ST[:, 32:64]
        TMP32 = blocks(ST[:, 64:96], 4)
        IWC = ST[:, 96:100]
        MAX8 = ST[0:TS, 0:8]
        MAX8P = ST[:, 100:108]
        M8 = ST[0:TS, 16:24]
        RS = [SR[:, 0:T], RSF[:, :], RSF[:, :]]
        S = SR[0:TS, :]
        BT = blocks(RB[:, 0:2048], H)
        qT = blocks(R2[:, :], H)
        V = blocks(R1[:, 0:4096], 4)
        kT = blocks(R1[:, 4096:8704], H)
        Vn = R1[:, 8704:9728]
        MB = R3[:, 1280:2560]
        L = [R3[:, 2560 + 1280 * i:3840 + 1280 * i] for i in range(2)]
        PT = blocks(R3[:, 5120:7168], 4)
        KO = [R3[:, 5120 + 1024 * i:6144 + 1024 * i] for i in range(2)]
        ring = [R1[:, 1024 * i:1024 * i + 1024] for i in range(8)]
        LS = blocks(R2[:, 0:2 * NCOL], 2)
        OS = [blocks(R2[:, 256 * i:256 * i + 256], 2) for i in range(2)]
        MG = SR
        QN = blocks(R1[:, 8192:8704], H)
        NBd = [R2[:, 4352:4608], at("NBd1", o_ikw, 256)[:, :]]
        PTs = R3[:, 0:2 * NCOL].rearrange("p (g k c) -> p g k c", g=2, k=NPG)
        QZ = R3[:, 4352:6400].rearrange("p (h b c) -> p h b c", h=H, b=8)
        kTn = blocks(R3[:, 6400:7424], H)
        KTb = [blocks(RB[:, 1024 * i:1024 * i + 1024], H) for i in range(2)]
        SV = blocks(R1[:, 4608:9728], 5)
        SG = R3[:, 0:1024]
        SB = blocks(R3[:, 1024:2048], 8)
        WS = blocks(R3[:, 2048:3072], 8)
        WT = blocks(R3[:, 3072:4096], 8)
        BD = blocks(R3[0:TS, 4096:4608], 8)
        TMPS = [SR[:, 576 * i:576 * i + 576] for i in range(2)]
        JUNK = SR[:, 1152:2176]
        HPb = [[CV[:, 594 * (2 * i + k):594 * (2 * i + k) + 594] for k in range(2)] for i in range(2)]
        CB = [[CV[:, 2376 + 592 * (2 * i + k):2968 + 592 * (2 * i + k)] for k in range(2)] for i in range(2)]
        SRAW = blocks(R1[:, 5760:6528], 6)
        STT_ = STH[:, 0:704]
        HCP = STH[:, 704:792]
        HCS = STH[:, 792:1496]
        CO = blocks(RB[:, 0:896], 7)
        YO = blocks(R1[:, 0:1024 * R], R)
        MX = [ST[:, 24 + 16 * i:28 + 16 * i] for i in range(2)]
        NM = [ST[:, 28 + 16 * i:32 + 16 * i] for i in range(2)]
        SU = [ST[:, 32 + 16 * i:36 + 16 * i] for i in range(2)]
        RC = [ST[:, 36 + 16 * i:40 + 16 * i] for i in range(2)]
        SS = ST[:, 60:65]
        EARLY = ST[:, 112:114]

        PS = ctx.enter_context(nc.psum_tensor("PS", [P, 8, 512], F32))

        sems = {}

        def S_(name):
            if name not in sems:
                sems[name] = ctx.enter_context(nc.semaphore(name))
            return sems[name]

        single_filled = S_("single_filled")
        pair_filled = [S_(f"pair_filled{i}") for i in range(2)]
        single_drained = [S_(f"single_drained{i}") for i in range(4)]
        pair_drained = [S_(f"pair_drained{i}") for i in range(2)]
        weights_in = [S_(f"weights_in{i}") for i in range(NW)]
        idx_in = [[S_(f"idx_pages_in{a}_{i}") for i in range(4)] for a in range(2)]
        page_in = [S_(f"page_in{i}") for i in range(8)]
        block = ctx.enter_context(nc.Block())

        def bank(*n):
            return PS[:, 4 + single.slots[n][1], :]

        def pbank(*n):
            return PS[:, 2 * pair.slots[n][0]:2 * pair.slots[n][0] + 2, :]

        def ptile(*n):
            return pbank(*n)[:, :, 0:HALF]

        def halves(a):
            return a.rearrange("p (a t) -> p a t", a=2)

        def filled(e, *n):
            if n in single.slots:
                e.wait_ge(single_filled, single.slots[n][0] + 1)
            else:
                at, use = pair.slots[n]
                e.wait_ge(pair_filled[at], use + 1)

        def drained(e, *n):
            if n in single.slots:
                e.wait_ge(single_drained[single.slots[n][1]], single.slots[n][2] + 1)
            else:
                at, use = pair.slots[n]
                e.wait_ge(pair_drained[at], use + 1)

        def claim(e, *n):
            if n in single.slots:
                _, k, use = single.slots[n]
                if use:
                    e.wait_ge(single_drained[k], use)
            else:
                k, use = pair.slots[n]
                if use:
                    e.wait_ge(pair_drained[k], use)

        def drains(*n):
            return single_drained[single.slots[n][1]] if n in single.slots else pair_drained[pair.slots[n][0]]

        def width(r):
            return P if r < 4 else TS

        def chunk_used(e, n):
            name, last_tile = chunk_list[n]
            if name[0] == 'dn' and name[2] == 0:
                e.wait_ge(S_("down_halves"), name[1] + 1)
            else:
                filled(e, *last_tile)

        def page_freed(e, seq):
            if seq < 8:
                if seq == 0:
                    filled(e, 'pv', H - 1)
                    e.wait_ge(S_("v_stored"), 32)
                if seq == 4:
                    e.wait_ge(S_("ring_free"), 1)
                return
            G, kind, n = (seq - 8) // 128, (seq - 8) // 64 % 2, (seq - 8) % 64
            if kind == 0:
                e.wait_ge(single_filled, single.slots['kp', G, n, 1][0] + 1)
            else:
                e.wait_ge(S_("v_pages_used"), 64 * G + n + 1)

        def next_chunk(tile):
            n = chunk_of(tile)
            return chunk_list[n + NW][0] if chunk_list[n][1] == tile else None

        def chunk_of(tile):
            return chunks[(tile[0], tile[1])][0] if tile[0] == 'sv' else chunks[(tile[0], tile[1] // 2)][0]

        def chunk_words(name):
            return {'ikw': 72 * KT, 'dn': 11 * P}.get(name[0], 256 * KT)

        POOL_SPLITS = ('k', 'v', 'sv')
        low_count, counts = {}, [0, 0]
        for name, _ in chunk_list:
            on_pool = name[0] in POOL_SPLITS
            counts[on_pool] += 1
            low_count[name] = (S_("low_ready_pool" if on_pool else "low_ready"), counts[on_pool])

        def split_low(e, *name):
            n, c = chunks[name][0], chunk_words(name)
            e.wait_ge(S_("high_ready"), n + 1)
            e.tensor_tensor(WL[n % NW][:, 0:c], W[n % NW][:, 0:c], WH[n % NH][:, 0:c].bitcast(F32),
                            ALU.subtract).then_inc(low_count[name][0], 1)

        def down_splits(c):
            return (4 + c,) if c < 2 else (2 * c + 2, 2 * c + 3) if c < 7 else ()

        def split_after(split):
            first, seen = {}, set()
            for n, (name, tile) in enumerate(chunk_list):
                kind = name[0]
                if kind == 'dn':
                    continue
                elif kind in ('v', 'sv'):
                    t = (kind, name[1], 0)
                elif kind == 'up':
                    t = (kind, name[1], 0)
                elif kind == 'ikw':
                    t = name
                else:
                    t = (kind, 2 * name[1])
                first.setdefault(t, []).append(n)

            def after(*tile):
                for n in first.get(tile, ()):
                    if n + 1 < len(chunk_list):
                        split(*chunk_list[n + 1][0])
            return after

        def page_id(e, b, kp):
            return e.value_load(PTAB[0:1, b * NPAGES + kp:b * NPAGES + kp + 1], min_val=0, max_val=n_phys - 1)

        def idx_pages(e, s, a):
            kc, p = s // 4, s % 4
            for j in range(4):
                v = page_id(e, 2 * p + a, 4 * kc + j)
                e.dma_start(IKN[s % 4][:, j, a, :], cache_idx_k[0, bass.ds(v, 1), :, :].rearrange("o p d -> (o p) d"))\
                    .then_inc(idx_in[a][s % 4], 16)

        @block.sync
        def _(sp):
            w_in_v = w_in[0].rearrange("(k p) n -> p k n", p=P)

            def load_chunk(name):
                n = chunks[name][0]
                slot = n % NW
                if n >= NW:
                    chunk_used(sp, n - NW)
                kind, i = name[0], (name[1] if len(name) > 1 else 0)
                dst = blocks(W[slot][:, :], KT)
                if kind in ('iq', 'q', 'k', 'v', 'sv', 'su', 'gb', 'ga'):
                    c = COL[kind] + 256 * i
                    sp.dma_start(dst, w_in_v[:, :, c:c + 256]).then_inc(weights_in[slot], 16)
                elif kind == 'ikw':
                    d = W[slot][:, 0:576].rearrange("p (k c) -> p k c", k=KT)
                    sp.dma_start(d[:, :, 0:64], w_in_v[:, :, COL['ik']:COL['ik'] + 64]).then_inc(weights_in[slot], 16)
                    sp.dma_start(d[:, :, 64:72], w_in_v[:, :, COL['iw']:COL['iw'] + 8]).then_inc(weights_in[slot], 16)
                elif kind in ('wb', 'wa', 'out'):
                    m = {'wb': w_branch_b, 'wa': w_branch_a, 'out': w_out}[kind]
                    sp.dma_start(dst, m[0].rearrange("(k p) n -> p k n", p=P)[:, :, 256 * i:256 * i + 256])\
                        .then_inc(weights_in[slot], 16)
                elif kind == 'up':
                    u = w_up[0].rearrange("(k p) n -> p k n", p=P)
                    for a in range(2):
                        sp.dma_start(dst[:, :, 128 * a:128 * a + 128], u[:, :, FF * a + P * i:FF * a + P * i + P])\
                            .then_inc(weights_in[slot], 16)
                else:
                    c, kh = name[1:]
                    u = w_down[0].rearrange("(k p) n -> p k n", p=P)
                    sp.dma_start(blocks(W[slot][:, 0:1408], 11), u[:, 11 * kh:11 * kh + 11, P * c:P * c + P])\
                        .then_inc(weights_in[slot], 16)

            sp.dma_start(CST[:, 0:NKEPT], consts[:, 0:NKEPT]).then_inc(S_("ident_in"), 16)
            for r in range(R):
                src = x_prompt[0, P * r:P * r + P, :] if r < 4 else x_sample.rearrange("b s d -> (b s) d")
                sp.dma_start(XL[0:width(r), r, :], src).then_inc(S_(f"x_in{r}"), 16)
            sp.dma_start(CST[:, NKEPT:NCONST], consts[:, NKEPT:NCONST]).then_inc(S_("consts_in"), 16)
            for i, g in enumerate((norm_mix_g[0], norm_ffn_g[0], norm_final_g)):
                sp.dma_start(VR[8 * i:8 * i + 8, 0, :], g.rearrange("(k c) -> k c", k=8)).then_inc(S_("vec_in"), 16)
            cw = ffn_conv_w[0].rearrange("j (f c) -> (j f) c", c=P)
            sp.dma_start(VR[24:128, 0, :], cw[0:104, :]).then_inc(S_("vec_in"), 16)
            sp.dma_start(VR[0:28, 1, :], cw[104:132, :]).then_inc(S_("vec_in"), 16)
            sp.dma_start(VR[28:72, 1, :], ffn_conv_b[0].rearrange("(f c) -> f c", c=P)).then_inc(S_("vec_in"), 16)
            sp.dma_start(RBT, rel_bias).then_inc(S_("rb_in"), 16)
            sp.dma_start(PTAB[:, :], page_table.rearrange("(o b) n -> o (b n)", o=1)).then_inc(S_("table_in"), 16)
            for name in (('iq', 0), ('iq', 1), ('ikw',)):
                load_chunk(name)
            sp.wait_ge(S_("table_in"), 16)

            for s in range(16):
                if s >= 4:
                    for name in {4: [('q', 0), ('q', 1), ('q', 2)], 8: [('q', 3)], 12: [('k', 0)]}.get(s, ()):
                        load_chunk(name)
                    filled(sp, 't', s - 4)
                idx_pages(sp, s, 0)
                if s == 7:
                    for r in range(R):
                        for q in range(2):
                            drained(sp, 'x', r, q)
                    sp.dma_start(x_scr[0], xT0).then_inc(S_("x_out"), 16)
            for k in ('k', 'v', 'sv'):
                for i in range(4):
                    if (k, i) != ('k', 0) and (k, i) != ('sv', 3):
                        load_chunk((k, i))

            def side_loads(*place):
                for tile in side_at.get(place, ()):
                    name = next_chunk(tile)
                    if name:
                        load_chunk(name)

            for h in range(H):
                for i in range(2):
                    side_loads('B', h, i)

            def load_page(seq):
                if seq >= 256:
                    return
                G, kind, n = seq // 128, seq // 64 % 2, seq % 64
                b, kp = (4 * G + n % 4, n // 4) if kind == 0 else (4 * G + n // 16, n % 16)
                page_freed(sp, seq)
                v = page_id(sp, b, kp)
                sp.dma_start(ring[seq % 8], (cache_k, cache_v)[kind][0, bass.ds(v, 1)]
                             .rearrange("o p h d -> (o p) (h d)")).then_inc(page_in[seq % 8], 16)

            side_loads('start')
            for seq in range(4):
                load_page(seq)
            sp.wait_ge(S_("sample_mask"), 1)
            sp.dma_start(mask_scr, S).then_inc(S_("mask_out"), 16)
            sp.wait_ge(S_("mask_out"), 16)
            for j in range(4):
                sp.dma_start(MG[32 * j:32 * j + 32, :], mask_scr[0:32, :]).then_inc(S_("mask_in0"), 16)
            for seq in range(4, 8):
                load_page(seq)
            for G in range(2):
                for n in range(64):
                    load_page(128 * G + n + 8)
                side_loads('softmax', G, 0)
                side_loads('softmax', G, 1)
                for b in range(4):
                    for kp in range(NPG):
                        if kp < NPAGES:
                            load_page(128 * G + 64 + 16 * b + kp + 8)
                        side_loads('V', G, b, kp)

            side_loads('end')
            filled(sp, *side[-1])
            for i in range(2):
                sp.wait_ge(S_(f"side_stored{i}"), 16 * len(side) // 2)
            for i in range(4):
                sp.dma_start(GAT[:, 2 * i:2 * i + 2, :], side_scr['ga'][:, 2 * i:2 * i + 2, :])\
                    .then_inc(S_(f"ga_back{i}"), 16)
            filled(sp, 'ot', 1, 3, 1)
            sp.dma_start(SV[:, 0:4, :], sv_scr[0:4].rearrange("r p c -> p r c")).then_inc(S_("sv_back"), 16)
            sp.dma_start(SV[0:TS, 4, :], sv_scr[4, 0:TS, :]).then_inc(S_("sv_back"), 16)
            sp.dma_start(SG, bass.AP(sg_norm_g.tensor, 0, [[0, P], [1, 1024]])).then_inc(S_("sg_in"), 16)
            sp.dma_start(SB, bass.AP(sg_b.tensor, 0, [[0, P], [1, 1024]]).rearrange("p (g t) -> p g t", g=8))\
                .then_inc(S_("sg_in"), 16)
            sp.dma_start(WS, sg_w_s[0].rearrange("g t s -> t g s")).then_inc(S_("ws_in"), 16)
            sp.dma_start(obT, side_scr['su']).then_inc(S_("su_back"), 16)
            load_chunk(('wa', 3))
            sp.dma_start(GBT, side_scr['gb']).then_inc(S_("gb_back"), 16)
            for i in range(4):
                load_chunk(('wb', i))
            for i in range(4):
                drained(sp, 'wb', 2 * i)
                drained(sp, 'wb', 2 * i + 1)
                sp.dma_start(xT1[:, 2 * i:2 * i + 2, :], x_scr[0][:, 2 * i:2 * i + 2, :])\
                    .then_inc(S_(f"x_back{i}"), 16)
                if i < 2:
                    load_chunk(('out', i))
            filled(sp, 'wb', 7)
            raw = state_ffn_conv[0].rearrange("b w (f c) -> (b w f) c", c=P)
            sp.dma_start(SRAW[:, 0:5, :], raw[0:640, :].rearrange("(r p) c -> p r c", p=P)).then_inc(S_("state_in"), 16)
            sp.dma_start(SRAW[0:64, 5, :], raw[640:704, :]).then_inc(S_("state_in"), 16)
            for i in (2, 3):
                load_chunk(('out', i))
            for f in range(FB):
                load_chunk(('up', f))
                if f == 2:
                    drained(sp, 'out', 7)
                    drained(sp, 'out', 6)
                    sp.dma_start(x_scr[1], xT1).then_inc(S_("x_out"), 16)
            for c, kh in DOWN[:2]:
                load_chunk(('dn', c, kh))
            filled(sp, 'up', FB - 1, 1)
            sp.dma_start(xT2, x_scr[1]).then_inc(S_("x_back_ffn"), 16)
            for c, kh in DOWN[2:]:
                load_chunk(('dn', c, kh))
            sp.wait_ge(S_("conv_rows"), 1)
            filled(sp, 'ho', 1)
            drained(sp, 'ho', 1)
            sp.dma_start(conv_prompt[0].rearrange("o w (f c) -> (o w f) c", c=P), CO[0:88, 0, :])\
                .then_inc(S_("stored_sp"), 16)
            cs = conv_sample[0].rearrange("b w (f c) -> (b w f) c", c=P)
            sp.dma_start(cs[0:640, :].rearrange("(r p) c -> p r c", p=P), CO[:, 1:6, :]).then_inc(S_("stored_sp"), 16)
            sp.dma_start(cs[640:704, :], CO[0:64, 6, :]).then_inc(S_("stored_sp"), 16)
            for r in range(R):
                drained(sp, 'y', r, 0)
                drained(sp, 'y', r, 1)
                dst = y_prompt[0, P * r:P * r + P, :] if r < 4 else y_sample.rearrange("b s d -> (b s) d")
                sp.dma_start(dst, YO[0:width(r), r, :]).then_inc(S_("y_stored"), 16)
            sp.wait_ge(S_("stored_sp"), 48)
            sp.wait_ge(S_("y_stored"), 16 * R)

        @block.gpsimd
        def _(pool):
            steps = [0]

            def link(ins):
                steps[0] += 1
                ins.then_inc(S_("pool_step"), 1)
                pool.wait_ge(S_("pool_step"), steps[0])

            link(pool.memset(IKPAD[64:128, 0, :], 0.0))
            link(pool.memset(IKPAD[0:64, 1, :], 0.0))
            link(pool.memset(IQB[:, :, :], 0.0))
            pool.memset(ones[:, :], 1.0).then_inc(S_("ones_set"), 1)
            pool.wait_ge(S_("ones_set"), 1)
            pool.wait_ge(S_("rb_in"), 16)
            pool.tensor_copy(RBB, RBT[:, :, None].broadcast_to([32, H, P])).then_inc(S_("rbb_set"), 1)
            pool.wait_ge(S_("rbb_set"), 1)
            pool.wait_ge(S_("x_in4"), 16)
            pool.wait_ge(S_("table_in"), 16)
            for s in range(4):
                idx_pages(pool, s, 1)
            drained(pool, 'bias', H - 1)
            link(pool.memset(Vn[64:128, :], 0.0))
            pool.dma_start(bias_scr, BV).then_inc(S_("bias_out"), 16)
            pool.wait_ge(S_("bias_out"), 16)
            pool.dma_start(BT, bass.AP(bias_scr.tensor, 127, [[H * BIASW - 1, P], [BIASW, H], [1, 256]]))\
                .then_inc(S_("bt_in"), 16)
            for g in range(2):
                for j in range(4):
                    for b in range(4):
                        pool.dma_start(NBr[32 * j + 8 * b:32 * j + 8 * b + 8, g, :],
                                       bass.AP(bias_scr.tensor, 127 + (4 * g + j) * BIASW,
                                               [[H * BIASW - 1, 8], [1, 136]])).then_inc(S_("nbr_in"), 16)
            drained(pool, 'ikw')
            drained(pool, 'iqsw')
            for a in range(2):
                rows = slice(64 * a, 64 * a + 64)
                d = IQB[rows, :, 64 * a:64 * a + 64].rearrange("p q (m e t) -> p q m e t", m=4, e=2)
                o = iqT[rows, :, TP:T].rearrange("p m (q u t) -> p q m u t", q=4, u=2)[:, :, :, a, :]
                w = IQSW[rows, :, :].rearrange("p m (q u t) -> p q m u t", q=4, u=2)[:, :, :, a, :]
                link(pool.tensor_copy(d[:, :, :, a, :], o))
                link(pool.tensor_copy(d[:, :, :, 1 - a, :], w))
            pool.memset(ST[:, 110:111], 0.0).then_inc(S_("iqb_ready"), 1)
            pool.wait_ge(S_("iw_ready"), 1)
            pool.dma_start(ik_prompt[0, 0].rearrange("(r p) d -> p r d", p=P), IKWT[:, 0:4, 0:64])\
                .then_inc(S_("stored_pool"), 16)
            pool.dma_start(ik_sample[0].rearrange("b s d -> (b s) d"), IKWT[0:TS, 4, 0:64])\
                .then_inc(S_("stored_pool"), 16)
            for s in range(4, 16):
                filled(pool, 't', s - 4)
                idx_pages(pool, s, 1)
            for i in range(4):
                split_low(pool, 'k', i)
            split_low(pool, 'v', 0)
            for r in range(R):
                drained(pool, 'kt', r, 1)
                drained(pool, 'kt', r, 0)
                dst = (k_prompt[0, 0, P * r:P * r + P].rearrange("p h d -> p (h d)") if r < 4
                       else k_sample[0].rearrange("b s h d -> (b s) (h d)"))
                pool.dma_start(dst, KO[r % 2][0:width(r), :]).then_inc(S_(f"k_stored{r % 2}"), 16)
            def bias_mask(h):
                if h:
                    drained(pool, 'pl', h - 1, 3)
                pool.tensor_tensor(MB[:, 0:128], MS[:, 0:128], BT[:, h, 128:256], ALU.add)
                for r in range(1, 4):
                    o = SP_OFF[r] + P * (r - 1)
                    if r > 1:
                        pool.tensor_scalar(MB[:, SP_OFF[r]:o], MS[:, SP_OFF[r]:o], BT[:, h, 0:1], None, ALU.add)
                    last = pool.tensor_tensor(MB[:, o:o + 256], MS[:, o:o + 256], BT[:, h, :], ALU.add)
                last.then_inc(S_("bias_mask_ready"), 1)

            pool.wait_ge(S_("prompt_mask"), 3)
            pool.wait_ge(S_("bt_in"), 16)
            bias_mask(0)
            for i in range(1, 4):
                split_low(pool, 'v', i)
            drained(pool, 'v', 3, 4)
            pool.dma_start(v_prompt[0, 0].rearrange("(r p) h d -> p r (h d)", p=P), V).then_inc(S_("v_stored"), 16)
            pool.dma_start(v_sample[0].rearrange("b s h d -> (b s) (h d)"), Vn[0:TS, :]).then_inc(S_("v_stored"), 16)
            split_low(pool, 'sv', 0)
            for h in range(1, H):
                bias_mask(h)
                if h % 2 and h < 7:
                    split_low(pool, 'sv', (h + 1) // 2)

            filled(pool, 'pv', H - 1)
            drained(pool, 'pv', H - 1)
            pool.wait_ge(S_("k_stored0"), 48)
            pool.wait_ge(S_("k_stored1"), 32)
            link(pool.memset(kTn[:, :, TS:P], 0.0))
            link(pool.tensor_copy(kTn[:, :, 0:TS], kT[:, :, TP:T]))
            link(pool.tensor_copy(QN, qT[:, :, TP:T]))
            pool.memset(ST[0:1, 110:111], 0.0).then_inc(S_("ring_free"), 1)
            link(pool.memset(QZ, 0.0))
            for b in range(NB_):
                c = b % 4
                last = pool.tensor_copy(QZ[:, :, b, 8 * c:8 * c + 8], qT[:, :, TP + 8 * b:TP + 8 * b + 8])
            last.then_inc(S_("sample_queries"), 1)
            pool.wait_ge(S_("sample_queries"), 1)
            pool.wait_ge(S_("nbr_in"), 16 * 32)
            pool.wait_ge(S_("stored_pool"), 32)
            for g in range(2):
                pool.tensor_scalar(NBd[g][:, 0:128], NBr[:, g, 0:128], NBr[:, g, 0:1], None, ALU.subtract)
                pool.tensor_scalar(NBd[g][:, 128:192].rearrange("p (b t) -> p b t", b=8),
                                   NBr[:, g, None, 128:136].broadcast_to([P, 8, 8]), NBr[:, g, 0:1], None,
                                   ALU.subtract)
                pool.memset(NBd[g][:, 192:256], 0.0).then_inc(S_("new_bias"), 1)
            drained(pool, 'kl', 0, NPG - 1)
            for j in range(4):
                pool.dma_start(MG[32 * j:32 * j + 32, :], mask_scr[32:64, :]).then_inc(S_("mask_in1"), 16)

            pool.wait_ge(S_("ws_in"), 16)
            pool.affine_select(out=WS, in_=WS, pattern=[[0, 8], [-1, P]], compare_op=ALU.is_ge, fill=0.0,
                               base=0, channel_multiplier=1).then_inc(S_("ws_causal"), 1)
            pool.wait_ge(S_("sv_normed"), 1)
            pool.dma_start(sgv_sample[0].rearrange("b s d -> (b s) d"), SV[0:TS, 4, :]).then_inc(S_("stored_pool"), 16)
            pool.wait_ge(S_("su_back"), 16)
            for g in range(8):
                drained(pool, 'sgs', g)
                pool.tensor_tensor(obT[:, g, :], obT[:, g, :], TMPS[g % 2], ALU.mult).then_inc(S_("ob_whole"), 1)
            for c in range(8):
                drained(pool, 'wb', c)
                pool.tensor_tensor(mT[:, c, :], mT[:, c, :], TMPS[c % 2], ALU.add)\
                    .then_inc(S_("merged"), 1)
            def squares_sum(i):
                for k in range(1, 7):
                    pool.wait_ge(S_("squares_act"), (0, 4, 12)[i] + k + 1)
                    pool.tensor_tensor(SQ[i][:, 0, :], SQ[i][:, 0, :], SQ[i][:, k, :], ALU.add)\
                        .then_inc(S_("squares_summed"), 1)
                    pool.wait_ge(S_("squares_summed"), 6 * i - 6 + k)

            squares_sum(1)
            filled(pool, 'rms', 1, 1)
            pool.wait_ge(S_("stored_pool"), 48)
            for i in range(2):
                for k in range(2):
                    link(pool.memset(HPb[i][k][:, 0:2], 0.0))
            drained(pool, 'state', 1)
            for f in range(FB):
                for k in range(2):
                    fb = FB * k + f
                    hp = HPb[f % 2][k]
                    smp = hp[:, 514:594].rearrange("p (b c) -> p b c", b=8)
                    if f >= 2:
                        pool.wait_ge(S_("act_whole"), f - 1)
                    pool.tensor_copy(smp[:, :, 0:2],
                                     STT_.rearrange("p (b w f) -> p b w f", b=8, w=2)[:, :, :, fb])\
                        .then_inc(S_("state_put"), 1)
                for k in range(2):
                    fb = FB * k + f
                    hp = HPb[f % 2][k]
                    smp = hp[:, 514:594].rearrange("p (b c) -> p b c", b=8)
                    drained(pool, 'up', f, k)
                    pool.tensor_copy(HCP.rearrange("p (w f) -> p w f", w=2)[:, :, fb], hp[:, 512:514])
                    last = pool.tensor_copy(HCS.rearrange("p (b w f) -> p b w f", b=8, w=2)[:, :, :, fb],
                                            smp[:, :, 8:10])
                last.then_inc(S_("conv_rows"), 1)
            squares_sum(2)

        @block.tensor
        def _(pe):
            def done(ins, *n):
                ins.then_inc(single_filled if n in single.slots else pair_filled[pair.slots[n][0]], 1)

            def split(name, width, nk=KT):
                n = chunks[name][0]
                pe.wait_ge(*low_count[name])
                return (blocks(WH[n % NH][:, 0:nk * width], nk), blocks(WL[n % NW][:, 0:nk * width], nk))

            def products(out, wts, cols, x, k, n, tokens, first, last):
                hi, lo = wts
                pe.matmul(out, hi[:, k, cols], x.hi_block(n)[:, tokens], start=first, stop=False)
                pe.matmul(out, hi[:, k, cols], x.lo_block(n)[:, tokens], start=False, stop=False)
                return pe.matmul(out, lo[:, k, cols], x.hi_block(n)[:, tokens], start=False, stop=last)

            def project3(name, wts, cols, x, ready=None):
                claim(pe, *name)
                m = cols.stop - cols.start
                for a in range(2):
                    for k in range(KT):
                        if ready and a == 0:
                            ready(k)
                        last = products(ptile(*name)[0:m, a, :], wts, cols, x, k, k,
                                        slice(HALF * a, HALF * a + HALF), k == 0, k == KT - 1)
                done(last, *name)

            def column(c):
                return slice(P * (c % 2), P * (c % 2) + P)

            def rms_sum(i, k):
                if i and k == 0:
                    pe.wait_ge(S_("squares_summed"), 6 * i)
                elif i or k < 4:
                    pe.wait_ge(S_("squares_act"), (0, 4, 12)[i] + k + 1)
                else:
                    pe.wait_ge(S_("squares_dve"), k - 3)
                for a in range(2):
                    if k == 0:
                        claim(pe, 'rms', i, a)
                    last = pe.matmul(bank('rms', i, a)[:, 0:HALF], ones[:, :], SQ[i][:, k, HALF * a:HALF * a + HALF],
                                     start=(k == 0), stop=(k == KT - 1))
                    if k == KT - 1:
                        done(last, 'rms', i, a)

            def row_tile(kind, c, r):
                hi, lo = split((kind, c), 256)
                claim(pe, kind, c, r)
                out, t = pbank(kind, c, r)[0:width(r), 0, 0:256], slice(P * r, P * r + width(r))
                for k in range(KT):
                    pe.matmul(out, xn1.hi_block(k)[:, t], hi[:, k, :], start=(k == 0), stop=False)
                    pe.matmul(out, xn1.hi_block(k)[:, t], lo[:, k, :], start=False, stop=False)
                    last = pe.matmul(out, xn1.lo_block(k)[:, t], hi[:, k, :], start=False, stop=(k == KT - 1))
                done(last, kind, c, r)

            def column_tile(kind, c):
                project3((kind, c), split((kind, c // 2), 256), column(c), xn1)

            def sides(*place):
                for tile in side_at.get(place, ()):
                    (row_tile if tile[0] == 'sv' else column_tile)(*tile)

            pe.wait_ge(S_("ident_in"), 16)
            for r in range(R):
                pe.wait_ge(S_(f"x_in{r}"), 16)
                for q in range(2):
                    claim(pe, 'x', r, q)
                    w = width(r)
                    for i in range(4):
                        last = pe.transpose(bank('x', r, q)[:, P * i:P * i + w],
                                            XL[0:w, r, P * (4 * q + i):P * (4 * q + i) + P], ident[0:w, 0:w])
                    done(last, 'x', r, q)
            pe.wait_ge(S_("vec_in"), 96)
            claim(pe, 'vec')
            pe.transpose(bank('vec')[:, 0:128], VR[:, 0, :], ident)
            done(pe.transpose(bank('vec')[:, 128:200], VR[0:72, 1, :], ident[0:72, 0:72]), 'vec')
            pe.wait_ge(S_("ones_set"), 1)
            for k in range(KT):
                rms_sum(0, k)
            pe.wait_ge(S_("rbb_set"), 1)
            pe.wait_ge(S_("consts_in"), 16)
            for h in range(H):
                claim(pe, 'bias', h)
                done(pe.matmul(bank('bias', h)[:, 0:BIASW], RBB[:, h, :], const('bucket', 32), start=True, stop=True),
                     'bias', h)
            for m in range(4):
                project3(('iq', m), split(('iq', m // 2), 256), column(m), xn1,
                         (lambda k: pe.wait_ge(S_("xn_ready"), k + 1)) if m == 0 else None)
            project3(('ikw',), split(('ikw',), 72), slice(0, 72), xn1)
            drained(pe, 'iq', 3)
            claim(pe, 'iqsw')
            for m in range(4):
                last = pe.matmul(bank('iqsw')[:, 64 * m:64 * m + 64], const('swap'), iqT[:, m, TP:T],
                                 start=True, stop=True)
            done(last, 'iqsw')
            drained(pe, 'ikw')
            for i, (a, b) in enumerate(((0, TP), (TP, T))):
                claim(pe, f'ikd{i}')
                done(pe.matmul(bank(f'ikd{i}')[:, 0:b - a], const('dup', 72), IKW[0:72, a:b], start=True, stop=True),
                     f'ikd{i}')
            claim(pe, 'ikwT')
            for r in range(R):
                last = pe.transpose(bank('ikwT')[0:width(r), 72 * r:72 * r + 72],
                                    IKW[0:72, P * r:P * r + width(r)], ident[0:72, 0:72])
            done(last, 'ikwT')
            pe.wait_ge(S_("iw_ready"), 1)
            claim(pe, 'iwrep')
            for p in range(4):
                last = pe.matmul(bank('iwrep')[:, 8 * p:8 * p + 8], const('selp', TS)[:, P * p:P * p + P],
                                 IWS[0:TS, 4, :], start=True, stop=True)
            done(last, 'iwrep')
            drained(pe, 'ikd0')
            for r in range(1, 4):
                for h in range(H):
                    claim(pe, 'ps', r, h)
                    done(pe.matmul(bank('ps', r, h)[:, 0:P * (r + 1)], iqT[:, h // 2, P * r:P * r + P],
                                   IKPAD[:, h % 2, 0:P * (r + 1)], start=True, stop=True), 'ps', r, h)
            pe.wait_ge(S_("iqb_ready"), 1)
            pe.wait_ge(S_("swm_ready"), 1)
            for s in range(18):
                if s < 16:
                    for a in range(2):
                        pe.wait_ge(idx_in[a][s % 4], 64 * (s // 4 + 1))
                    claim(pe, 't', s)
                    for j in range(4):
                        last = pe.transpose(bank('t', s)[:, P * j:P * j + P],
                                            IKN[s % 4][:, j, :, :].rearrange("p a d -> p (a d)"), ident)
                    done(last, 't', s)
                if 1 <= s < 17:
                    drained(pe, 't', s - 1)
                    claim(pe, 's1', s - 1)
                    done(pe.matmul(bank('s1', s - 1), IQB[:, (s - 1) % 4, :], IKT[(s - 1) % 2], start=True, stop=True),
                         's1', s - 1)
                if s >= 2:
                    kc, p = (s - 2) // 4, (s - 2) % 4
                    drained(pe, 's1', s - 2)
                    if p == 0:
                        claim(pe, 'ss', kc)
                    last = pe.matmul(pbank('ss', kc)[0:TS, 0, :], SWM[:, p, :], RL2[(s - 2) % 2],
                                     start=(p == 0), stop=(p == 3))
                    if p == 3:
                        done(last, 'ss', kc)
                    else:
                        last.then_inc(S_("heads_summed"), 1)
                if s % 2 == 1 and s < 16:
                    column_tile('q', s // 2)
            drained(pe, 'ikd1')
            claim(pe, 's1n')
            for p in range(4):
                last = pe.matmul(bank('s1n')[:, 8 * p:8 * p + 8], IQB[:, p, :], IKNEW[:, p, :], start=True, stop=True)
            done(last, 's1n')
            drained(pe, 's1n')
            claim(pe, 'ssn')
            for p in range(4):
                last = pe.matmul(pbank('ssn')[0:TS, 0, 0:8], SWM[:, p, :], RLN[:, 8 * p:8 * p + 8],
                                 start=(p == 0), stop=(p == 3))
            done(last, 'ssn')

            for c in range(8):
                column_tile('k', c)
            drained(pe, 'k', 7)
            for r in range(R):
                for q in range(2):
                    claim(pe, 'kt', r, q)
                    for i in range(4):
                        last = pe.transpose(bank('kt', r, q)[0:width(r), P * i:P * i + P],
                                            kT[:, 4 * q + i, P * r:P * r + width(r)], ident)
                    done(last, 'kt', r, q)
            def prompt_logits(h):
                for r in range(4):
                    claim(pe, 'pl', h, r)
                    done(pe.matmul(bank('pl', h, r)[:, 0:P * (r + 1)], qT[:, h, P * r:P * r + P],
                                   kT[:, h, 0:P * (r + 1)], start=True, stop=True), 'pl', h, r)

            for c in range(4):
                if c == 3:
                    prompt_logits(0)
                for r in range(R):
                    row_tile('v', c, r)
            drained(pe, 'v', 3, 4)
            for h in range(H + 1):
                if h < H:
                    if h + 1 < H:
                        prompt_logits(h + 1)
                    sides('B', h, 0)
                if h:
                    drained(pe, 'pt', h - 1, 3)
                    claim(pe, 'pv', h - 1)
                    for s in range(4):
                        last = pe.matmul(bank('pv', h - 1)[:, P * s:TP], V[:, s, HD * (h - 1):HD * h],
                                         PT[:, s, P * s:TP], start=(s == 0), stop=(s == 3), skip_group_check=True)
                    done(last, 'pv', h - 1)
                if h < H:
                    sides('B', h, 1)
                    for r in range(4):
                        pe.wait_ge(S_("probs_ready"), 4 * h + r + 1)
                        claim(pe, 'pt', h, r)
                        for s in range(r + 1):
                            last = pe.transpose(bank('pt', h, r)[:, P * s:P * s + P],
                                                L[h % 2][:, SP_OFF[r] + P * s:SP_OFF[r] + P * s + P], ident)
                        done(last, 'pt', h, r)

            sides('start')
            for G in range(2):
                for n in range(65):
                    if n < 64:
                        seq = 128 * G + n
                        pe.wait_ge(page_in[seq % 8], 16 * (seq // 8 + 1))
                        for u in range(2):
                            claim(pe, 'kp', G, n, u)
                            for i in range(4):
                                h = 4 * u + i
                                last = pe.transpose(bank('kp', G, n, u)[:, P * i:P * i + P],
                                                    ring[seq % 8][:, HD * h:HD * h + HD], ident)
                            done(last, 'kp', G, n, u)
                    if (G, n) == (0, 1):
                        pe.wait_ge(S_("sample_queries"), 1)
                    if n:
                        kp, bb = (n - 1) // 4, (n - 1) % 4
                        if bb == 0:
                            claim(pe, 'kl', G, kp)
                        for u in range(2):
                            drained(pe, 'kp', G, n - 1, u)
                            for j in range(4):
                                h = 4 * u + j
                                last = pe.matmul(pbank('kl', G, kp)[32 * j:32 * j + 32, u, 0:P],
                                                 QZ[:, h, 4 * G + bb, :], KTb[(n - 1) % 2][:, h, :],
                                                 start=(bb == 0), stop=(bb == 3))
                        if bb == 3:
                            done(last, 'kl', G, kp)
                claim(pe, 'kl', G, NPG - 1)
                for u in range(2):
                    for j in range(4):
                        h = 4 * u + j
                        last = pe.matmul(pbank('kl', G, NPG - 1)[32 * j:32 * j + 32, u, 0:P],
                                         QN[:, h, 32 * G:32 * G + 32], kTn[:, h, :], start=True, stop=True)
                done(last, 'kl', G, NPG - 1)
                for g in range(2):
                    sides('softmax', G, g)
                    pe.wait_ge(S_("sample_exp"), 2 * G + g + 1)
                    for q in range(5):
                        claim(pe, 'st', G, g, q)
                        for i in range(4 if q < 4 else 1):
                            c = P * (4 * q + i)
                            last = pe.transpose(bank('st', G, g, q)[:, P * i:P * i + P], LS[:, g, c:c + P], ident)
                        done(last, 'st', G, g, q)
                drained(pe, 'st', G, 0, 4)
                drained(pe, 'st', G, 1, 4)
                for b in range(4):
                    claim(pe, 'o', G, b)
                    for kp in range(NPG):
                        if kp < NPAGES:
                            seq = 128 * G + 64 + 16 * b + kp
                            pe.wait_ge(page_in[seq % 8], 16 * (seq // 8 + 1))
                            page = ring[seq % 8]
                        else:
                            page = Vn[:, :]
                        for u in range(2):
                            for j in range(4):
                                h = 4 * u + j
                                last = pe.matmul(pbank('o', G, b)[32 * j:32 * j + 32, u, 0:HD],
                                                 PTs[:, u, kp, 32 * j:32 * j + 32], page[:, HD * h:HD * h + HD],
                                                 start=(kp == 0), stop=(kp == NPG - 1))
                        if kp < NPAGES:
                            last.then_inc(S_("v_pages_used"), 1)
                        else:
                            done(last, 'o', G, b)
                        sides('V', G, b, kp)
                    drained(pe, 'o', G, b)
                    for g in range(2):
                        claim(pe, 'ot', G, b, g)
                        done(pe.transpose(bank('ot', G, b, g)[:, 0:P], OS[b % 2][:, g, :], ident), 'ot', G, b, g)

            sides('end')
            for c in range(8):
                project3(('wa', c), split(('wa', c // 2), 256), column(c), oa,
                         (lambda k: pe.wait_ge(S_("oa_split"), k + 1)) if c == 0 else None)
            pe.wait_ge(S_("ws_causal"), 1)
            for q in range(2):
                claim(pe, 'w', q)
                for i in range(4):
                    last = pe.transpose(bank('w', q)[:, P * i:P * i + P], WS[:, 4 * q + i, :], ident)
                done(last, 'w', q)
            drained(pe, 'w', 1)
            claim(pe, 'bd')
            done(pe.matmul(bank('bd')[0:TS, 0:64], const('rep', 8), WT[0:8, :, 0:8], start=True, stop=True), 'bd')
            pe.wait_ge(S_("sv_normed"), 1)
            pe.wait_ge(S_("bd_ready"), 1)
            for g in range(8):
                claim(pe, 'sg', g)
                for c in range(4):
                    last = pe.matmul(bank('sg', g)[:, P * c:P * c + P], SV[:, c, P * g:P * g + P], WT[:, g, :],
                                     start=True, stop=True)
                done(last, 'sg', g)
                claim(pe, 'sgs', g)
                done(pe.matmul(bank('sgs', g)[:, 0:TS], SV[0:TS, 4, P * g:P * g + P], BD[:, g, :],
                               start=True, stop=True), 'sgs', g)
            for c in range(8):
                project3(('wb', c), split(('wb', c // 2), 256), column(c), ob,
                         (lambda k: pe.wait_ge(S_("ob_split"), k + 1)) if c == 0 else None)
            for c in range(8):
                project3(('out', c), split(('out', c // 2), 256), column(c), mg,
                         (lambda k: pe.wait_ge(S_("mg_split"), k + 1)) if c == 0 else None)
                if c == 0:
                    pe.wait_ge(S_("state_in"), 32)
                    for q in range(2):
                        claim(pe, 'state', q)
                        for i in range(4 if q == 0 else 2):
                            n = 64 if (q, i) == (1, 1) else P
                            last = pe.transpose(bank('state', q)[:, P * i:P * i + n], SRAW[0:n, 4 * q + i, :],
                                                ident[0:n, 0:n])
                        done(last, 'state', q)
            rms_sum(1, 0)
            rms_sum(1, 7)
            for f in range(FB):
                wts = split(('up', f), 256)
                for k2 in range(2):
                    project3(('up', f, k2), wts, column(k2), xn2,
                             (lambda k: pe.wait_ge(S_("xn_ready"), 8 + k + 1)) if (f, k2) == (0, 0) else None)
            def down(c, kh):
                hi, lo = split(('dn', c, kh), P, 11)
                if kh == 0:
                    claim(pe, 'dn', c)
                for a in range(2):
                    out, t = ptile('dn', c)[:, a, :], slice(HALF * a, HALF * a + HALF)
                    for k in range(11):
                        n = 11 * kh + k
                        if c == 0 and a == 0:
                            pe.wait_ge(S_("act_ready"), n + 1)
                        pe.matmul(out, hi[:, k, :], gated(n, 0)[:, t], start=(n == 0), stop=False)
                        pe.matmul(out, hi[:, k, :], gated(n, 1)[:, t], start=False, stop=False)
                        last = pe.matmul(out, lo[:, k, :], gated(n, 0)[:, t], start=False, stop=(n == FB - 1))
                if kh == 0:
                    last.then_inc(S_("down_halves"), 1)
                else:
                    done(last, 'dn', c)

            for c, kh in DOWN:
                down(c, kh)
                if (c, kh) == (1, 1):
                    pe.wait_ge(S_("conv_rows"), FB)
                    for q in range(2):
                        claim(pe, 'ho', q)
                        for i in range(4 if q == 0 else 3):
                            n = 4 * q + i
                            src = HCP if n == 0 else HCS[:, P * (n - 1):min(P * n, 704)]
                            m = src.shape[-1]
                            last = pe.transpose(bank('ho', q)[0:m, P * i:P * i + P], src, ident)
                        done(last, 'ho', q)
            rms_sum(2, 0)
            rms_sum(2, 7)
            for q in range(2):
                pe.wait_ge(S_("xn_whole"), 20 + 4 * q)
                for r in range(R):
                    claim(pe, 'y', r, q)
                    for i in range(4):
                        last = pe.transpose(bank('y', r, q)[0:width(r), P * i:P * i + P],
                                            YN[:, 4 * q + i, P * r:P * r + width(r)], ident)
                    done(last, 'y', r, q)

        @block.scalar
        def _(act):
            def split_high(*name):
                n, value = chunks[name]
                act.wait_ge(weights_in[n % NW], value)
                if n >= NH:
                    chunk_used(act, n - NH)
                c = chunk_words(name)
                act.activation(WH[n % NH][:, 0:c], W[n % NW][:, 0:c], ACT.Copy).then_inc(S_("high_ready"), 1)

            def square(i, kind, c):
                if kind:
                    drained(act, kind, c)
                act.activation(SQ[i][:, c, :], xT[i][:, c, :], ACT.Square).then_inc(S_("squares_act"), 1)

            def root(i):
                drained(act, 'rms', i, 0)
                drained(act, 'rms', i, 1)
                act.activation(RS[i], RS[i], ACT.Sqrt).then_inc(S_("rms_root"), 1)

            def high(x, k, ready, value, signal):
                act.wait_ge(S_(ready), value)
                act.activation(x.hi_block(k), x.whole_block(k), ACT.Copy).then_inc(S_(signal), 1)

            after = split_after(split_high)

            def side_tile(*tile):
                i = side.index(tile)
                after(*tile)
                filled(act, *tile)
                if i >= 2:
                    act.wait_ge(S_(f"side_stored{i % 2}"), 16 * (i // 2))
                kind, c = tile[0], tile[1]
                if kind == 'sv':
                    n = width(tile[2])
                    dst, src = stage[i % 2][0:n, 0:256], pbank(*tile)[0:n, 0, 0:256]
                    out = sv_scr[tile[2], 0:n, 256 * c:256 * c + 256]
                else:
                    dst, src, out = halves(stage[i % 2]), ptile(*tile), side_scr[kind][:, c, :]
                act.activation(dst, src, {'sv': ACT.Copy, 'su': ACT.Gelu_apprx_tanh}.get(kind, ACT.Sigmoid))\
                    .then_inc(drains(*tile), 1)
                drained(act, *tile)
                act.dma_start(out, dst if kind == 'sv' else stage[i % 2]).then_inc(S_(f"side_stored{i % 2}"), 16)

            def sides(*place):
                for tile in side_at.get(place, ()):
                    side_tile(*tile)

            def query(c):
                after('q', c)
                filled(act, 'q', c)
                act.activation(halves(qT[:, c, :]), ptile('q', c), ACT.Copy, scale=ATT_SCALE).then_inc(drains('q', c), 1)

            for r in range(R):
                filled(act, 'x', r, 0)
                act.activation(xT0[:, 0:4, P * r:P * r + width(r)], blocks(bank('x', r, 0), 4)[:, :, 0:width(r)],
                               ACT.Copy).then_inc(drains('x', r, 0), 1)
            drained(act, 'x', R - 1, 0)
            for k in range(4):
                square(0, None, k)
            split_high('iq', 0)
            root(0)
            for h in range(H):
                filled(act, 'bias', h)
                act.activation(BV[:, h, :], bank('bias', h)[:, 0:BIASW], ACT.Copy).then_inc(drains('bias', h), 1)
            for k in range(KT):
                high(xn1, k, "xn_whole", k + 1, "xn_high")
            for m in range(4):
                after('iq', m)
                filled(act, 'iq', m)
                act.activation(halves(iqT[:, m, :]), ptile('iq', m), ACT.Copy).then_inc(drains('iq', m), 1)
            after('ikw')
            filled(act, 'ikw')
            act.activation(halves(IKW[0:72, :]), ptile('ikw')[0:72], ACT.Copy).then_inc(drains('ikw'), 1)
            k = 0
            for r in range(1, 4):
                for h in range(H):
                    filled(act, 'ps', r, h)
                    if k >= 2:
                        act.wait_ge(S_("relu_used"), k - 1)
                    act.activation(RL[k % 2][:, 0:P * (r + 1)], bank('ps', r, h)[:, 0:P * (r + 1)], ACT.Relu)\
                        .then_inc(drains('ps', r, h), 1)
                    k += 1
            for s in range(18):
                if s < 16:
                    filled(act, 't', s)
                    if s >= 2:
                        filled(act, 's1', s - 2)
                    act.activation(IKT[s % 2], bank('t', s), ACT.Copy).then_inc(drains('t', s), 1)
                if 1 <= s < 17:
                    filled(act, 's1', s - 1)
                    if s >= 3:
                        kc, p = (s - 3) // 4, (s - 3) % 4
                        if p == 3:
                            filled(act, 'ss', kc)
                        else:
                            act.wait_ge(S_("heads_summed"), 3 * kc + p + 1)
                    act.activation(RL2[(s - 1) % 2], bank('s1', s - 1), ACT.Relu).then_inc(drains('s1', s - 1), 1)
                if s % 2 == 1 and s < 16:
                    query(s // 2)
            filled(act, 's1n')
            act.activation(RLN, bank('s1n')[:, 0:32], ACT.Relu).then_inc(drains('s1n'), 1)
            act.wait_ge(S_("bias_out"), 16)
            for c in range(8):
                after('k', c)
                filled(act, 'k', c)
                act.activation(halves(kT[:, c, :]), ptile('k', c), ACT.Copy).then_inc(drains('k', c), 1)
            for r in range(R):
                for q in range(2):
                    filled(act, 'kt', r, q)
                    if r >= 2 and q == 0:
                        act.wait_ge(S_(f"k_stored{r % 2}"), 16 * (r // 2))
                    act.activation(KO[r % 2][0:width(r), 512 * q:512 * q + 512], bank('kt', r, q)[0:width(r)],
                                   ACT.Copy).then_inc(drains('kt', r, q), 1)
            def prompt_exp(h):
                act.wait_ge(S_("max_ready"), h + 1)
                for r in range(4):
                    n, o = P * (r + 1), SP_OFF[r]
                    last = act.activation(L[h % 2][:, o:o + n], L[h % 2][:, o:o + n], ACT.Exp,
                                          bias=NM[h % 2][:, r:r + 1], accum_out=SU[h % 2][:, r:r + 1])
                last.then_inc(S_("exp_done"), 1)

            for c in range(4):
                if c == 3:
                    after('v', 3, 0)
                    prompt_exp(0)
                for r in range(R):
                    if c < 3:
                        after('v', c, r)
                    filled(act, 'v', c, r)
                    dst = V[:, r, 256 * c:256 * c + 256] if r < 4 else Vn[0:TS, 256 * c:256 * c + 256]
                    act.activation(dst, pbank('v', c, r)[0:width(r), 0, 0:256], ACT.Copy).then_inc(drains('v', c, r), 1)
            for h in range(H + 1):
                if h < H:
                    sides('B', h, 0)
                if h:
                    filled(act, 'pv', h - 1)
                    if h == 1:
                        act.wait_ge(S_("x_out"), 16)
                    act.activation(oaT[:, h - 1, 0:TP], bank('pv', h - 1), ACT.Copy).then_inc(drains('pv', h - 1), 1)
                if h < H:
                    sides('B', h, 1)
                    if h == 0:
                        act.wait_ge(S_("k_stored0"), 48)
                        act.wait_ge(S_("k_stored1"), 32)
                    for r in range(4):
                        filled(act, 'pt', h, r)
                        act.activation(PT[:, 0:r + 1, P * r:P * r + P], blocks(bank('pt', h, r), 4)[:, 0:r + 1, :],
                                       ACT.Copy).then_inc(drains('pt', h, r), 1)
                    if h + 1 < H:
                        prompt_exp(h + 1)
            sides('start')
            for G in range(2):
                for n in range(64):
                    filled(act, 'kp', G, n, 0)
                    act.activation(KTb[n % 2][:, 0:4, :], blocks(bank('kp', G, n, 0), 4), ACT.Copy)\
                        .then_inc(drains('kp', G, n, 0), 1)
                act.wait_ge(S_("sample_max"), G + 1)
                for g in range(2):
                    act.activation(LS[:, g, :], LS[:, g, :], ACT.Exp, bias=NM[0][:, g:g + 1],
                                   accum_out=SU[0][:, g:g + 1]).then_inc(S_("sample_exp"), 1)
                sides('softmax', G, 0)
                for q in range(5):
                    filled(act, 'st', G, 0, q)
                    m = 4 if q < 4 else 1
                    act.activation(PTs[:, 0, 4 * q:4 * q + m, :], blocks(bank('st', G, 0, q), 4)[:, 0:m, :], ACT.Copy)\
                        .then_inc(drains('st', G, 0, q), 1)
                sides('softmax', G, 1)
                for b in range(4):
                    for kp in range(NPG):
                        sides('V', G, b, kp)
                    t = TP + 32 * G + 8 * b
                    for g in range(2):
                        filled(act, 'ot', G, b, g)
                        act.activation(oaT[:, 4 * g:4 * g + 4, t:t + 8],
                                       blocks(bank('ot', G, b, g)[:, 0:P], 4)[:, :, 8 * b:8 * b + 8], ACT.Copy)\
                            .then_inc(drains('ot', G, b, g), 1)
            for g in range(2):
                drained(act, 'ot', 1, 3, g)
            for g in range(8):
                act.activation(oa.hi_block(g), oa.whole_block(g), ACT.Copy).then_inc(S_("oa_high"), 1)
            sides('end')
            after('wa', 0)
            act.wait_ge(S_("sv_back"), 32)
            for r in range(R):
                act.activation(SV[0:width(r), r, :], SV[0:width(r), r, :], ACT.Gelu_apprx_tanh)\
                    .then_inc(S_("sv_gelu"), 1)
            for c in (2, 4):
                after('wa', c)
            act.wait_ge(S_("sv_mean"), 1)
            act.activation(SS, SS, ACT.Sqrt).then_inc(S_("sv_root"), 1)
            after('wa', 6)
            filled(act, 'wa', 7)
            for g in range(8):
                high(ob, g, "ob_whole", g + 1, "ob_high")
            for c in range(8):
                after('wb', c)
                high(mg, c, "merged", c + 1, "mg_high")
            for c in range(8):
                after('out', c)
                square(1, 'out', c)
            root(1)
            for k in range(KT):
                high(xn2, k, "xn_whole", 8 + k + 1, "xn_high")

            def gated_high(f):
                act.wait_ge(S_("act_whole"), f + 1)
                act.activation(gated(f, 0), gated_whole(f), ACT.Copy).then_inc(S_("act_high"), 1)

            for f in range(FB):
                for k in range(2):
                    after('up', f, k)
                    filled(act, 'up', f, k)
                    if f >= 2:
                        act.wait_ge(S_("act_whole"), f - 1)
                        act.wait_ge(S_("conv_rows"), f - 1)
                    hp, pt = HPb[f % 2][k], pbank('up', f, k)
                    act.activation(hp[:, 2:2 + HALF], pt[:, 0, 0:HALF], ACT.Copy)
                    act.activation(hp[:, 2 + HALF:514], pt[:, 1, 0:TP - HALF], ACT.Copy)
                    act.activation(hp[:, 514:594].rearrange("p (b c) -> p b c", b=8)[:, :, 2:10],
                                   pt[:, 1, TP - HALF:HALF].rearrange("p (b c) -> p b c", b=8), ACT.Copy)\
                        .then_inc(drains('up', f, k), 1)
                    if k == 1 and f:
                        gated_high(f - 1)
                    drained(act, 'up', f, k)
                    act.wait_ge(S_("state_put"), 2 * f + k + 1)
                    fb = FB * k + f
                    act.activation(CB[f % 2][k], hp[:, 2:594], ACT.Identity, bias=VT[:, 156 + fb:157 + fb],
                                   scale=VT[:, 112 + fb:113 + fb]).then_inc(S_("tap2_done"), 1)
                act.wait_ge(S_("taps_done"), 2 * f + 1)
                act.activation(CB[f % 2][0], CB[f % 2][0], ACT.Silu).then_inc(S_("silu_done"), 1)
            split_high('dn', *DOWN[1])
            gated_high(FB - 1)
            for i in (2, 3):
                split_high('dn', *DOWN[i])
            for c in range(8):
                for i in down_splits(c):
                    split_high('dn', *DOWN[i])
                square(2, 'dn', c)
            root(2)
            for r in range(R):
                filled(act, 'y', r, 0)
                act.activation(YO[0:width(r), r, 0:512], bank('y', r, 0)[0:width(r)], ACT.Copy)\
                    .then_inc(drains('y', r, 0), 1)

        @block.vector
        def _(dve):
            steps = [0]

            def link(ins):
                steps[0] += 1
                ins.then_inc(S_("dve_step"), 1)
                dve.wait_ge(S_("dve_step"), steps[0])

            def low(x, k, ready, value, signal):
                dve.wait_ge(S_(ready), value)
                dve.tensor_tensor(x.lo_block(k), x.whole_block(k), x.hi_block(k).bitcast(F32), ALU.subtract)\
                    .then_inc(S_(signal), 1)

            after = split_after(lambda *name: split_low(dve, *name) if name[0] not in POOL_SPLITS else None)

            def squares_low():
                for k in range(4, 8):
                    dve.tensor_tensor(SQ[0][:, k, :], xT0[:, k, :], xT0[:, k, :], ALU.mult)\
                        .then_inc(S_("squares_dve"), 1)

            def normalise(i, gcol):
                for a in range(2):
                    filled(dve, 'rms', i, a)
                    dve.tensor_scalar(halves(RS[i])[:, a, :], bank('rms', i, a)[:, 0:HALF], 1.0 / D, EPS,
                                      ALU.mult, ALU.add).then_inc(drains('rms', i, a), 1)
                dve.wait_ge(S_("rms_root"), i + 1)
                link(dve.reciprocal(RS[i], RS[i]))

                def whole(k):
                    dst = YN if i == 2 else (xn1, xn2)[i].whole
                    dve.scalar_tensor_tensor(dst[:, k, :], xT[i][:, k, :], VT[:, gcol + k:gcol + k + 1], RS[i],
                                             ALU.mult, ALU.mult).then_inc(S_("xn_whole"), 1)

                for k in range(KT):
                    whole(k)
                    if i < 2 and k:
                        low((xn1, xn2)[i], k - 1, "xn_high", 8 * i + k, "xn_ready")
                if i < 2:
                    low((xn1, xn2)[i], KT - 1, "xn_high", 8 * i + KT, "xn_ready")

            for r in range(R):
                filled(dve, 'x', r, 1)
                dve.tensor_copy(xT0[:, 4:8, P * r:P * r + width(r)], blocks(bank('x', r, 1), 4)[:, :, 0:width(r)])\
                    .then_inc(drains('x', r, 1), 1)
            drained(dve, 'x', R - 1, 1)
            squares_low()
            filled(dve, 'vec')
            dve.tensor_copy(VT[:, :], bank('vec')[:, 0:200]).then_inc(drains('vec'), 1)
            drained(dve, 'vec')
            drained(dve, 'x', R - 1, 0)
            split_low(dve, 'iq', 0)
            normalise(0, 0)
            for t in (('iq', 0), ('iq', 2)):
                after(*t)
            dve.wait_ge(S_("ident_in"), 16)
            dve.wait_ge(S_("consts_in"), 16)
            dve.tensor_copy(MS[:, 0:P], const('caus'))
            filled(dve, 'iqsw')
            dve.tensor_copy(IQSW, blocks(bank('iqsw')[:, 0:256], 4)).then_inc(drains('iqsw'), 1)
            filled(dve, 'ikd0')
            dve.tensor_copy(IKPAD[0:64, 0, :], bank('ikd0')[0:64])
            dve.tensor_copy(IKPAD[64:128, 1, :], bank('ikd0')[64:128]).then_inc(drains('ikd0'), 1)
            filled(dve, 'ikd1')
            nk = bank('ikd1')[:, 0:64].rearrange("p (q u t) -> p q u t", q=4, u=2)
            dve.tensor_copy(IKNEW[0:64], nk[0:64, :, 0, :])
            dve.tensor_copy(IKNEW[64:128], nk[64:128, :, 1, :]).then_inc(drains('ikd1'), 1)
            filled(dve, 'ikwT')
            dve.tensor_copy(IKWT[:, 0:4, :], blocks(bank('ikwT')[:, 0:288], 4))
            dve.tensor_copy(IKWT[0:TS, 4, :], bank('ikwT')[0:TS, 288:360]).then_inc(drains('ikwT'), 1)
            drained(dve, 'ikwT')
            dve.tensor_scalar(IWS[:, 0:4, :], IKWT[:, 0:4, 64:72], IDX_SCALE, None, ALU.mult)
            dve.tensor_scalar(IWS[0:TS, 4, :], IKWT[0:TS, 4, 64:72], IDX_SCALE, None, ALU.mult)\
                .then_inc(S_("iw_ready"), 1)
            filled(dve, 'iwrep')
            dve.tensor_tensor(TMP32, blocks(bank('iwrep')[:, 0:32], 4),
                              const('hmask')[:, None, :].broadcast_to([P, 4, 8]), ALU.mult).then_inc(drains('iwrep'), 1)
            drained(dve, 'iwrep')
            link(dve.tensor_reduce(IWC, TMP32, AX_X, ALU.add))
            for p in range(4):
                last = dve.tensor_scalar(SWM[:, p, :], const('selT')[:, TS * p:TS * p + TS], IWC[:, p:p + 1], None,
                                         ALU.mult)
            last.then_inc(S_("swm_ready"), 1)
            def prompt_best(r):
                n, o = P * (r + 1), SP_OFF[r]
                for k in range(TOPK_P // 8):
                    link(dve.max(MAX8P, MS[:, o:o + n]))
                    link(dve.match_replace(MS[:, o:o + n], MAX8P, MS[:, o:o + n], MARK))
                dve.tensor_scalar(MS[:, o:o + n], MS[:, o:o + n], MARK, NEG, ALU.not_equal, ALU.mult)\
                    .then_inc(S_("prompt_mask"), 1)

            k = 0
            for r in range(1, 4):
                n, o = P * (r + 1), SP_OFF[r]
                for h in range(H):
                    drained(dve, 'ps', r, h)
                    if h == 0:
                        dve.tensor_scalar(MS[:, o:o + n], RL[k % 2][:, 0:n], IWS[:, r, h:h + 1], None, ALU.mult)\
                            .then_inc(S_("relu_used"), 1)
                    else:
                        dve.wait_ge(S_("relu_used"), k)
                        dve.scalar_tensor_tensor(MS[:, o:o + n], RL[k % 2][:, 0:n], IWS[:, r, h:h + 1],
                                                 MS[:, o:o + n], ALU.mult, ALU.add).then_inc(S_("relu_used"), 1)
                    k += 1
                dve.wait_ge(S_("relu_used"), k)
                link(dve.tensor_tensor(MS[:, o + P * r:o + n], MS[:, o + P * r:o + n], const('caus'), ALU.add))
            after('ikw')
            after('q', 0)
            prompt_best(1)
            for kc in range(4):
                filled(dve, 'ss', kc)
                dve.tensor_copy(S[:, 512 * kc:512 * kc + 512], pbank('ss', kc)[0:TS, 0, :]).then_inc(drains('ss', kc), 1)
                if kc < 3:
                    after('q', 2 * kc + 2)
                if kc < 2:
                    prompt_best(kc + 2)
            filled(dve, 'ssn')
            dve.tensor_tensor(S[:, PAST:NKEY], pbank('ssn')[0:TS, 0, 0:8], const('newcausal', TS), ALU.add)\
                .then_inc(drains('ssn'), 1)
            drained(dve, 'ssn')
            rounds = [TOPK_S // 8]

            def sample_best(n):
                for _ in range(min(n, rounds[0])):
                    rounds[0] -= 1
                    link(dve.max(MAX8, S[:, 0:NKEY]))
                    link(dve.match_replace(S[:, 0:NKEY], MAX8, S[:, 0:NKEY], MARK))

            sample_best(18)

            def prompt_max(h):
                dve.wait_ge(S_("bias_mask_ready"), h + 1)
                for r in range(4):
                    n, o = P * (r + 1), SP_OFF[r]
                    filled(dve, 'pl', h, r)
                    dve.tensor_tensor_reduce(out=L[h % 2][:, o:o + n], in0=bank('pl', h, r)[:, 0:n], in1=MB[:, o:o + n],
                                             scale=1.0, scalar=MARK, op0=ALU.add, op1=ALU.max,
                                             accum_out=MX[h % 2][:, r:r + 1]).then_inc(drains('pl', h, r), 1)
                drained(dve, 'pl', h, 3)
                dve.tensor_scalar(NM[h % 2], MX[h % 2], -1.0, None, ALU.mult).then_inc(S_("max_ready"), 1)

            prompt_max(0)
            sample_best(4)
            for h in range(H):
                dve.wait_ge(S_("exp_done"), h + 1)
                link(dve.reciprocal(RC[h % 2], SU[h % 2]))
                for r in range(4):
                    n, o = P * (r + 1), SP_OFF[r]
                    dve.tensor_scalar(L[h % 2][:, o:o + n], L[h % 2][:, o:o + n], RC[h % 2][:, r:r + 1], None, ALU.mult)\
                        .then_inc(S_("probs_ready"), 1)
                if h + 1 < H:
                    prompt_max(h + 1)
                for i in range(2):
                    for tile in side_at['B', h, i]:
                        after(*tile)
                sample_best((2, 2, 1, 2, 1, 1, 1, 0)[h])
            sample_best(TOPK_S)
            link(dve.tensor_scalar(M8, S[:, PAST:NKEY], MARK, NEG, ALU.not_equal, ALU.mult))
            dve.tensor_scalar(S[:, 0:PAST], S[:, 0:PAST], MARK, NEG, ALU.not_equal, ALU.mult)
            dve.memset(S[:, PAST + TS:NCOL], NEG)
            dve.tensor_tensor(S[:, PAST:PAST + TS].rearrange("p (b t) -> p b t", b=8),
                              const('newblock', TS).rearrange("p (b t) -> p b t", b=8),
                              M8[:, None, :].broadcast_to([TS, 8, 8]), ALU.add).then_inc(S_("sample_mask"), 1)
            def splits(*place):
                for tile in side_at.get(place, ()):
                    after(*tile)

            splits('start')

            for G in range(2):

                def logits(kp):
                    filled(dve, 'kl', G, kp)
                    if kp == 0:
                        dve.wait_ge(S_(f"mask_in{G}"), 64)
                    for g in range(2):
                        last = dve.scalar_tensor_tensor(LS[:, g, P * kp:P * kp + P], pbank('kl', G, kp)[:, g, 0:P],
                                                        NBr[:, g, 0:1], MG[:, P * kp:P * kp + P], ALU.add, ALU.add)
                    last.then_inc(drains('kl', G, kp), 1)

                for n in range(64):
                    filled(dve, 'kp', G, n, 1)
                    dve.tensor_copy(KTb[n % 2][:, 4:8, :], blocks(bank('kp', G, n, 1), 4))\
                        .then_inc(drains('kp', G, n, 1), 1)
                    if n % 4 == 0 and n:
                        logits(n // 4 - 1)
                    if n == 48:
                        drained(dve, 'kl', G, 11)
                        dve.tensor_reduce(EARLY, LS[:, :, 0:12 * P], AX_X, ALU.max)
                logits(15)
                logits(16)
                if G == 0:
                    dve.wait_ge(S_("new_bias"), 2)
                drained(dve, 'kl', G, 16)
                for g in range(2):
                    link(dve.tensor_tensor(LS[:, g, 1920:NCOL], LS[:, g, 1920:NCOL], NBd[g], ALU.add))
                link(dve.tensor_reduce(MX[0][:, 0:2], LS[:, :, 12 * P:NCOL], AX_X, ALU.max))
                link(dve.tensor_tensor(MX[0][:, 0:2], MX[0][:, 0:2], EARLY, ALU.max))
                dve.tensor_scalar(NM[0][:, 0:2], MX[0][:, 0:2], -1.0, None, ALU.mult).then_inc(S_("sample_max"), 1)
                splits('softmax', G, 0)
                dve.wait_ge(S_("sample_exp"), 2 * G + 2)
                link(dve.reciprocal(RC[0][:, 0:2], SU[0][:, 0:2]))
                splits('softmax', G, 1)
                for q in range(5):
                    filled(dve, 'st', G, 1, q)
                    m = 4 if q < 4 else 1
                    dve.tensor_copy(PTs[:, 1, 4 * q:4 * q + m, :], blocks(bank('st', G, 1, q), 4)[:, 0:m, :])\
                        .then_inc(drains('st', G, 1, q), 1)
                for b in range(4):
                    for kp in range(NPAGES):
                        splits('V', G, b, kp)
                    filled(dve, 'o', G, b)
                    if b >= 2:
                        filled(dve, 'ot', G, b - 2, 1)
                    for g in range(2):
                        last = dve.tensor_scalar(OS[b % 2][:, g, :], pbank('o', G, b)[:, g, 0:HD], RC[0][:, g:g + 1],
                                                 None, ALU.mult)
                    last.then_inc(drains('o', G, b), 1)
                    splits('V', G, b, NPAGES)
            for k in range(8):
                low(oa, k, "oa_high", k + 1, "oa_split")
            splits('end')
            link(dve.memset(SS, 1.0))
            for c in range(8):
                after('wa', c)
                dve.wait_ge(S_(f"ga_back{c // 2}"), 16)
                filled(dve, 'wa', c)
                dve.tensor_tensor(halves(mT[:, c, :]), halves(GAT[:, c, :]), ptile('wa', c), ALU.mult)\
                    .then_inc(drains('wa', c), 1)
                for r in {3: (0, 1), 4: (2, 3), 5: (4,)}.get(c, ()):
                    w = width(r)
                    dve.wait_ge(S_("sv_gelu"), r + 1)
                    link(dve.tensor_tensor_reduce(out=JUNK[0:w], in0=SV[0:w, r, :], in1=SV[0:w, r, :], scale=1.0,
                                                  scalar=0.0, op0=ALU.mult, op1=ALU.add, accum_out=SS[0:w, r:r + 1]))
                if c == 5:
                    dve.tensor_scalar(SS, SS, 1.0 / D, EPS, ALU.mult, ALU.add).then_inc(S_("sv_mean"), 1)
                if c == 6:
                    dve.wait_ge(S_("sv_root"), 1)
                    dve.wait_ge(S_("sg_in"), 32)
                    link(dve.reciprocal(SS, SS))
                    for r in range(R):
                        w = width(r)
                        last = dve.scalar_tensor_tensor(SV[0:w, r, :], SV[0:w, r, :], SS[0:w, r:r + 1], SG[0:w, :],
                                                        ALU.mult, ALU.mult)
                    last.then_inc(S_("sv_normed"), 1)
            for q in range(2):
                filled(dve, 'w', q)
                dve.tensor_copy(WT[:, 4 * q:4 * q + 4, :], blocks(bank('w', q), 4)).then_inc(drains('w', q), 1)
            filled(dve, 'bd')
            dve.tensor_tensor(BD.rearrange("p g (b t) -> p g b t", b=8),
                              bank('bd')[0:TS, 0:64].rearrange("p (g t) -> p g t", g=8)[:, :, None, :]
                              .broadcast_to([TS, 8, 8, 8]),
                              const('bd', TS).rearrange("p (b t) -> p b t", b=8)[:, None, :, :]
                              .broadcast_to([TS, 8, 8, 8]), ALU.mult).then_inc(drains('bd'), 1)
            drained(dve, 'bd')
            dve.memset(ST[0:1, 111:112], 0.0).then_inc(S_("bd_ready"), 1)
            for g in range(8):
                filled(dve, 'sg', g)
                if g >= 2:
                    dve.wait_ge(S_("ob_whole"), g - 1)
                dve.tensor_tensor(blocks(TMPS[g % 2][:, 0:TP], 4), blocks(bank('sg', g), 4),
                                  SB[:, g, None, :].broadcast_to([P, 4, P]), ALU.add).then_inc(drains('sg', g), 1)
                filled(dve, 'sgs', g)
                dve.tensor_tensor(blocks(TMPS[g % 2][:, TP:T], 8), blocks(bank('sgs', g)[:, 0:TS], 8),
                                  SB[:, g, None, 0:8].broadcast_to([P, 8, 8]), ALU.add).then_inc(drains('sgs', g), 1)
                if g:
                    low(ob, g - 1, "ob_high", g, "ob_split")
            low(ob, 7, "ob_high", 8, "ob_split")
            dve.wait_ge(S_("gb_back"), 16)
            for c in range(8):
                after('wb', c)
                filled(dve, 'wb', c)
                if c >= 2:
                    dve.wait_ge(S_("merged"), c - 1)
                else:
                    dve.wait_ge(S_("ob_whole"), 8)
                dve.tensor_tensor(halves(TMPS[c % 2]), halves(GBT[:, c, :]), ptile('wb', c), ALU.mult)\
                    .then_inc(drains('wb', c), 1)
                if c:
                    low(mg, c - 1, "mg_high", c, "mg_split")
            low(mg, 7, "mg_high", 8, "mg_split")

            def residual(kind, x, back, c):
                filled(dve, kind, c)
                dve.wait_ge(S_(back), 16)
                dve.tensor_tensor(halves(x[:, c, :]), halves(x[:, c, :]), ptile(kind, c), ALU.add)\
                    .then_inc(drains(kind, c), 1)

            for c in range(8):
                after('out', c)
                residual('out', xT1, f"x_back{c // 2}", c)
                if c == 0:
                    for q in range(2):
                        filled(dve, 'state', q)
                        n = 512 if q == 0 else 192
                        dve.tensor_copy(STT_[:, 512 * q:512 * q + n], bank('state', q)[:, 0:n])\
                            .then_inc(drains('state', q), 1)
            normalise(1, 8)
            def gated_low(f):
                dve.wait_ge(S_("act_high"), f + 1)
                dve.tensor_tensor(gated(f, 1), gated_whole(f), gated(f, 0).bitcast(F32), ALU.subtract)\
                    .then_inc(S_("act_ready"), 1)

            for f in range(FB):
                for k in range(2):
                    after('up', f, k)
                    fb = FB * k + f
                    hp, cb = HPb[f % 2][k], CB[f % 2][k]
                    dve.wait_ge(S_("tap2_done"), 2 * f + k + 1)
                    link(dve.scalar_tensor_tensor(cb, hp[:, 1:593], VT[:, 68 + fb:69 + fb], cb, ALU.mult, ALU.add))
                    dve.scalar_tensor_tensor(cb, hp[:, 0:592], VT[:, 24 + fb:25 + fb], cb, ALU.mult, ALU.add)\
                        .then_inc(S_("taps_done"), 1)
                dve.wait_ge(S_("silu_done"), f + 1)
                dve.wait_ge(S_("taps_done"), 2 * f + 2)
                if f == NG:
                    dve.wait_ge(S_("x_out"), 32)
                a, (cg, cv) = gated_whole(f), CB[f % 2]
                dve.tensor_tensor(a[:, 0:TP], cg[:, 0:TP], cv[:, 0:TP], ALU.mult)
                dve.tensor_tensor(blocks(a[:, TP:T], 8), window(cg), window(cv), ALU.mult).then_inc(S_("act_whole"), 1)
                if f:
                    gated_low(f - 1)
            split_low(dve, 'dn', *DOWN[1])
            gated_low(FB - 1)
            for i in (2, 3):
                split_low(dve, 'dn', *DOWN[i])
            for c in range(8):
                for i in down_splits(c):
                    split_low(dve, 'dn', *DOWN[i])
                residual('dn', xT2, "x_back_ffn", c)
                if c == 1:
                    for q in range(2):
                        filled(dve, 'ho', q)
                        if q == 0:
                            dve.tensor_copy(CO[0:88, 0, :], bank('ho', 0)[0:88, 0:128])
                            dve.tensor_copy(CO[:, 1:4, :], blocks(bank('ho', 0)[:, 128:512], 3)).then_inc(drains('ho', 0), 1)
                        else:
                            dve.tensor_copy(CO[:, 4:6, :], blocks(bank('ho', 1)[:, 0:256], 2))
                            dve.tensor_copy(CO[0:64, 6, :], bank('ho', 1)[0:64, 256:384]).then_inc(drains('ho', 1), 1)
            normalise(2, 16)
            for r in range(R):
                filled(dve, 'y', r, 1)
                dve.tensor_copy(YO[0:width(r), r, 512:1024], bank('y', r, 1)[0:width(r)])\
                    .then_inc(drains('y', r, 1), 1)


def window(c):
    return bass.AP(c.tensor, c.offset + 514, [c.ap[0], [10, 8], [1, 8]])


_INS = ['x_prompt', 'x_sample', 'cache_k', 'cache_v', 'cache_idx_k', 'state_ffn_conv', 'page_table', 'rel_bias',
        'norm_mix_g', 'w_in', 'sg_norm_g', 'sg_w_s', 'sg_b', 'w_branch_a', 'w_branch_b', 'w_out', 'norm_ffn_g',
        'w_up', 'ffn_conv_w', 'ffn_conv_b', 'w_down', 'norm_final_g']
_OUTS = [(1, TP, D), (NB_, NS, D), (1, 1, TP, H, HD), (1, 1, TP, H, HD), (1, 1, TP, IDX), (1, 1, 2, 2 * FF),
         (1, NB_, NS, H, HD), (1, NB_, NS, H, HD), (1, NB_, NS, IDX), (1, NB_, 2, 2 * FF), (1, NB_, NS, D)]


def kernel(**inputs):
    import concourse.bacc as _bacc
    from concourse.bass_utils import run_bass_kernel_spmd as _run

    nc = _bacc.Bacc("TRN2", target_bir_lowering=False, num_devices=1)
    arrays, args = {}, []
    for name in _INS:
        a = np.ascontiguousarray(inputs[name])
        arrays[f"in_{name}"] = a
        args.append(nc.dram_tensor(f"in_{name}", a.shape, mybir.dt.from_np(a.dtype), kind="ExternalInput").ap())
    c = shape_constants()
    arrays["in_consts"] = c
    args.append(nc.dram_tensor("in_consts", c.shape, F32, kind="ExternalInput").ap())
    for i, shape in enumerate(_OUTS):
        args.append(nc.dram_tensor(f"out_{i}", shape, F32, kind="ExternalOutput").ap())
    hybrid_kernel(nc, *args)
    r = _run(nc, [arrays], core_ids=[0])
    return tuple(r.results[0][f"out_{i}"] for i in range(len(_OUTS)))
```
